# Optimizing a Trainium2 kernel written in Bass

```python
import jax, jax.numpy as jnp
from jax import lax
import numpy as np
import math

D_MODEL = 1024
BATCH = 1
SEQ = 512
DEPTH = 2

GRID_W = 64
CTX_LEN = 256
CONV_W = 1024
CONV_K = 3
N_HEADS = 8
N_KV_HEADS = 2
HEAD_DIM = 128
GROUP = N_HEADS // N_KV_HEADS
Q_BLOCK = 128
ROPE_THETA = 10000.0
ROPE_AXIS_DIM = HEAD_DIM // 2
ROPE_PAIRS = ROPE_AXIS_DIM // 2
ATTN_SCALE = HEAD_DIM ** -0.5
GLA_HEADS = 4
GLA_DK = D_MODEL // 2
GLA_DV = D_MODEL
GLA_DKH = GLA_DK // GLA_HEADS
GLA_DVH = GLA_DV // GLA_HEADS
GLA_RANK = 16
GLA_TAU = 16.0
GLA_CHUNK = 64
N_BRANCH = 3
EPS = 1e-6

IN_SPLITS = (CONV_W, CONV_W, CONV_W, CONV_W,
             N_HEADS * HEAD_DIM, N_KV_HEADS * HEAD_DIM, N_KV_HEADS * HEAD_DIM,
             N_HEADS * HEAD_DIM,
             GLA_DK, GLA_DK, GLA_DV, GLA_RANK, GLA_RANK, GLA_DV,
             N_BRANCH * D_MODEL)
IN_WIDTH = sum(IN_SPLITS)


def _rmsnorm(x, g):
    xf = x.astype(jnp.float32)
    y = xf * lax.rsqrt(jnp.mean(xf * xf, axis=-1, keepdims=True) + EPS)
    return (y * g.astype(jnp.float32)).astype(x.dtype)

def _split_proj(p):
    offsets = np.cumsum(IN_SPLITS)[:-1].tolist()
    return jnp.split(p, offsets, axis=-1)

def _short_conv(u, w):
    up = jnp.pad(u, ((0, 0), (1, 1), (0, 0)))
    return w[0] * up[:, :-2] + w[1] * up[:, 1:-1] + w[2] * up[:, 2:]

def _axial_rope_tables(n_tokens):
    n_rows = n_tokens // GRID_W
    row = jnp.repeat(jnp.arange(n_rows, dtype=jnp.float32), GRID_W)
    col = jnp.tile(jnp.arange(GRID_W, dtype=jnp.float32), n_rows)
    freqs = ROPE_THETA ** (-jnp.arange(ROPE_PAIRS, dtype=jnp.float32) * 2.0 / ROPE_AXIS_DIM)
    ang = jnp.stack([row[:, None] * freqs, col[:, None] * freqs], axis=1)
    return jnp.cos(ang), jnp.sin(ang)

def _apply_rope(x, cos, sin):
    b_, t_, h_, _ = x.shape
    xr = x.reshape(b_, t_, h_, 2, 2, ROPE_PAIRS)
    x1, x2 = xr[..., 0, :], xr[..., 1, :]
    c_, s_ = cos[None, :, None], sin[None, :, None]
    out = jnp.stack([x1 * c_ - x2 * s_, x2 * c_ + x1 * s_], axis=-2)
    return out.reshape(b_, t_, h_, HEAD_DIM).astype(x.dtype)

def _attn_heads(q, k, v, q_g, k_g, rope):
    b_, t_ = q.shape[:2]
    q = _rmsnorm(q.reshape(b_, t_, N_HEADS, HEAD_DIM), q_g)
    k = _rmsnorm(k.reshape(b_, t_, N_KV_HEADS, HEAD_DIM), k_g)
    v = v.reshape(b_, t_, N_KV_HEADS, HEAD_DIM)
    if rope is not None:
        q = _apply_rope(q, *rope)
        k = _apply_rope(k, *rope)
    return q, k, v

def _sdpa_blocks(q, keys, vals):
    b_, t_ = q.shape[:2]
    nb = t_ // Q_BLOCK
    qb = q.reshape(b_, nb, Q_BLOCK, N_KV_HEADS, GROUP, HEAD_DIM).transpose(1, 0, 2, 3, 4, 5)

    def one_block(qblk):
        s = jnp.einsum('bqkgd,bskd->bkgqs', qblk, keys).astype(jnp.float32) * ATTN_SCALE
        p = jax.nn.softmax(s, axis=-1).astype(vals.dtype)
        return jnp.einsum('bkgqs,bskd->bqkgd', p, vals)

    o = lax.map(one_block, qb)
    return o.transpose(1, 0, 2, 3, 4, 5).reshape(b_, t_, N_HEADS * HEAD_DIM)

def _gla_inputs(q, k, v, r_f, r_b, w_df, b_df, w_db, b_db):
    b_, t_ = q.shape[:2]
    q = q.reshape(b_, t_, GLA_HEADS, GLA_DKH) * (GLA_DKH ** -0.5)
    k = k.reshape(b_, t_, GLA_HEADS, GLA_DKH)
    v = v.reshape(b_, t_, GLA_HEADS, GLA_DVH)
    la_f = (jax.nn.log_sigmoid((r_f @ w_df + b_df).astype(jnp.float32)) / GLA_TAU).reshape(b_, t_, GLA_HEADS, GLA_DKH)
    la_b = (jax.nn.log_sigmoid((r_b @ w_db + b_db).astype(jnp.float32)) / GLA_TAU).reshape(b_, t_, GLA_HEADS, GLA_DKH)
    return q, k, v, la_f, la_b

def _gla_scan(q, k, v, log_a, s0):
    b_, t_, h_, _ = q.shape
    dv = v.shape[-1]
    nc = t_ // GLA_CHUNK

    def chunks(a):
        return a.astype(jnp.float32).reshape(b_, nc, GLA_CHUNK, h_, a.shape[-1]).transpose(1, 0, 3, 2, 4)

    mask = jnp.tril(jnp.ones((GLA_CHUNK, GLA_CHUNK), dtype=bool))

    def step(s, inp):
        qc, kc, vc, ac = inp
        bcum = jnp.cumsum(ac, axis=2)
        o_inter = jnp.einsum('bhtd,bhde->bhte', qc * jnp.exp(bcum), s)
        diff = bcum[:, :, :, None, :] - bcum[:, :, None, :, :]
        decay = jnp.exp(jnp.where(mask[:, :, None], diff, -jnp.inf))
        att = jnp.einsum('bhtd,bhsd,bhtsd->bhts', qc, kc, decay)
        o_intra = jnp.einsum('bhts,bhse->bhte', att, vc)
        b_last = bcum[:, :, -1:, :]
        s_new = jnp.exp(b_last[:, :, 0, :])[..., None] * s + jnp.einsum('bhsd,bhse->bhde', kc * jnp.exp(b_last - bcum), vc)
        return s_new, o_inter + o_intra

    s_f, o = lax.scan(step, s0, (chunks(q), chunks(k), chunks(v), chunks(log_a)))
    o = o.transpose(1, 0, 3, 2, 4).reshape(b_, t_, h_, dv)
    return o.astype(v.dtype), s_f

def _flip(a):
    return jnp.flip(a, axis=1)

def _gla_bidirectional(ctx_in, lat_in):
    qc, kc, vc, lfc, lbc = ctx_in
    ql, kl, vl, lfl, lbl = lat_in
    s0 = jnp.zeros((qc.shape[0], GLA_HEADS, GLA_DKH, GLA_DVH), jnp.float32)
    o_cf, s_f = _gla_scan(qc, kc, vc, lfc, s0)
    o_cb, s_b = _gla_scan(_flip(qc), _flip(kc), _flip(vc), _flip(lbc), s0)
    o_lf, _ = _gla_scan(ql, kl, vl, lfl, s_f)
    o_lb, _ = _gla_scan(_flip(ql), _flip(kl), _flip(vl), _flip(lbl), s_b)
    return o_lf + _flip(o_lb), o_cf + _flip(o_cb)

def _mixer_output(parts, att_o, gla_o, conv_w_l, gla_g_l, w_br_conv_l, w_br_attn_l, w_br_gla_l, b_gate_l, w_out_l):
    a_b, a_c, a_x, a_z = parts[0], parts[1], parts[2], parts[3]
    z_attn, z_gla, mg = parts[7], parts[13], parts[14]
    b_, t_ = a_b.shape[:2]
    br_a = ((a_b * _short_conv(a_c * a_x, conv_w_l)) * jax.nn.silu(a_z)) @ w_br_conv_l
    br_b = (att_o * jax.nn.silu(z_attn)) @ w_br_attn_l
    br_c = (_rmsnorm(gla_o, gla_g_l).reshape(b_, t_, GLA_DV) * jax.nn.silu(z_gla)) @ w_br_gla_l
    g_a, g_b, g_c = jnp.split(jax.nn.sigmoid(mg + b_gate_l), N_BRANCH, axis=-1)
    return (g_a * br_a + g_b * br_b + g_c * br_c) @ w_out_l

def first_inputs(seed: int = 0) -> dict:
    key = jax.random.key(seed)
    ks = jax.random.split(key, 24)
    n = jax.random.normal
    f32 = jnp.float32
    return {
        "x": n(ks[0], (BATCH, SEQ, D_MODEL), f32),
        "c": n(ks[1], (BATCH, D_MODEL), f32),
        "ctx": n(ks[2], (BATCH, CTX_LEN, D_MODEL), f32),
        "c_ctx": n(ks[3], (D_MODEL,), f32),
        "w_ada": n(ks[4], (DEPTH, D_MODEL, 3 * D_MODEL), f32) * D_MODEL ** -0.5,
        "b_ada": 0.02 * n(ks[5], (DEPTH, 3 * D_MODEL), f32),
        "g_pre": 1.0 + 0.02 * n(ks[6], (DEPTH, D_MODEL), f32),
        "g_post": 1.0 + 0.02 * n(ks[7], (DEPTH, D_MODEL), f32),
        "w_in": n(ks[8], (DEPTH, D_MODEL, IN_WIDTH), f32) * D_MODEL ** -0.5,
        "conv_w": n(ks[9], (DEPTH, CONV_K, CONV_W), f32) * CONV_K ** -0.5,
        "q_norm_g": 1.0 + 0.02 * n(ks[10], (DEPTH, HEAD_DIM), f32),
        "k_norm_g": 1.0 + 0.02 * n(ks[11], (DEPTH, HEAD_DIM), f32),
        "w_decay_fwd": n(ks[12], (DEPTH, GLA_RANK, GLA_DK), f32) * GLA_RANK ** -0.5,
        "b_decay_fwd": 0.01 * n(ks[13], (DEPTH, GLA_DK), f32),
        "w_decay_bwd": n(ks[14], (DEPTH, GLA_RANK, GLA_DK), f32) * GLA_RANK ** -0.5,
        "b_decay_bwd": 0.01 * n(ks[15], (DEPTH, GLA_DK), f32),
        "gla_norm_g": 1.0 + 0.02 * n(ks[16], (DEPTH, GLA_DVH), f32),
        "w_br_conv": n(ks[17], (DEPTH, CONV_W, D_MODEL), f32) * CONV_W ** -0.5,
        "w_br_attn": n(ks[18], (DEPTH, N_HEADS * HEAD_DIM, D_MODEL), f32) * (N_HEADS * HEAD_DIM) ** -0.5,
        "w_br_gla": n(ks[19], (DEPTH, GLA_DV, D_MODEL), f32) * GLA_DV ** -0.5,
        "b_gate": 0.02 * n(ks[20], (DEPTH, N_BRANCH * D_MODEL), f32),
        "w_out": n(ks[21], (DEPTH, D_MODEL, D_MODEL), f32) * D_MODEL ** -0.5,
    }

def first_block(x, c, ctx, c_ctx, w_ada, b_ada, g_pre, g_post, w_in, conv_w, q_norm_g, k_norm_g,
              w_decay_fwd, b_decay_fwd, w_decay_bwd, b_decay_bwd, gla_norm_g,
              w_br_conv, w_br_attn, w_br_gla, b_gate, w_out):
    n_tok = x.shape[1]
    rope = _axial_rope_tables(n_tok)
    xc = ctx
    for l in range(DEPTH):
        last = l == DEPTH - 1
        mod_l = jax.nn.silu(c) @ w_ada[l] + b_ada[l]
        sh_l, sc_l, gt_l = jnp.split(mod_l[:, None, :], 3, axis=-1)
        mod_c = jax.nn.silu(c_ctx) @ w_ada[l] + b_ada[l]
        sh_c, sc_c, gt_c = jnp.split(mod_c, 3, axis=-1)
        h_l = _rmsnorm(x, g_pre[l]) * (1.0 + sc_l) + sh_l
        h_c = _rmsnorm(xc, g_pre[l]) * (1.0 + sc_c) + sh_c
        pl = _split_proj(h_l @ w_in[l])
        pc = _split_proj(h_c @ w_in[l])
        q_l, k_l, v_l = _attn_heads(pl[4], pl[5], pl[6], q_norm_g[l], k_norm_g[l], rope)
        q_c, k_c, v_c = _attn_heads(pc[4], pc[5], pc[6], q_norm_g[l], k_norm_g[l], None)
        keys = jnp.concatenate([k_l, k_c], axis=1)
        vals = jnp.concatenate([v_l, v_c], axis=1)
        att_l = _sdpa_blocks(q_l, keys, vals)
        dec = (w_decay_fwd[l], b_decay_fwd[l], w_decay_bwd[l], b_decay_bwd[l])
        gla_c_in = _gla_inputs(pc[8], pc[9], pc[10], pc[11], pc[12], *dec)
        gla_l_in = _gla_inputs(pl[8], pl[9], pl[10], pl[11], pl[12], *dec)
        gla_l, gla_c = _gla_bidirectional(gla_c_in, gla_l_in)
        shared = (conv_w[l], gla_norm_g[l], w_br_conv[l], w_br_attn[l], w_br_gla[l], b_gate[l], w_out[l])
        out_l = _mixer_output(pl, att_l, gla_l, *shared)
        if not last:
            att_c = _sdpa_blocks(q_c, k_c, v_c)
            out_c = _mixer_output(pc, att_c, gla_c, *shared)
            xc = xc + gt_c * _rmsnorm(out_c, g_post[l])
        x = x + gt_l * _rmsnorm(out_l, g_post[l])
    return x


DEPTH_2 = 1

HEAD_DIM_2 = 64
A_HEADS = 4
A_VDIM = 2 * HEAD_DIM_2
B_HEADS = 8
B_KV_HEADS = 2
B_WINDOW = 128
C_HEADS = 8
C_KV_HEADS = 2
CMP_BLOCK = 32
CMP_STRIDE = 16
CMP_HIDDEN = 256
SEL_BLOCK = 64
N_SELECT = 16
C_WINDOW = 512
MIX_WIDTH = B_HEADS * HEAD_DIM_2
D_FF = 4 * D_MODEL
NUM_BUCKETS = 32
MAX_DISTANCE = 128
TOTAL_HEADS = A_HEADS + B_HEADS + C_HEADS
SEL_Q_BLOCK = 64
NEG_INF = -1e30
FORCE_BONUS = 1e4

SPLIT_SIZES = (
    A_HEADS * 2 * HEAD_DIM_2,
    A_HEADS * 2 * HEAD_DIM_2,
    A_HEADS * A_VDIM,
    B_HEADS * HEAD_DIM_2,
    B_KV_HEADS * HEAD_DIM_2,
    B_KV_HEADS * HEAD_DIM_2,
    C_HEADS * HEAD_DIM_2,
    6 * C_KV_HEADS * HEAD_DIM_2,
    C_HEADS * 3,
    N_BRANCH * D_MODEL,
)
IN_COLS = sum(SPLIT_SIZES)


def rms_norm(x, g):
    xf = x.astype(jnp.float32)
    y = xf * lax.rsqrt(jnp.mean(xf * xf, axis=-1, keepdims=True) + EPS)
    return (y * g.astype(jnp.float32)).astype(x.dtype)

def rel_bucket(dist):
    n = jnp.maximum(dist, 0)
    max_exact = NUM_BUCKETS // 2
    nf = jnp.maximum(n, 1).astype(jnp.float32)
    large = max_exact + (jnp.log(nf / max_exact) / math.log(MAX_DISTANCE / max_exact)
                         * (NUM_BUCKETS - max_exact)).astype(jnp.int32)
    large = jnp.minimum(large, NUM_BUCKETS - 1)
    return jnp.where(n < max_exact, n, large)

def diff_attention(q, k, v, lam, bias_tab):
    B, S, H, _, D = q.shape
    nb = S // Q_BLOCK
    scale = D ** -0.5
    k_pos = jnp.arange(S)
    qb = q.reshape(B, nb, Q_BLOCK, H, 2, D).transpose(1, 0, 2, 3, 4, 5)

    def block(args):
        i, qi = args
        q_pos = i * Q_BLOCK + jnp.arange(Q_BLOCK)
        dist = q_pos[:, None] - k_pos[None, :]
        mask = dist >= 0
        bias = bias_tab[rel_bucket(dist)].transpose(2, 0, 1).astype(jnp.float32)
        s = jnp.einsum('bqhcd,bkhcd->cbhqk', qi, k).astype(jnp.float32) * scale + bias
        p = jax.nn.softmax(jnp.where(mask, s, NEG_INF), axis=-1)
        w = p[0] - lam * p[1]
        return jnp.einsum('bhqk,bkhe->bqhe', w.astype(v.dtype), v)

    out = lax.map(block, (jnp.arange(nb), qb))
    return out.transpose(1, 0, 2, 3, 4).reshape(B, S, H, v.shape[-1])

def banded_attention(q, k, v, bias_tab, window, sink=None):
    B, S, H, D = q.shape
    G = k.shape[2]
    R = H // G
    nb = S // Q_BLOCK
    n_prev = -(-window // Q_BLOCK)
    kw = (n_prev + 1) * Q_BLOCK

    def band(t):
        tb = t.reshape(B, nb, Q_BLOCK, G, D)
        tb = jnp.pad(tb, ((0, 0), (n_prev, 0), (0, 0), (0, 0), (0, 0)))
        return jnp.concatenate([tb[:, j:j + nb] for j in range(n_prev + 1)], axis=2)

    kb, vb = band(k), band(v)
    qb = q.reshape(B, nb, Q_BLOCK, G, R, D)
    r = jnp.arange(Q_BLOCK)
    c = jnp.arange(kw)
    dist = n_prev * Q_BLOCK + r[:, None] - c[None, :]
    k_pos = (jnp.arange(nb)[:, None] - n_prev) * Q_BLOCK + c[None, :]
    mask = ((dist >= 0) & (dist < window))[None] & (k_pos >= 0)[:, None, :]
    bias = bias_tab[rel_bucket(dist)].reshape(Q_BLOCK, kw, G, R).transpose(2, 3, 0, 1).astype(jnp.float32)
    s = jnp.einsum('bnqgrd,bnkgd->bngrqk', qb, kb).astype(jnp.float32) * D ** -0.5 + bias
    s = jnp.where(mask[:, None, None], s, NEG_INF)
    if sink is None:
        p = jax.nn.softmax(s, axis=-1)
    else:
        sk = sink.astype(jnp.float32).reshape(G, R, 1, 1)
        m = jnp.maximum(jnp.max(s, axis=-1, keepdims=True), sk)
        e = jnp.exp(s - m)
        p = e / (jnp.sum(e, axis=-1, keepdims=True) + jnp.exp(sk - m))
    o = jnp.einsum('bngrqk,bnkgd->bnqgrd', p.astype(v.dtype), vb)
    return o.reshape(B, S, H, D)

def compress_blocks(t, pos, w1, w2):
    B, S, G, D = t.shape
    nc = (S - CMP_BLOCK) // CMP_STRIDE + 1
    idx = jnp.arange(nc)[:, None] * CMP_STRIDE + jnp.arange(CMP_BLOCK)[None, :]
    blocks = t[:, idx] + pos[None, None, :, None, :]
    flat = blocks.transpose(0, 1, 3, 2, 4).reshape(B, nc, G, CMP_BLOCK * D)
    return jax.nn.gelu(flat @ w1) @ w2

def nsa_attention(q, kc, vc, ks, vs, kw, vw, gates, bias_tab):
    B, S, H, D = q.shape
    G = ks.shape[2]
    R = H // G
    nc = kc.shape[1]
    scale = D ** -0.5
    qg = q.reshape(B, S, G, R, D)
    t_pos = jnp.arange(S)

    c_start = jnp.arange(nc) * CMP_STRIDE
    cmask = (c_start + CMP_BLOCK - 1)[None, :] <= t_pos[:, None]
    s = jnp.einsum('bsgrd,bcgd->bgrsc', qg, kc).astype(jnp.float32) * scale
    p_cmp = jnp.where(cmask, jax.nn.softmax(jnp.where(cmask, s, NEG_INF), axis=-1), 0.0)
    o_cmp = jnp.einsum('bgrsc,bcgd->bsgrd', p_cmp.astype(vc.dtype), vc).reshape(B, S, H, D)

    n_blk = S // SEL_BLOCK
    j_start = jnp.arange(n_blk) * SEL_BLOCK
    overlap = ((c_start[:, None] < j_start[None, :] + SEL_BLOCK)
               & (c_start[:, None] + CMP_BLOCK > j_start[None, :])).astype(jnp.float32)
    imp = jnp.einsum('bgrsc,cj->bgsj', p_cmp, overlap)
    cur = t_pos // SEL_BLOCK
    jj = jnp.arange(n_blk)
    valid = j_start[None, :] <= t_pos[:, None]
    forced = (jj[None, :] == 0) | (jj[None, :] == cur[:, None]) | (jj[None, :] == cur[:, None] - 1)
    score = jnp.where(valid, imp + jnp.where(forced, FORCE_BONUS, 0.0), NEG_INF)
    n_sel = min(N_SELECT, n_blk)
    _, sel_idx = lax.top_k(score, n_sel)

    kbk = ks.reshape(B, n_blk, SEL_BLOCK, G, D).transpose(0, 3, 1, 2, 4)
    vbk = vs.reshape(B, n_blk, SEL_BLOCK, G, D).transpose(0, 3, 1, 2, 4)
    nqb = S // SEL_Q_BLOCK
    qs = qg.reshape(B, nqb, SEL_Q_BLOCK, G, R, D).transpose(1, 0, 2, 3, 4, 5)
    idx_b = sel_idx.reshape(B, G, nqb, SEL_Q_BLOCK, n_sel).transpose(2, 0, 1, 3, 4)
    bi = jnp.arange(B)[:, None, None, None]
    gi = jnp.arange(G)[None, :, None, None]
    bias_g = bias_tab.reshape(NUM_BUCKETS, G, R).transpose(1, 0, 2)

    def sel_block(args):
        i, qi, ii = args
        kg = kbk[bi, gi, ii]
        vg = vbk[bi, gi, ii].reshape(B, G, SEL_Q_BLOCK, n_sel * SEL_BLOCK, D)
        q_pos = i * SEL_Q_BLOCK + jnp.arange(SEL_Q_BLOCK)
        k_pos = (ii[..., None] * SEL_BLOCK + jnp.arange(SEL_BLOCK)).reshape(B, G, SEL_Q_BLOCK, n_sel * SEL_BLOCK)
        dist = q_pos[None, None, :, None] - k_pos
        mask = dist >= 0
        bias = bias_g[gi, rel_bucket(dist)].transpose(0, 1, 4, 2, 3).astype(jnp.float32)
        s = jnp.einsum('bqgrd,bgqnkd->bgrqnk', qi, kg).reshape(B, G, R, SEL_Q_BLOCK, n_sel * SEL_BLOCK)
        s = s.astype(jnp.float32) * scale + bias
        p = jax.nn.softmax(jnp.where(mask[:, :, None], s, NEG_INF), axis=-1)
        return jnp.einsum('bgrqk,bgqkd->bqgrd', p.astype(vg.dtype), vg)

    o_sel = lax.map(sel_block, (jnp.arange(nqb), qs, idx_b))
    o_sel = o_sel.transpose(1, 0, 2, 3, 4, 5).reshape(B, S, H, D)

    o_win = banded_attention(q, kw, vw, bias_tab, C_WINDOW)

    g = jax.nn.sigmoid(gates.astype(jnp.float32)).astype(q.dtype)
    out = g[..., 0:1] * o_cmp + g[..., 1:2] * o_sel + g[..., 2:3] * o_win
    return out.reshape(B, S, H * D)

def second_inputs(seed: int = 0) -> dict:
    key = jax.random.key(seed)
    ks = jax.random.split(key, 17)

    def nrm(k, shape, scale):
        return jax.random.normal(k, shape, jnp.float32) * scale

    return {
        'x': nrm(ks[0], (BATCH, SEQ, D_MODEL), 1.0),
        'w_in': nrm(ks[1], (DEPTH_2, D_MODEL, IN_COLS), D_MODEL ** -0.5),
        'qk_gain': 1.0 + nrm(ks[2], (DEPTH_2, 8, HEAD_DIM_2), 0.1),
        'diff_lambda': nrm(ks[3], (DEPTH_2, 4, HEAD_DIM_2), 0.1),
        'diff_subln': 1.0 + nrm(ks[4], (DEPTH_2, A_VDIM), 0.1),
        'sinks': nrm(ks[5], (DEPTH_2, B_HEADS), 0.5),
        'cmp_pos': nrm(ks[6], (DEPTH_2, 2, CMP_BLOCK, HEAD_DIM_2), 0.5),
        'cmp_w1': nrm(ks[7], (DEPTH_2, 2, CMP_BLOCK * HEAD_DIM_2, CMP_HIDDEN), (CMP_BLOCK * HEAD_DIM_2) ** -0.5),
        'cmp_w2': nrm(ks[8], (DEPTH_2, 2, CMP_HIDDEN, HEAD_DIM_2), CMP_HIDDEN ** -0.5),
        'w_branch': nrm(ks[9], (DEPTH_2, N_BRANCH, MIX_WIDTH, D_MODEL), MIX_WIDTH ** -0.5),
        'w_out': nrm(ks[10], (DEPTH_2, D_MODEL, D_MODEL), D_MODEL ** -0.5),
        'norm_mix': 1.0 + nrm(ks[11], (DEPTH_2, D_MODEL), 0.1),
        'norm_mlp': 1.0 + nrm(ks[12], (DEPTH_2, D_MODEL), 0.1),
        'w_up': nrm(ks[13], (DEPTH_2, D_MODEL, D_FF), D_MODEL ** -0.5),
        'w_down': nrm(ks[14], (DEPTH_2, D_FF, D_MODEL), D_FF ** -0.5),
        'rel_bias': nrm(ks[15], (NUM_BUCKETS, TOTAL_HEADS), 0.5),
    }

def second_block(x, w_in, qk_gain, diff_lambda, diff_subln, sinks, cmp_pos, cmp_w1, cmp_w2,
              w_branch, w_out, norm_mix, norm_mlp, w_up, w_down, rel_bias):
    B, S, _ = x.shape
    points = []
    acc = 0
    for size in SPLIT_SIZES[:-1]:
        acc += size
        points.append(acc)
    bias_a = rel_bias[:, :A_HEADS]
    bias_b = rel_bias[:, A_HEADS:A_HEADS + B_HEADS]
    bias_c = rel_bias[:, A_HEADS + B_HEADS:]

    for layer in range(DEPTH_2):
        h = rms_norm(x, norm_mix[layer])
        proj = h @ w_in[layer]
        aq, ak, av, bq, bk, bv, cq, ckv, cg, mg = jnp.split(proj, points, axis=-1)
        gains = qk_gain[layer]

        aq = rms_norm(aq.reshape(B, S, A_HEADS, 2, HEAD_DIM_2), gains[0])
        ak = rms_norm(ak.reshape(B, S, A_HEADS, 2, HEAD_DIM_2), gains[1])
        av = av.reshape(B, S, A_HEADS, A_VDIM)
        lmb = diff_lambda[layer].astype(jnp.float32)
        lam_init = 0.8 - 0.6 * math.exp(-0.3 * layer)
        lam = jnp.exp(jnp.sum(lmb[0] * lmb[1])) - jnp.exp(jnp.sum(lmb[2] * lmb[3])) + lam_init
        oa = diff_attention(aq, ak, av, lam, bias_a)
        oa = (rms_norm(oa, diff_subln[layer]) * (1.0 - lam_init)).reshape(B, S, MIX_WIDTH)

        bq = rms_norm(bq.reshape(B, S, B_HEADS, HEAD_DIM_2), gains[2])
        bk = rms_norm(bk.reshape(B, S, B_KV_HEADS, HEAD_DIM_2), gains[3])
        bv = bv.reshape(B, S, B_KV_HEADS, HEAD_DIM_2)
        ob = banded_attention(bq, bk, bv, bias_b, B_WINDOW, sinks[layer]).reshape(B, S, MIX_WIDTH)

        cq = rms_norm(cq.reshape(B, S, C_HEADS, HEAD_DIM_2), gains[4])
        ckv = ckv.reshape(B, S, 6, C_KV_HEADS, HEAD_DIM_2)
        kc = rms_norm(compress_blocks(ckv[:, :, 0], cmp_pos[layer, 0], cmp_w1[layer, 0], cmp_w2[layer, 0]), gains[5])
        vc = compress_blocks(ckv[:, :, 1], cmp_pos[layer, 1], cmp_w1[layer, 1], cmp_w2[layer, 1])
        ksel = rms_norm(ckv[:, :, 2], gains[6])
        kwin = rms_norm(ckv[:, :, 4], gains[7])
        oc = nsa_attention(cq, kc, vc, ksel, ckv[:, :, 3], kwin, ckv[:, :, 5],
                           cg.reshape(B, S, C_HEADS, 3), bias_c)

        branches = jnp.stack([oa, ob, oc], axis=0)
        y = jnp.einsum('nbsm,nmd->bsnd', branches, w_branch[layer])
        gate = jax.nn.sigmoid(mg.reshape(B, S, N_BRANCH, D_MODEL).astype(jnp.float32)).astype(y.dtype)
        x = x + jnp.sum(gate * y, axis=2) @ w_out[layer]

        h = rms_norm(x, norm_mlp[layer])
        x = x + jnp.square(jax.nn.relu(h @ w_up[layer])) @ w_down[layer]
    return x


def setup_inputs(seed=0):
    out = dict(first_inputs(seed))
    for name, value in second_inputs(seed + 1).items():
        if name != "x":
            out[name + "_2"] = value
    return out


def reference(
    x, c, ctx, c_ctx, w_ada, b_ada, g_pre, g_post, w_in, conv_w, q_norm_g, k_norm_g,
    w_decay_fwd, b_decay_fwd, w_decay_bwd, b_decay_bwd, gla_norm_g, w_br_conv, w_br_attn,
    w_br_gla, b_gate, w_out, w_in_2, qk_gain_2, diff_lambda_2, diff_subln_2, sinks_2, cmp_pos_2,
    cmp_w1_2, cmp_w2_2, w_branch_2, w_out_2, norm_mix_2, norm_mlp_2, w_up_2, w_down_2,
    rel_bias_2,
):
    x = first_block(
        x, c, ctx, c_ctx, w_ada, b_ada, g_pre, g_post, w_in, conv_w, q_norm_g, k_norm_g,
        w_decay_fwd, b_decay_fwd, w_decay_bwd, b_decay_bwd, gla_norm_g, w_br_conv, w_br_attn,
        w_br_gla, b_gate, w_out,
    )
    return second_block(
        x, w_in_2, qk_gain_2, diff_lambda_2, diff_subln_2, sinks_2, cmp_pos_2, cmp_w1_2,
        cmp_w2_2, w_branch_2, w_out_2, norm_mix_2, norm_mlp_2, w_up_2, w_down_2, rel_bias_2,
    )


_drawn_inputs = setup_inputs


def setup_inputs(seed=0):
    import zlib

    import numpy as np

    out = dict(_drawn_inputs(seed))
    spreads = {}
    factors = {'g_post': 3.087,
     'q_norm_g': 8.0,
     'k_norm_g': 8.0,
     'b_decay_fwd': 8.0,
     'b_decay_bwd': 8.0,
     'gla_norm_g': 7.551,
     'b_gate': 8.0,
     'sinks_2': 50.693,
     'qk_gain_2': 3.066,
     'diff_subln_2': 4.12}
    for name, (base, spread) in spreads.items():
        noise = np.random.default_rng([zlib.crc32(name.encode()), seed]).standard_normal(out[name].shape)
        drawn = base * np.exp(spread * noise) if base else spread * noise
        out[name] = __import__('jax').numpy.asarray(drawn.astype(out[name].dtype))
    for name, factor in factors.items():
        out[name] = (out[name] * factor).astype(out[name].dtype)
    return out
```

```python
from contextlib import ExitStack, contextmanager

import numpy as np

import concourse.bass as bass
from concourse import mybir

F32 = mybir.dt.float32
ACT = mybir.ActivationFunctionType
ALU = mybir.AluOpType
AX = mybir.AxisListType
ds = bass.ds

P = 128
D = 1024
KT = D // P
LAT, CTX = 512, 256
ALL = LAT + CTX
LT, CT = LAT // P, CTX // P
NT = LT + CT
DEPTH = 2
HEADS, HD = 8, 128
GHEADS, DK, DV = 4, 128, 256
RANK = 16
TAU = 16.0
EPS = 1e-6
LEVELS = 7
NEG = -1e30

CB, CC, CX, CZ = 0, 1024, 2048, 3072
CQ = 4096
CK = CQ + HEADS * HD
CV = CK + 256
CZA = CV + 256
GQ = CZA + 1024
GK = GQ + 512
GV = GK + 512
GR = GV + 1024
GZ = GR + 2 * RANK
CMG = GZ + 1024

AQ, AK, AV = 0, 512, 1024
BQ = 1536
BK = BQ + 512
BV = BK + 128
CQ2 = BV + 128
CKV = CQ2 + 512
CG = CKV + 768
MG2 = CG + 24
NB2 = 31
BUCKETS = 32
TOE = LAT + P - 1
FF = 4096

R_BADA, R_GPRE, R_GPOST, R_CONV, R_GLAG, R_BG, R_QG, R_KG, R_C = 0, 24, 32, 40, 64, 66, 90, 91, 92
R_ROWS = 108
LAM0 = 0.8 - 0.6
GELU = float(np.sqrt(2 / np.pi))
N_PHASES1 = 1 + 11 * DEPTH
S_GAIN, S_SUB, S_MIX, S_MLP = 0, 8, 9, 17
S_ROWS = 25

RING = 4


def constants():
    i = np.arange(P)
    c = {"ident": np.eye(P), "ones": np.ones((P, P)), "blk": (i[:, None] // 64 == i[None] // 64),
         "anti": np.eye(P)[::-1]}
    rot = np.zeros((P, P))
    for d in range(P):
        if d % 64 < 32:
            rot[d + 32, d] = -1
        else:
            rot[d - 32, d] = 1
    c["rot"] = rot
    t = np.arange(LAT)
    pos = np.stack([t // 64, t % 64]).astype(np.float32)
    freq = (np.float32(10000.0) ** (-np.arange(32, dtype=np.float32) * np.float32(2.0) / np.float32(64))).astype(np.float32)
    ang = pos[i // 64] * freq[i % 32][:, None]
    c["cos"], c["sin"] = np.cos(ang), np.sin(ang)
    s, t = i[:, None], i[None, :]
    sums, pairs = [], []
    for back in (False, True):
        m = np.zeros((9, P, P))
        k = np.zeros((8, P, P))
        m[0], m[8] = (s <= t), (s > t)
        for lv in range(LEVELS):
            h = 64 >> lv
            mid = (t // (2 * h)) * 2 * h + h
            m[1 + lv] = np.where(t >= mid, (s >= mid) & (s <= t), (s > t) & (s < mid))
            k[lv] = (s // (2 * h) == t // (2 * h)) & (s % (2 * h) < h) & (t % (2 * h) >= h)
        k[7] = s == t
        if back:
            m, k = m[:, ::-1, ::-1], k[:, ::-1, ::-1]
        sums.append(m.transpose(1, 0, 2).reshape(P, -1) / TAU)
        pairs.append(k.transpose(1, 0, 2).reshape(P, -1))
    c["sums"], c["pairs"] = np.concatenate(sums, 1), np.concatenate(pairs, 1)
    return np.concatenate([np.asarray(v, np.float32) for v in c.values()], axis=1)


C_AT = {}
_at = 0
for _n, _w in (("ident", P), ("ones", P), ("blk", P), ("anti", P), ("rot", P), ("cos", LAT), ("sin", LAT),
               ("sums", 2 * 9 * P), ("pairs", 2 * 8 * P)):
    C_AT[_n] = (_at, _w)
    _at += _w
C_COLS = _at


C2_COLS = 2 * (TOE + 1) + 2 * LT * 32


def constants2():
    dist = LAT - 1 - np.arange(TOE)
    n = np.maximum(dist, 0)
    nf = np.maximum(n, 1).astype(np.float32)
    large = 16 + (np.log(nf / np.float32(16)) / np.float32(np.log(128 / 16)) * 16).astype(np.int32)
    bucket = np.where(n < 16, n, np.minimum(large, BUCKETS - 1))
    out = np.zeros((P, 2 * (TOE + 1) + 2 * LT * 32), np.float32)
    for w, ok in enumerate((dist >= 0, (dist >= 0) & (dist < 128))):
        b = np.where(ok, bucket, BUCKETS)
        out[b, w * (TOE + 1) + np.arange(TOE)] = 1
    t = np.arange(LAT)
    keep = (np.arange(NB2)[None] * 16 + 31 <= t[:, None]).reshape(LT, P, NB2).transpose(1, 0, 2)
    base = 2 * (TOE + 1)
    m = out[:, base:].reshape(P, 2, LT, 32)
    m[:, 0, :, :NB2] = keep
    m[:, 1, :, :NB2] = np.where(keep, 0, NEG)
    return out


class Steps:

    def __init__(self, eng, sem):
        self.eng, self.sem, self.base, self.k = eng, sem, 0, 0

    def __call__(self, ins):
        ins.then_inc(self.sem, 1)
        self.k += 1

    def settle(self):
        self.eng.wait_ge(self.sem, self.base + self.k)

    @contextmanager
    def loop(self, i, n, per):
        start = self.base + self.k
        self.base, self.k = start + i * per, 0
        yield
        assert self.k == per, (self.k, per)
        self.base, self.k = start + n * per, 0


class Turns:

    def __init__(self, size):
        self.size, self.k, self.add = size, 0, 0

    def slot(self):
        return self.k % self.size

    def earlier(self):
        return self.k // self.size + self.add

    def number(self):
        return self.k + self.add * self.size

    def next(self):
        self.k += 1

    def uses_of(self, slot):
        return (self.k - slot + self.size - 1) // self.size + self.add

    @contextmanager
    def loop(self, i, n, per):
        assert per % self.size == 0, per
        start = self.k
        self.add = i * (per // self.size)
        yield
        assert self.k == start + per, (self.k - start, per)
        self.k, self.add = start + n * per, 0


N_INPUTS = 3 + 10 * DEPTH + 5


def two_blocks(nc, a, out, stop=None):
    ctx = ExitStack()
    with ctx:
        def sb(name, shape):
            return ctx.enter_context(nc.sbuf_tensor(name, shape, F32))

        def sem(name):
            return ctx.enter_context(nc.semaphore(name))

        ring = sb("ring", [P, RING, KT, P])
        xT = sb("xT", [P, KT, ALL])
        hT = sb("hT", [P, KT, ALL])
        con = sb("con", [P, C_COLS])
        par = [sb(f"par{l}", [P, R_ROWS]) for l in range(DEPTH)]
        par2 = sb("par2", [P, S_ROWS])
        modl = sb("modl", [P, 24, 2])
        scale1 = sb("scale1", [P, KT, 2])
        gpost = sb("gpost", [P, KT, 2])
        half_bg = sb("half_bg", [P, 24])
        stat = sb("stat", [P, 4, 8])
        FREE = 2 * KT * ALL + 17600
        arena = sb("arena", [P, FREE])
        ps = ctx.enter_context(nc.psum_tensor("ps", [P, 8 * 512], F32))
        small = sb("small", [P, 96])
        cond_t, cond_s = small[:, 0:16], small[:, 16:32]
        cond = small[:, 32:48].rearrange("p (a b) -> p a b", a=2)
        eps, one = small[:, 48:49], small[:, 49:50]
        consts, onec = eps, one
        used = [0]

        def take(*shape, at=None):
            n = int(np.prod(shape))
            o = used[0] if at is None else at
            used[0] = o + n
            assert used[0] <= FREE, (shape, used[0], FREE)
            v = arena[:, o:o + n]
            if len(shape) == 2:
                v = v.rearrange("p (a b) -> p a b", a=shape[0])
            if len(shape) == 3:
                v = v.rearrange("p (a b c) -> p a b c", a=shape[0], b=shape[1])
            return v

        def const(name):
            o, w = C_AT[name]
            return con[:, o:o + w]

        ident, ones, blk, anti, rot = (const(n) for n in ("ident", "ones", "blk", "anti", "rot"))
        cos, sin = const("cos"), const("sin")
        sums = const("sums").rearrange("p (d n) -> p d n", d=2)
        pairs = const("pairs").rearrange("p (d l t) -> p d l t", d=2, l=8)

        y = take(KT, ALL)
        acc = take(KT, ALL)
        base = used[0]
        y_in = take(NT, D, at=0)
        tab = [take(P) for _ in range(3)]
        sqb = take(2, ALL, at=base)
        rs = take(ALL)
        lnb = take(ALL)
        tha = take(ALL)
        tmp = take(ALL)
        conv_u = take(LAT + 2 + CTX + 2)
        conv_t = take(ALL)
        bcopy = take(ALL)
        kT = take(2, ALL, at=base)
        vN = take(NT, 256)
        qT = take(2, ALL)
        qsq = take(ALL)
        qln = take(ALL)
        qrs = take(ALL)
        rope_t = take(LAT)
        rope_s = take(LAT)
        prob = take(2, ALL)
        pT = take(NT, LAT)
        pTc = take(CT, CTX)
        zth = take(ALL)
        zsi = take(ALL)
        gr = take(ALL, at=base)
        gwd = take(2, 512)
        gq = take(ALL)
        gk = take(ALL)
        gv = take(NT, DV)
        gla = take(2, NT, P)
        gtmp = take(2, ALL)
        gE = take(9, P)
        gqE = take(3, 8 * P)
        gkE = take(2, 8 * P)
        gam = take(8, P)
        gatt = take(2, P)
        gkN = take(2, P)
        gS = take(2, DV)
        gdec = take(3)
        gsq = gqE.rearrange("p a b -> p (a b)")[:, 0:2 * ALL].rearrange("p (a b) -> p a b", a=2)

        spare = [C_AT["cos"][0]]

        def take_con(*shape):
            n = int(np.prod(shape))
            o = spare[0]
            spare[0] = o + n
            assert spare[0] <= C_COLS
            v_ = con[:, o:o + n]
            if len(shape) == 2:
                v_ = v_.rearrange("p (a b) -> p a b", a=shape[0])
            return v_

        con2 = take_con(C2_COLS)
        onehot = con2[:, 0:2 * (TOE + 1)].rearrange("p (w m) -> p w m", w=2)
        cmask = con2[:, 2 * (TOE + 1):].rearrange("p (k t c) -> p k t c", k=2, t=LT)
        vA = take_con(LT, 512)
        vB, vS, vW = (take_con(LT, P) for _ in range(3))
        y2 = take(12, LAT, at=0)
        acc2 = acc
        kB, kS, kW = take(LAT, at=base), take(LAT), take(LAT)
        gates = take(LT, 24)
        kc = take(64)
        vc = take(2, 64)
        lam, sinkb = small[:, 50:54], small[:, 54:62]
        stat2 = small[:, 64:96].rearrange("p (a b) -> p a b", a=4)
        n2sq, n2ln, n2rs, n2raw = take(LAT), take(LAT), take(LAT), take(LAT)
        assert used[0] >= base + 4 * ALL
        base2 = used[0]
        relb = take(20, at=base2)
        brow = take(2, TOE + 1)
        lamb = take(256)
        lamp = take(64)
        prep_end = used[0]
        w1k = take(32, 256, at=0)
        w1v = take(32, 256, at=base2)
        tk = take(2, LAT)
        posrow = take(2, P)
        pos = take(2, 32)
        tpos = take(NB2, 32)
        w2k, w2v = take(2, P), take(2, 64)
        hid = take(2, 128)
        hx = take(4, 128)
        qt_ = take(4, LAT, at=base2)
        wb = take(5, LAT)
        vAh = take(LT, P)
        prob2 = take(4, LAT)
        pT2 = take(2, LT, LAT)
        pTcmp = take(LAT)
        tha2, tmp2 = take(LAT, at=base2), take(LAT)
        U = take(FF // P, LAT, at=0)
        rl = take(LAT)
        ob = take(LT, D, at=0)

        def bank(b, n=512):
            return ps[:, b * 512:b * 512 + n]

        def pair(s, n=ALL):
            return ps[:, s * 1024:s * 1024 + n]

        w_landed = [sem(f"w_landed{s}") for s in range(RING)]
        w_used = sem("w_used")
        pair_free = [sem(f"pair_free{s}") for s in range(2)]
        phase, inputs_in, out_done = sem("phase"), sem("inputs_in"), sem("out_done")
        act_own, dve_own = sem("act_own"), sem("dve_own")
        x_turned, par_turned = sem("x_turned"), sem("par_turned")
        sq_ready, sq_used, ms_done, rs_ready = sem("sq_ready"), sem("sq_used"), sem("ms_done"), sem("rs_ready")
        cond_tanh, cond_ready, z_tanh, c_copied = sem("cond_tanh"), sem("cond_ready"), sem("z_tanh"), sem("c_copied")
        scores_done, max_done, exp_done, prob_done = (sem(n) for n in ("scores_done", "max_done", "exp_done", "prob_done"))
        turned, pT_ready, pv_done, head_out = (sem(n) for n in ("turned", "pT_ready", "pv_done", "head_out"))
        qsq_ready, qms_done, qms_read, qrs_ready = (sem(n) for n in ("qsq_ready", "qms_done", "qms_read", "qrs_ready"))
        qn_ready, rot_done, rot_read, q_ready = (sem(n) for n in ("qn_ready", "rot_done", "rot_read", "q_ready"))
        za_tanh, za_silu = sem("za_tanh"), sem("za_silu")
        wd_zero, wd_in = sem("wd_zero"), sem("wd_in")
        dec_done, dec_ln, la_ready = sem("dec_done"), sem("dec_ln"), sem("la_ready")
        sum_done, e_ready, qk_ready, att_done = (sem(n) for n in ("sum_done", "e_ready", "qk_ready", "att_done"))
        att_ready, k_turned, kN_ready = sem("att_ready"), sem("k_turned"), sem("kN_ready")
        o_done, o_read, s_done, s_ready = sem("o_done"), sem("o_read"), sem("s_done"), sem("s_ready")
        gsq_ready, gms_done, grs_ready, gla_out = (sem(n) for n in ("gsq_ready", "gms_done", "grs_ready", "gla_out"))
        masked = sem("masked")

        relb_ready = sem("relb_ready")
        in2, tab2_turned, rows_done, rows_kept = sem("in2"), sem("tab2_turned"), sem("rows_done"), sem("rows_kept")
        rows_mm, lam_sum, w1_in, hid_ready, hid_done = (sem(n) for n in ("rows_mm", "lam_sum", "w1_in", "hid_ready", "hid_done"))
        hx_ready, gelu_arg, gelu_tanh = sem("hx_ready"), sem("gelu_arg"), sem("gelu_tanh")
        bias_in, sq2_ready, ms2_done, rs2_ready = sem("bias_in"), sem("sq2_ready"), sem("ms2_done"), sem("rs2_ready")
        n2_ready, scores2, max2, exp2 = sem("n2_ready"), sem("scores2"), sem("max2"), sem("exp2")
        prob2_ready, turned2, pT2_ready, pv2 = sem("prob2_ready"), sem("turned2"), sem("pT2_ready"), sem("pv2")
        o2_read, relu_ready, out_turned, out_copied = sem("o2_read"), sem("relu_ready"), sem("out_turned"), sem("out_copied")
        rows_dram = nc.dram_tensor("bias_rows", [20, TOE + 1], F32).ap()

        heads2, turns2 = [], 0
        for kind, g, subs in (("A", 0, ("c0", "c1")), ("B", 0, ("b",)), ("B", 1, ("b",)),
                              ("C", 0, ("sel", "win", "cmp")), ("C", 1, ("sel", "win", "cmp"))):
            for qt in range(LT):
                for sub in subs:
                    lo = max(qt - 1, 0) * P if kind == "B" else 0
                    w = NB2 if sub == "cmp" else (qt + 1) * P - lo
                    tn = None if sub == "c0" else turns2
                    turns2 += tn is not None
                    heads2.append(dict(kind=kind, g=g, qt=qt, sub=sub, lo=lo, w=w, turn=tn,
                                       end=qt == LT - 1 and sub == subs[-1]))
        NS2 = len(heads2)
        NORM0 = 4
        LEAD = 3

        def mm(o, l, r, first, last):
            return nc.tensor.matmul(o, l, r, start=first, stop=last)

        def row(buf, j, lo=0, hi=None):
            if isinstance(j, int):
                return buf[:, j, lo:hi]
            return buf[:, ds(j, 1), lo:hi].rearrange("p a n -> p (a n)")

        def score_bank(n, w):
            return bank((6, 7, 0, 2)[n % 4], w)

        def col(buf, j):
            return buf[:, j:j + 1] if isinstance(j, int) else buf[:, ds(j, 1)]

        def spans(n):
            return [(0, LAT)] + ([(LAT, ALL)] if n == ALL else [])

        def gla_units(l):
            fwd = [4, 5, 0, 1, 2, 3]
            bwd = [5, 4, 3, 2, 1, 0]
            units, seen, f = [], set(), 0
            for a_, b_ in zip(fwd, bwd):
                for d, t in ((0, a_), (1, b_)):
                    full = l == 0 or t < LT
                    units.append((d, t, full, t in seen, f))
                    if full:
                        seen.add(t)
                        f += 1
            return units, f

        FILL = [[((0, 4), None, None), ((4, 8), None, None), ((8, 16), None, None), (None, (0, 2), (2, 5)),
                 (None, (5, 7), (7, 10)), (None, (10, 14), None), (None, (14, 16), None)],
                [((0, 4), None, None), ((4, 8), None, None), (None, (0, 2), (2, 4)), (None, (4, 6), (6, 7)),
                 (None, (7, 8), None)]]
        FILL_LAST = [[(None, (0, 2), None), (None, (2, 4), None), (None, (4, 6), None), (None, (6, 8), None),
                      (None, (8, 12), None), (None, (12, 15), None), (None, (15, 16), None)],
                     [(None, (0, 2), None), (None, (2, 4), None), (None, (4, 6), None), (None, (6, 7), None),
                      (None, (7, 8), None)]]
        SQUARE_AT, NORM_AT = [2, 1], [3, 2]

        GU = [gla_units(l) for l in range(DEPTH)]
        NU = 2 * NT
        F_BASE = [0, GHEADS * GU[0][1]]
        QU = [NT, LT]
        U_BASE = [0, HEADS * NT]
        NORMED = 2 + HEADS
        N_ROWS = [R_ROWS, R_ROWS, S_ROWS]

        block = ctx.enter_context(nc.Block())

        @block.sync
        def _(sp):
            tiles = Turns(RING)

            def load(src, kt=KT, m=P):
                if not (isinstance(tiles.number(), int) and tiles.number() < RING):
                    sp.wait_ge(w_used, tiles.number() + 1 - RING)
                v = src.rearrange("(k p) m -> p k m", p=P)
                s = tiles.slot()
                for h in (64, 0):
                    sp.dma_start(ring[h:h + 64, s, 0:kt, 0:m], v[h:h + 64]).then_inc(w_landed[s], 16)
                tiles.next()

            def rows(dst, r, src, c0=0):
                n, w = src.shape
                sp.dma_start(dst[r:r + n, c0:c0 + w], src).then_inc(inputs_in, 16)

            sp.dma_start(con[:], a["con"]).then_inc(inputs_in, 16)
            sp.dma_start(y_in[:, 0:LT, :], a["x"][0].rearrange("(t p) f -> p t f", p=P)).then_inc(inputs_in, 16)
            sp.dma_start(y_in[:, LT:NT, :], a["ctx"][0].rearrange("(t p) f -> p t f", p=P)).then_inc(inputs_in, 16)

            def as_rows(v):
                return v.rearrange("(r c) -> r c", c=P)

            for l in range(DEPTH):
                dst = tab[l]
                rows(dst, R_BADA, as_rows(a["b_ada"][l]))
                rows(dst, R_GPRE, as_rows(a["g_pre"][l]))
                rows(dst, R_GPOST, as_rows(a["g_post"][l]))
                rows(dst, R_CONV, a["conv_w"][l].rearrange("k (r c) -> (k r) c", c=P))
                rows(dst, R_GLAG, as_rows(a["gla_norm_g"][l]))
                rows(dst, R_BG, as_rows(a["b_gate"][l]))
                rows(dst, R_QG, as_rows(a["q_norm_g"][l]))
                rows(dst, R_KG, as_rows(a["k_norm_g"][l]))
                rows(dst, R_C, as_rows(a["c"][0]))
                rows(dst, R_C + 8, as_rows(a["c_ctx"]))
            rows(tab[2], S_GAIN, a["qk_gain_2"][0])
            rows(tab[2], S_GAIN, a["qk_gain_2"][0], c0=64)
            rows(tab[2], S_SUB, a["diff_subln_2"])
            rows(tab[2], S_MIX, as_rows(a["norm_mix_2"][0]))
            rows(tab[2], S_MLP, as_rows(a["norm_mlp_2"][0]))

            for l in range(DEPTH):
                ada, w = a["w_ada"][l], a["w_in"][l]
                first = 0
                if l == 0:
                    for s in range(4):
                        load(ada[:, s * P:(s + 1) * P])
                    first = 1
                with sp.Fori(0, 6 - first) as i, tiles.loop(i, 6 - first, 4):
                    for s in range(4):
                        load(ada[:, ds(i * 512 + first * 512 + s * P, P)])
                with sp.Fori(0, KT) as i, tiles.loop(i, KT, 4):
                    for c in (CZ, CC, CX, CB):
                        load(w[:, ds(i * P + c, P)])

                def branch(b, src, kt=KT):
                    with sp.Fori(0, KT // 2) as i, tiles.loop(i, KT // 2, 4):
                        for s in range(2):
                            load(w[:, ds(i * 256 + CMG + b * D + s * P, P)])
                            load(src[:, ds(i * 256 + s * P, P)], kt)

                branch(0, a["w_br_conv"][l])
                for c in (CK, CK + P, CV, CV + P, CQ):
                    load(w[:, c:c + P])
                with sp.Fori(0, HEADS // 2 - 1) as i, tiles.loop(i, HEADS // 2 - 1, 4):
                    for s in range(2):
                        load(w[:, ds(i * 256 + CQ + (s + 1) * P, P)])
                        load(w[:, ds(i * 256 + CZA + s * P, P)])
                load(w[:, CQ + 7 * P:CQ + 8 * P])
                load(w[:, CZA + 6 * P:CZA + 7 * P])
                load(w[:, CZA + 7 * P:CZA + 8 * P])
                branch(1, a["w_br_attn"][l])
                load(w[:, GR:GR + 32], m=32)
                with sp.Fori(0, GHEADS) as i, tiles.loop(i, GHEADS, 4):
                    load(w[:, ds(i * P + GQ, P)])
                    load(w[:, ds(i * P + GK, P)])
                    load(w[:, ds(i * DV + GV, P)])
                    load(w[:, ds(i * DV + GV + P, P)])
                with sp.Fori(0, 2) as i, tiles.loop(i, 2, 4):
                    for s in range(4):
                        load(w[:, ds(i * 512 + GZ + s * P, P)])
                branch(2, a["w_br_gla"][l])
                with sp.Fori(0, 2) as i, tiles.loop(i, 2, 4):
                    for s in range(4):
                        load(a["w_out"][l][:, ds(i * 512 + s * P, P)])
            w = a["w_in_2"][0]
            for c in range(4):
                load(w[:, AV + c * P:AV + (c + 1) * P])
            sp.wait_ge(phase, 3 * N_PHASES1)
            sp.dma_start(con2, a["con2"]).then_inc(in2, 16)
            sp.dma_start(relb[0:BUCKETS], a["rel_bias_2"]).then_inc(in2, 16)
            sp.dma_start(lamb, a["diff_lambda_2"][0].rearrange("(o a) b -> o (a b)", o=1).to_broadcast([P, 256])).then_inc(in2, 16)
            sp.dma_start(sinkb, a["sinks_2"].to_broadcast([P, 8])).then_inc(in2, 16)
            for c in (BK, BV):
                load(w[:, c:c + P])
            for c in range(6):
                load(w[:, CKV + c * P:CKV + (c + 1) * P])
            load(w[:, CG:CG + 24], m=24)

            def load_halves(c, i):
                sp.wait_ge(w_used, tiles.number() + 1 - RING)
                s = tiles.slot()
                for g in (1, 0):
                    sp.dma_start(ring[:, s, :, g * 64:(g + 1) * 64],
                                 w[:, ds(i * 64 + c + g * 256, 64)].rearrange("(k p) m -> p k m", p=P))\
                        .then_inc(w_landed[s], 16)
                tiles.next()

            sp.wait_ge(rows_kept, 48)
            with sp.Fori(0, 4) as i, tiles.loop(i, 4, 4):
                load(w[:, ds(i * P + AQ, P)])
                load(w[:, ds(i * P + AK, P)])
                load_halves(BQ, i)
                load_halves(CQ2, i)
                sp.wait_ge(phase, 3 * (N_PHASES1 + 3))
                sp.wait_ge(scores2, i * NS2)
                for k in (4, 3, 2, 1, 0):
                    r = rows_dram[ds(i + 4 * k, 1), 0:LAT]
                    sp.dma_start(wb[:, k], bass.AP(r.tensor, r.offset, [[1, P], [1, LAT]])).then_inc(bias_in, 16)
            for b in range(3):
                wbr = a["w_branch_2"][0, b]
                with sp.Fori(0, KT // 2) as i, tiles.loop(i, KT // 2, 4):
                    for s in range(2):
                        load(w[:, ds(i * 256 + MG2 + b * D + s * P, P)])
                        src = wbr[:, ds(i * 256 + s * P, P)]
                        if b == 0:
                            load(src, 4)
                        else:
                            sp.wait_ge(w_used, tiles.number() + 1 - RING)
                            v = src.rearrange("(h k p) m -> h p k m", h=2, p=64)
                            for h in (1, 0):
                                sp.dma_start(ring[h * 64:(h + 1) * 64, tiles.slot(), 0:4], v[h])\
                                    .then_inc(w_landed[tiles.slot()], 16)
                            tiles.next()
            with sp.Fori(0, 2) as i, tiles.loop(i, 2, 4):
                for s in range(4):
                    load(a["w_out_2"][0][:, ds(i * 512 + s * P, P)])
            with sp.Fori(0, 8) as i, tiles.loop(i, 8, 4):
                for s in range(4):
                    load(a["w_up_2"][0][:, ds(i * 512 + s * P, P)])
            with sp.Fori(0, 4) as i, tiles.loop(i, 4, 8):
                for s in range(2):
                    for k in range(4):
                        load(a["w_down_2"][0][k * D:(k + 1) * D, ds(i * 256 + s * P, P)])
            for t in range(LT):
                sp.wait_ge(out_copied, t + 1)
                sp.dma_start(out[0, t * P:(t + 1) * P, :], ob[:, t]).then_inc(out_done, 16)
            sp.wait_ge(out_done, 16 * LT)

        @block.gpsimd
        def _(pool):
            for l in range(DEPTH):
                pool.wait_ge(wd_zero, l + 1)
                for d, (wn, bn) in enumerate((("w_decay_fwd", "b_decay_fwd"), ("w_decay_bwd", "b_decay_bwd"))):
                    pool.dma_start(gwd[d * RANK:(d + 1) * RANK, d], a[wn][l]).then_inc(wd_in, 16)
                    pool.dma_start(gwd[32:33, d], a[bn][l:l + 1, :]).then_inc(wd_in, 16)
            pool.wait_ge(rows_done, 2)
            pool.dma_start(rows_dram[0:4], brow[0:4, 0]).then_inc(rows_kept, 16)
            pool.dma_start(rows_dram[4:12], brow[4:12, 1]).then_inc(rows_kept, 16)
            pool.dma_start(rows_dram[12:20], brow[12:20, 0]).then_inc(rows_kept, 16)
            pool.wait_ge(phase, 3 * (N_PHASES1 + 1))
            pool.wait_ge(rows_kept, 48)
            for kv, (w1, w2) in enumerate(((w1k, w2k), (w1v, w2v))):
                for h in (0, 64):
                    pool.dma_start(w1[h:h + 64], a["cmp_w1_2"][0, kv].rearrange("(j d) h -> d j h", d=64)).then_inc(w1_in, 16)
                    pool.dma_start(posrow[0:32, kv, h:h + 64], a["cmp_pos_2"][0, kv]).then_inc(w1_in, 16)
                for h in (0, 64)[:2 - kv]:
                    pool.dma_start(w2[:, :, h:h + 64], a["cmp_w2_2"][0, kv].rearrange("(k p) d -> p k d", p=P)).then_inc(w1_in, 16)

        @block.tensor
        def _(pe):
            tiles, uses = Turns(RING), Turns(2)
            ends = [0]
            norms = [0]

            def phase_end(name):
                pe.drain().then_inc(phase, 1)
                ends[0] += 3
                pe.wait_ge(phase, ends[0])
                return name == stop

            def all_read():
                for s in range(2):
                    pe.wait_ge(pair_free[s], uses.uses_of(s))

            def begin_tile():
                pe.wait_ge(w_landed[tiles.slot()], tiles.earlier() * 32 + 32)
                pe.wait_ge(pair_free[uses.slot()], uses.earlier())
                return ring[:, tiles.slot()], uses.slot()

            def end_tile(last):
                last.then_inc(w_used, 1)
                tiles.next()
                uses.next()

            def half_tile(w, s, src, lo, hi, kt=KT, m=P):
                for k in range(kt):
                    last = mm(pair(s)[0:m, lo:hi], w[:, k, 0:m], src[:, k, lo:hi], k == 0, k == kt - 1)
                return last

            def turned_tile(src, n=ALL, kt=KT, m=P):
                w, s = begin_tile()
                for lo, hi in spans(n):
                    last = half_tile(w, s, src, lo, hi, kt, m)
                end_tile(last)

            def token_tile(nt=NT, m=P):
                w, s = begin_tile()
                for t in range(nt):
                    for k in range(KT):
                        last = mm(pair(s, 1024)[:, t * m:(t + 1) * m], hT[:, k, t * P:(t + 1) * P], w[:, k, 0:m],
                                  k == 0, k == KT - 1)
                end_tile(last)

            def mean_square(n):
                for f in range(KT):
                    pe.wait_ge(sq_ready, norms[0] * KT + f + 1)
                    for lo, hi in spans(n):
                        last = mm(bank(4, 1024)[:, lo:hi], ones, sqb[:, f % 2, lo:hi], f == 0, f == KT - 1)
                    last.then_inc(sq_used, 1)
                norms[0] += 1

            pe.wait_ge(inputs_in, 16 * N_INPUTS)
            for j in range(3):
                n = N_ROWS[j]
                nc.tensor.transpose(bank(4 + j, n), tab[j][0:n, :], ident[0:n, 0:n]).then_inc(par_turned, 1)
            for f in range(KT):
                pe.wait_ge(pair_free[uses.slot()], uses.earlier())
                for t in range(NT):
                    last = nc.tensor.transpose(pair(uses.slot())[:, t * P:(t + 1) * P],
                                               y_in[:, t, f * P:(f + 1) * P], ident)
                last.then_inc(x_turned, 1)
                uses.next()
            if phase_end("load"):
                return

            def branch(n):
                with pe.Fori(0, KT // 2) as i, tiles.loop(i, KT // 2, 4), uses.loop(i, KT // 2, 4):
                    for s in range(2):
                        turned_tile(hT, n)
                        turned_tile(y, n)

            for l in range(DEPTH):
                n = ALL if l == 0 else LAT
                qu = QU[l]
                pe.wait_ge(cond_ready, l + 1)
                with pe.Fori(0, 6) as i, tiles.loop(i, 6, 4), uses.loop(i, 6, 4):
                    for _ in range(4):
                        w, s = begin_tile()
                        for k in range(KT):
                            last = mm(pair(s)[:, 0:2], w[:, k], cond[:, :, k], k == 0, k == KT - 1)
                        end_tile(last)
                if phase_end(f"ada{l}"):
                    return
                mean_square(ALL)
                if phase_end(f"norm{l}"):
                    return
                with pe.Fori(0, KT) as i, tiles.loop(i, KT, 4), uses.loop(i, KT, 4):
                    for _ in range(4):
                        turned_tile(hT, n)
                if phase_end(f"conv{l}"):
                    return
                branch(n)
                if phase_end(f"branch{l}0"):
                    return

                def norm_mm(c, m, free=None):
                    pe.wait_ge(qsq_ready, c + 1)
                    pe.wait_ge(*(free or (rot_read, c)))
                    for lo, hi in spans(m):
                        last = mm(bank(4, 1024)[:, lo:hi], ones, qsq[:, lo:hi], True, True)
                    last.then_inc(qms_done, 1)

                def rotate(c, src, free=None):
                    pe.wait_ge(qn_ready, c + 1)
                    pe.wait_ge(*(free or (qms_read, c + 1)))
                    mm(bank(4), rot, src[:, 0:LAT], True, True).then_inc(rot_done, 1)

                nb = NORMED * l
                turned_tile(hT)
                norm_mm(nb, ALL)
                rotate(nb, kT[:, 0])
                turned_tile(hT)
                norm_mm(nb + 1, ALL)
                rotate(nb + 1, kT[:, 1])
                token_tile()
                token_tile()
                turned_tile(hT, n)
                norm_mm(nb + 2, n)
                rotate(nb + 2, qT[:, 0])

                def step(off, i, kv, last_head=False):
                    q, nq = qT[:, off % 2], qT[:, (off + 1) % 2]
                    u0 = i * (2 * qu) + (U_BASE[l] + off * qu)
                    hn = i * 2 + (HEADS * l + off)
                    c = i * 2 + (nb + 3 + off)

                    def scores(t):
                        if t == 0:
                            pe.wait_ge(q_ready, c)
                        pe.wait_ge(exp_done, u0 + t)
                        qs = q[:, t * P:(t + 1) * P]
                        if t < LT:
                            mm(bank(6), qs, kT[:, kv, 0:LAT], True, True)
                            mm(bank(7, CTX), qs, kT[:, kv, LAT:ALL], True, True).then_inc(scores_done, 1)
                        else:
                            mm(bank(6, CTX), qs, kT[:, kv, LAT:ALL], True, True).then_inc(scores_done, 1)

                    def turn(t, free):
                        pe.wait_ge(prob_done, u0 + t + 1)
                        pe.wait_ge(*free)
                        for s in range(NT if t < LT else CT):
                            x = nc.tensor.transpose(bank(4, 1024)[:, s * P:(s + 1) * P],
                                                    prob[:, t % 2, s * P:(s + 1) * P], ident)
                        x.then_inc(turned, 1)

                    steps = KT * len(spans(n))

                    def fill(part):
                        if part is None:
                            return
                        if part[0] == 0:
                            begin_tile()
                        w, s = ring[:, tiles.slot()], uses.slot()
                        for k in range(*part):
                            lo, hi = spans(n)[k // KT]
                            last = mm(pair(s)[:, lo:hi], w[:, k % KT], hT[:, k % KT, lo:hi], k % KT == 0, k % KT == KT - 1)
                        if part[1] == steps:
                            end_tile(last)

                    table = FILL_LAST[l] if last_head else FILL[l]
                    for t in range(qu):
                        queries, gate1, gate2 = table[t]
                        scores(t)
                        fill(queries)
                        fill(gate1)
                        free = (pT_ready, u0 + t) if t else (head_out, hn)
                        if not last_head and t == NORM_AT[l]:
                            norm_mm(c, n, free)
                            free = (qms_read, c + 1)
                        if not last_head and t == NORM_AT[l] + 1:
                            rotate(c, nq, free)
                            free = (rot_read, c + 1)
                        fill(gate2)
                        turn(t, free)
                    fill(table[qu][1])
                    pe.wait_ge(pT_ready, u0 + qu)
                    for s in range(NT):
                        last = mm(bank(4), vN[:, s, kv * P:(kv + 1) * P], pT[:, s], s == 0, s == NT - 1)
                    if qu > LT:
                        for s in range(CT):
                            last = mm(bank(5, CTX), vN[:, LT + s, kv * P:(kv + 1) * P], pTc[:, s], s == 0, s == CT - 1)
                    last.then_inc(pv_done, 1)

                all_read()
                with pe.Fori(0, 2) as i, tiles.loop(i, 2, 4), uses.loop(i, 2, 4):
                    step(0, i, 0)
                    step(1, i, 0)
                step(0, 2, 1)
                step(1, 2, 1)
                step(0, 3, 1)
                step(1, 3, 1, True)
                if phase_end(f"attn{l}"):
                    return
                branch(n)
                if phase_end(f"branch{l}1"):
                    return

                turned_tile(hT, ALL, m=32)
                pe.wait_ge(wd_in, 64 * (l + 1))
                all_read()
                units, nf = GU[l]
                turned_tile(hT, n)

                def head(i, last_head=False):
                    hh = i + GHEADS * l
                    u0 = hh * NU
                    f0 = i * nf + F_BASE[l]
                    turned_tile(hT)
                    pe.wait_ge(grs_ready, hh * 2)
                    pe.wait_ge(s_ready, u0)
                    for d in range(2):
                        for t in range(NT):
                            last = mm(bank(4 + 2 * d, 1024)[:, t * P:(t + 1) * P], gr[0:33, t * P:(t + 1) * P],
                                      gwd[0:33, d, i * P:(i + 1) * P] if isinstance(i, int) else gwd[0:33, d, ds(i * P, P)],
                                      True, True)
                    last.then_inc(dec_done, 1)
                    token_tile()
                    token_tile()
                    pe.wait_ge(la_ready, hh * 2 + 2)

                    def exponents(j):
                        d, t, full = units[j][:3]
                        pe.wait_ge(e_ready, u0 + j)
                        if full:
                            for c in range(3):
                                last = mm(bank(c, 384), gla[:, d, t], sums[:, d, c * 384:(c + 1) * 384], True, True)
                        else:
                            for c, k in ((0, 0), (1, 8)):
                                last = mm(bank(c, P), gla[:, d, t], sums[:, d, k * P:(k + 1) * P], True, True)
                        last.then_inc(sum_done, 1)

                    def levels(j):
                        d, t, full, _, f = units[j]
                        pe.wait_ge(qk_ready, u0 + j + 1)
                        pe.wait_ge(kN_ready, u0 + j)
                        nc.tensor.transpose(bank(6, P), gkE[:, j % 2, 7 * P:8 * P], ident).then_inc(k_turned, 1)
                        if full:
                            pe.wait_ge(masked, f0 + f)
                            for lv in range(LEVELS):
                                mm(bank(3, 1024)[:, lv * P:(lv + 1) * P], gkE[:, j % 2, lv * P:(lv + 1) * P],
                                   gqE[:, j % 3, (lv + 1) * P:(lv + 2) * P], True, True)
                            mm(bank(3, 1024)[:, 7 * P:8 * P], gk[:, t * P:(t + 1) * P], gq[:, t * P:(t + 1) * P],
                               True, True).then_inc(att_done, 1)

                    def outputs(j):
                        d, t, full, _, f = units[j]
                        if full:
                            pe.wait_ge(s_ready, u0 + max(j - 1, 0))
                            pe.wait_ge(att_ready, f0 + f + 1)
                            pe.wait_ge(o_read, f0 + f)
                            for v in range(2):
                                mm(bank(5, DV)[:, v * P:(v + 1) * P], gS[:, d, v * P:(v + 1) * P], gqE[:, j % 3, 0:P],
                                   True, False)
                                last = mm(bank(5, DV)[:, v * P:(v + 1) * P], gv[:, t, v * P:(v + 1) * P], gatt[:, f % 2],
                                          False, True)
                            last.then_inc(o_done, 1)
                        pe.wait_ge(kN_ready, u0 + j + 1)
                        pe.wait_ge(s_ready, u0 + j)
                        mm(bank(7, DV), gkN[:, j % 2], gv[:, t], True, True).then_inc(s_done, 1)

                    all_read()
                    exponents(0)
                    for j in range(NU):
                        if j + 1 < NU:
                            exponents(j + 1)
                        levels(j)
                        if j:
                            outputs(j - 1)
                    outputs(NU - 1)
                    if not last_head:
                        pe.wait_ge(e_ready, u0 + NU)
                        pe.wait_ge(masked, f0 + nf)
                        turned_tile(hT, n)
                    pe.wait_ge(gsq_ready, hh + 1)
                    for lo, hi in spans(n):
                        for v in range(2):
                            last = mm(bank(4, 1024)[:, lo:hi], ones, gsq[:, v, lo:hi], v == 0, v == 1)
                    last.then_inc(gms_done, 1)

                with pe.Fori(0, GHEADS - 1) as i, tiles.loop(i, GHEADS - 1, 4), uses.loop(i, GHEADS - 1, 4):
                    head(i)
                head(GHEADS - 1, True)
                if phase_end(f"gla{l}"):
                    return
                with pe.Fori(0, 2) as i, tiles.loop(i, 2, 4), uses.loop(i, 2, 4):
                    for _ in range(4):
                        turned_tile(hT, n)
                if phase_end(f"glaz{l}"):
                    return
                branch(n)
                if phase_end(f"branch{l}2"):
                    return
                with pe.Fori(0, 2) as i, tiles.loop(i, 2, 4), uses.loop(i, 2, 4):
                    for _ in range(4):
                        turned_tile(acc, n)
                if phase_end(f"out{l}"):
                    return
                mean_square(n)
                if phase_end(f"post{l}"):
                    return
            norms2, turn_base = [0], [0]

            def block_norm_mm(c, m, n=LAT):
                pe.wait_ge(sq2_ready, c + 1)
                pe.wait_ge(rs2_ready, c)
                mm(bank(3, n), m, n2sq[:, 0:n], True, True).then_inc(ms2_done, 1)

            mean_square(LAT)
            pe.wait_ge(in2, 64)
            pe.wait_ge(relb_ready, 1)
            for w_ in range(2):
                for lo, hi in ((0, 512), (512, TOE)):
                    last = mm(pair(w_)[0:20, lo:hi], relb[0:BUCKETS + 1, 0:20], onehot[0:BUCKETS + 1, w_, lo:hi], True, True)
            last.then_inc(rows_mm, 1)
            if phase_end("norm2"):
                return
            for _ in range(4):
                token_tile(LT)
            turned_tile(hT, LAT)
            block_norm_mm(0, blk)
            token_tile(LT)
            turned_tile(hT, LAT)
            turned_tile(hT, LAT)
            turned_tile(hT, LAT)
            block_norm_mm(1, blk)
            token_tile(LT)
            turned_tile(hT, LAT)
            block_norm_mm(2, blk)
            token_tile(LT)
            token_tile(LT, m=24)
            pe.wait_ge(w1_in, 16 * 11)
            for kv in range(2):
                nc.tensor.transpose(bank(6 + kv, 32), posrow[0:32, kv], ident[0:32, 0:32]).then_inc(tab2_turned, 1)
            if phase_end("kv2"):
                return
            for kv, w1 in enumerate((w1k, w1v)):
                pe.wait_ge(hid_ready, kv + 1)
                for m in range(2):
                    for g in range(2):
                        for j in range(32):
                            last = mm(bank(6 - 2 * kv + g)[:, m * NB2:(m + 1) * NB2], w1[g * 64:(g + 1) * 64, j, m * P:(m + 1) * P],
                                      tpos[g * 64:(g + 1) * 64, :, j], j == 0, j == 31)
                last.then_inc(hid_done, 1)
            pe.wait_ge(hid_ready, 3)
            for k in range(2):
                last = mm(bank(0, 2 * NB2), w2k[:, k], hid[:, 0, k * 62:(k + 1) * 62], k == 0, k == 1)
            last.then_inc(hid_done, 1)
            block_norm_mm(3, blk, 2 * NB2)
            pe.wait_ge(hid_ready, 4)
            for g in range(2):
                for k in range(2):
                    o = k * 62 + g * NB2
                    last = mm(bank(2)[0:NB2, g * 64:(g + 1) * 64], hid[:, 1, o:o + NB2], w2v[:, k], k == 0, k == 1)
            last.then_inc(hid_done, 1)
            if phase_end("cmp"):
                return
            with pe.Fori(0, 4) as i, tiles.loop(i, 4, 4), uses.loop(i, 4, 4):
                c0 = i * 5 + NORM0
                s0, t0 = i * NS2, i * turns2
                pe.wait_ge(exp2, i * NS2)
                for c in range(4):
                    turned_tile(hT, LAT)
                    if c:
                        block_norm_mm(c0 + (c - 1), blk)
                block_norm_mm(c0 + 3, blk)
                pe.wait_ge(n2_ready, c0 + 4)
                pe.wait_ge(bias_in, i * 80 + 80)

                def scores(n):
                    u = heads2[n]
                    b = score_bank(n, u["w"])
                    pe.wait_ge(exp2, s0 + max(n - 3, 0))
                    g, q0 = u["g"] * 64, u["qt"] * P
                    if u["kind"] == "A":
                        g = 64 * (u["sub"] == "c1")
                        q, k = qt_[g:g + 64, 0, q0:q0 + P], qt_[g:g + 64, 1]
                    elif u["kind"] == "B":
                        q, k = qt_[g:g + 64, 2, q0:q0 + P], kB[g:g + 64]
                    else:
                        q, k = qt_[g:g + 64, 3, q0:q0 + P], (kW if u["sub"] == "win" else kS)[g:g + 64]
                    if u["sub"] == "cmp":
                        mm(b, q, kc[g:g + 64, u["g"] * NB2:(u["g"] + 1) * NB2], True, False)
                        mm(b, ident, cmask[:, 1, u["qt"], 0:NB2], False, True).then_inc(scores2, 1)
                    else:
                        slot = {"A": 0, "B": 1, "C": 3}[u["kind"]] + u["g"]
                        mm(b, q, k[:, u["lo"]:u["lo"] + u["w"]], True, False)
                        mm(b, anti, wb[:, slot, LAT - u["w"]:LAT], False, True).then_inc(scores2, 1)

                def turn(n):
                    u = heads2[n]
                    tn = u["turn"]
                    if tn is None:
                        return
                    pe.wait_ge(prob2_ready, t0 + tn + 1)
                    pe.wait_ge(pT2_ready, t0 + (tn - 1) if tn else i * turns2)
                    src = prob2[:, (n - 1 if u["kind"] == "A" else n) % 4]
                    if u["sub"] == "cmp":
                        last = nc.tensor.transpose(bank(4 + tn % 2)[0:NB2, 0:P], src[:, 0:NB2], ident)
                    else:
                        for k in range(u["w"] // P):
                            last = nc.tensor.transpose(bank(4 + tn % 2)[:, k * P:(k + 1) * P], src[:, k * P:(k + 1) * P], ident)
                    last.then_inc(turned2, 1)

                def values(n):
                    u = heads2[n]
                    g = u["g"] * 64
                    pe.wait_ge(pT2_ready, t0 + u["turn"] + 1)
                    pe.wait_ge(o2_read, i * 3 + {"A": 0, "B": 1, "C": 2}[u["kind"]])
                    if u["kind"] == "A":
                        for s in range(LT):
                            last = mm(bank(1)[:, s * P:], vAh[:, s], pT2[:, 0, s, s * P:], s == 0, s == LT - 1)
                    elif u["kind"] == "B":
                        for t in range(LT):
                            for s in range(max(t - 1, 0), t + 1):
                                last = mm(bank(1)[g:g + 64, t * P:(t + 1) * P], vB[:, s, g:g + 64],
                                          pT2[:, 0, s, t * P:(t + 1) * P], s == max(t - 1, 0), s == t)
                    else:
                        for s in range(LT):
                            mm(bank(1)[g:g + 64, s * P:], vS[:, s, g:g + 64], pT2[:, 0, s, s * P:], s == 0, False)
                            mm(bank(1)[g:g + 64, s * P:], vW[:, s, g:g + 64], pT2[:, 1, s, s * P:], False, False)
                        last = mm(bank(1)[g:g + 64, :], vc[0:NB2, u["g"]], pTcmp[0:NB2], False, True)
                    last.then_inc(pv2, 1)

                for n in range(LEAD):
                    scores(n)
                for n in range(NS2):
                    if n + LEAD < NS2:
                        scores(n + LEAD)
                    ended = n > 0 and heads2[n - 1]["end"]
                    if ended:
                        values(n - 1)
                    turn(n)
                    if ended and heads2[n - 1]["kind"] == "A":
                        block_norm_mm(c0 + 4, ones)
                values(NS2 - 1)
            if phase_end("heads"):
                return
            for b in range(3):
                with pe.Fori(0, KT // 2) as i, tiles.loop(i, KT // 2, 4), uses.loop(i, KT // 2, 4):
                    for s in range(2):
                        turned_tile(hT, LAT)
                        turned_tile(y2[:, 4 * b:4 * b + 4], LAT, kt=4)
            if phase_end("branches2"):
                return
            with pe.Fori(0, 2) as i, tiles.loop(i, 2, 4), uses.loop(i, 2, 4):
                for _ in range(4):
                    turned_tile(acc, LAT)
            if phase_end("out2"):
                return
            mean_square(LAT)
            if phase_end("norm3"):
                return
            with pe.Fori(0, 8) as i, tiles.loop(i, 8, 4), uses.loop(i, 8, 4):
                for _ in range(4):
                    turned_tile(hT, LAT)
            if phase_end("up"):
                return
            with pe.Fori(0, 4) as i, tiles.loop(i, 4, 8), uses.loop(i, 4, 2):
                for _ in range(2):
                    pe.wait_ge(pair_free[uses.slot()], uses.earlier())
                    for f in range(4):
                        pe.wait_ge(w_landed[tiles.slot()], tiles.earlier() * 32 + 32)
                        for k in range(KT):
                            last = mm(bank(2 * uses.slot()), ring[:, tiles.slot(), k], U[:, f * KT + k],
                                      f == 0 and k == 0, f == 3 and k == KT - 1)
                        last.then_inc(w_used, 1)
                        tiles.next()
                    uses.next()
            if phase_end("down"):
                return
            for t in range(LT):
                if t >= 2:
                    pe.wait_ge(out_copied, t - 1)
                for f in range(KT):
                    last = nc.tensor.transpose(pair(uses.slot(), 1024)[:, f * P:(f + 1) * P], xT[:, f, t * P:(t + 1) * P], ident)
                last.then_inc(out_turned, 1)
                uses.next()
            phase_end("end")

        @block.scalar
        def _(act):
            tiles, uses = Turns(RING), Turns(2)
            own = Steps(act, act_own)
            ends, norms = [0], [0]

            def do(o, i, f, **kw):
                return nc.scalar.activation(o, i, f, **kw)

            def phase_end(name):
                act.drain().then_inc(phase, 1)
                ends[0] += 3
                act.wait_ge(phase, ends[0])
                return name == stop

            def product():
                act.wait_ge(w_used, tiles.number() + 1)
                return uses.slot()

            def release(ins):
                ins.then_inc(pair_free[uses.slot()], 1)
                skip()

            def skip(n=1):
                for _ in range(n):
                    tiles.next()
                    uses.next()

            def last_read():
                k = uses.k - 1
                act.wait_ge(pair_free[k % 2], k // 2 + 1 + uses.add)

            def inverse_root(dst, lnbuf, src, count, sem_read=None):
                ins = do(lnbuf, src, ACT.Ln, scale=1.0 / count, bias=eps)
                if sem_read is None:
                    own(ins)
                    own.settle()
                else:
                    ins.then_inc(sem_read[0], 1)
                    act.wait_ge(*sem_read)
                return do(dst, lnbuf, ACT.Exp, scale=-0.5)

            def squares(src, n):
                for f in range(KT):
                    c = norms[0] * KT + f
                    if f >= 2:
                        act.wait_ge(sq_used, c - 1)
                    do(sqb[:, f % 2, 0:n], src[:, f, 0:n], ACT.Square).then_inc(sq_ready, 1)
                norms[0] += 1
                act.wait_ge(sq_used, norms[0] * KT)
                inverse_root(rs[:, 0:n], lnb[:, 0:n], bank(4, n), D).then_inc(rs_ready, 1)

            for j in range(3):
                act.wait_ge(par_turned, j + 1)
                own(do((par + [par2])[j][:, 0:N_ROWS[j]], bank(4 + j, N_ROWS[j]), ACT.Copy))
            for f in range(KT):
                act.wait_ge(x_turned, f + 1)
                do(xT[:, f, :], pair(uses.slot()), ACT.Copy).then_inc(pair_free[uses.slot()], 1)
                uses.next()
            if phase_end("load"):
                return

            def branch(b, n):
                with act.Fori(0, KT // 2) as i, tiles.loop(i, KT // 2, 4), uses.loop(i, KT // 2, 4):
                    for s in range(2):
                        p = product()
                        last_read()
                        release(do(tha[:, 0:n], pair(p, n), ACT.Tanh, scale=0.5,
                                   bias=col(half_bg, i * 2 + (b * KT + s))))
                        skip()

            for l in range(DEPTH):
                n = ALL if l == 0 else LAT
                qu = QU[l]
                do(cond_t, par[l][:, R_C:R_C + 16], ACT.Tanh, scale=0.5).then_inc(cond_tanh, 1)
                for _ in range(24):
                    skip()
                if phase_end(f"ada{l}"):
                    return
                squares(xT, ALL)
                if phase_end(f"norm{l}"):
                    return
                with act.Fori(0, KT) as i, tiles.loop(i, KT, 4), uses.loop(i, KT, 4):
                    p = product()
                    last_read()
                    do(tha[:, 0:n], pair(p, n), ACT.Tanh, scale=0.5).then_inc(z_tanh, 1)
                    skip()
                    p = product()
                    release(do(bcopy[:, 0:n], pair(p, n), ACT.Copy))
                    skip(2)
                if phase_end(f"conv{l}"):
                    return
                branch(0, n)
                if phase_end(f"branch{l}0"):
                    return

                def square_tile(c, m):
                    p = product()
                    act.wait_ge(qms_done, c)
                    do(qsq[:, 0:m], pair(p, m), ACT.Square).then_inc(qsq_ready, 1)
                    skip()

                def root_tile(c, m):
                    act.wait_ge(qms_done, c + 1)
                    act.wait_ge(qn_ready, c)
                    inverse_root(qrs[:, 0:m], qln[:, 0:m], bank(4, m), HD, (qms_read, c + 1)).then_inc(qrs_ready, 1)

                nb = NORMED * l
                for c in range(2):
                    square_tile(nb + c, ALL)
                    root_tile(nb + c, ALL)
                for c in range(2):
                    p = product()
                    ins = do(vN[:, :, c * P:(c + 1) * P], pair(p).rearrange("p (t m) -> p t m", m=P), ACT.Copy)
                    release(ins)
                square_tile(nb + 2, n)
                root_tile(nb + 2, n)

                def step(off, i, last_head=False):
                    u0 = i * (2 * qu) + (U_BASE[l] + off * qu)
                    hn = i * 2 + (HEADS * l + off)
                    c = i * 2 + (nb + 3 + off)

                    def exp(t):
                        w = ALL if t < LT else CTX
                        act.wait_ge(max_done, u0 + t + 1)
                        if t >= 2:
                            act.wait_ge(turned, u0 + t - 1)
                        else:
                            act.wait_ge(pv_done, hn)
                        do(prob[:, t % 2, 0:w], bank(6, w), ACT.Exp, scale=HD ** -0.5, bias=stat[:, t % 2, 1:2],
                           accum_out=stat[:, t % 2, 2:3]).then_inc(exp_done, 1)

                    def copy(t):
                        act.wait_ge(turned, u0 + t + 1)
                        act.wait_ge(pv_done, hn)
                        if t < LT:
                            do(pT[:, :, t * P:(t + 1) * P], bank(4, ALL).rearrange("p (s q) -> p s q", q=P),
                               ACT.Copy).then_inc(pT_ready, 1)
                        else:
                            o = (t - LT) * P
                            do(pTc[:, :, o:o + P], bank(4, CTX).rearrange("p (s q) -> p s q", q=P),
                               ACT.Copy).then_inc(pT_ready, 1)

                    for t in range(qu):
                        exp(t)
                        if not last_head and t == SQUARE_AT[l]:
                            square_tile(c, n)
                        if not last_head and t == NORM_AT[l]:
                            root_tile(c, n)
                        copy(t)
                    p = product()
                    act.wait_ge(za_silu, hn)
                    do(zth[:, 0:n], pair(p, n), ACT.Tanh, scale=0.5).then_inc(za_tanh, 1)
                    skip()

                with act.Fori(0, HEADS // 2 - 1) as i, tiles.loop(i, HEADS // 2 - 1, 4), uses.loop(i, HEADS // 2 - 1, 4):
                    step(0, i)
                    step(1, i)
                step(0, 3)
                step(1, 3, True)
                if phase_end(f"attn{l}"):
                    return
                branch(1, n)
                if phase_end(f"branch{l}1"):
                    return
                p = product()
                do(gr[0:32, :], pair(p)[0:32, :], ACT.Copy).then_inc(pair_free[uses.slot()], 1)
                skip()
                units, nf = GU[l]
                def queries():
                    p = product()
                    release(do(gq[:, 0:n], pair(p, n), ACT.Copy, scale=DK ** -0.5))

                def head(i, last_head=False):
                    hh = i + GHEADS * l
                    u0 = hh * NU
                    p = product()
                    release(do(gk, pair(p), ACT.Copy))
                    act.wait_ge(dec_done, hh + 1)
                    act.wait_ge(gla_out, hh)
                    for d in range(2):
                        own(do(gtmp[:, d], bank(4 + 2 * d, ALL), ACT.Abs))
                        own.settle()
                        own(do(gtmp[:, d], gtmp[:, d], ACT.Exp, scale=-1.0))
                        own.settle()
                        do(gtmp[:, d], gtmp[:, d], ACT.Ln, bias=one).then_inc(dec_ln, 1)
                    for v in range(2):
                        p = product()
                        release(do(gv[:, :, v * P:(v + 1) * P], pair(p).rearrange("p (t m) -> p t m", m=P), ACT.Copy))

                    def exponentials(j):
                        act.wait_ge(sum_done, u0 + j + 1)
                        act.wait_ge(qk_ready, u0 + j)
                        if units[j][2]:
                            ins = do(gE, bank(0, 1536).rearrange("p (c m) -> p c m", c=3)[:, :, 0:384], ACT.Exp)
                        else:
                            ins = do(gE[:, 0:9:8], bank(0, 1024).rearrange("p (c m) -> p c m", c=2)[:, :, 0:P], ACT.Exp)
                        ins.then_inc(e_ready, 1)

                    exponentials(0)
                    for j in range(NU):
                        if j + 1 < NU:
                            exponentials(j + 1)
                        act.wait_ge(k_turned, u0 + j + 1)
                        act.wait_ge(s_done, u0 + max(j - 1, 0))
                        do(gkN[:, j % 2], bank(6, P), ACT.Copy).then_inc(kN_ready, 1)
                    act.wait_ge(s_done, u0 + NU)
                    act.wait_ge(o_read, (i + 1) * nf + F_BASE[l])
                    yh = y[:, 2 * i:2 * i + 2, 0:n] if isinstance(i, int) else y[:, ds(i * 2, 2), 0:n]
                    do(gsq[:, :, 0:n], yh, ACT.Square).then_inc(gsq_ready, 1)
                    if not last_head:
                        queries()
                    act.wait_ge(gms_done, hh + 1)
                    inverse_root(gtmp[:, 0, 0:n], gtmp[:, 1, 0:n], bank(4, n), DV, (grs_ready, hh * 2 + 1))\
                        .then_inc(grs_ready, 1)

                queries()
                with act.Fori(0, GHEADS - 1) as i, tiles.loop(i, GHEADS - 1, 4), uses.loop(i, GHEADS - 1, 4), \
                        own.loop(i, GHEADS - 1, 4):
                    head(i)
                head(GHEADS - 1, True)
                if phase_end(f"gla{l}"):
                    return
                with act.Fori(0, 2) as i, tiles.loop(i, 2, 4), uses.loop(i, 2, 4):
                    for s in range(4):
                        p = product()
                        last_read()
                        do(tha[:, 0:n], pair(p, n), ACT.Tanh, scale=0.5).then_inc(z_tanh, 1)
                        skip()
                if phase_end(f"glaz{l}"):
                    return
                branch(2, n)
                if phase_end(f"branch{l}2"):
                    return
                with act.Fori(0, 2) as i, tiles.loop(i, 2, 4), uses.loop(i, 2, 4):
                    for s in range(4):
                        p = product()
                        release(do(row(y, i * 4 + s, 0, n), pair(p, n), ACT.Copy))
                if phase_end(f"out{l}"):
                    return
                squares(y, n)
                if phase_end(f"post{l}"):
                    return
            squares(xT, LAT)
            act.wait_ge(rows_mm, 1)
            for w_ in range(2):
                do(brow[0:20, w_, 0:TOE], pair(w_)[0:20, 0:TOE], ACT.Copy).then_inc(rows_done, 1)
            act.wait_ge(lam_sum, 2)
            own(do(lam[:, 2:4], lam[:, 0:2], ACT.Exp))
            if phase_end("norm2"):
                return

            def square2(c, src, n=LAT):
                act.wait_ge(ms2_done, c)
                do(n2sq[:, 0:n], src, ACT.Square).then_inc(sq2_ready, 1)

            def root2(c, count, n=LAT):
                act.wait_ge(ms2_done, c + 1)
                act.wait_ge(n2_ready, c)
                inverse_root(n2rs[:, 0:n], n2ln[:, 0:n], bank(3, n), count).then_inc(rs2_ready, 1)

            def tokens_out(dst):
                p = product()
                release(do(dst, bank(2 * p).rearrange("p (t m) -> p t m", m=P), ACT.Copy))

            def keep(c, src):
                act.wait_ge(n2_ready, c)
                return do(n2raw, src, ACT.Copy)

            def normed2(c):
                p = product()
                square2(c, bank(2 * p))
                release(keep(c, bank(2 * p)))
                root2(c, 64)

            for c in range(4):
                tokens_out(vA[:, :, c * P:(c + 1) * P])
            normed2(0)
            tokens_out(vB)
            for kv in range(2):
                p = product()
                release(do(tk[:, kv], bank(2 * p), ACT.Copy))
            normed2(1)
            tokens_out(vS)
            normed2(2)
            tokens_out(vW)
            p = product()
            release(do(gates, bank(2 * p, 96).rearrange("p (t m) -> p t m", m=24), ACT.Tanh, scale=0.5))
            for kv in range(2):
                act.wait_ge(tab2_turned, kv + 1)
                own(do(pos[:, kv], bank(6 + kv, 32), ACT.Copy))
            if phase_end("kv2"):
                return
            for kv in range(2):
                act.wait_ge(hid_done, kv + 1)
                for g in range(2):
                    do(hx[:, 2 * kv, 0:124].rearrange("p (m g c) -> p m g c", m=2, g=2)[:, :, g],
                       bank(6 - 2 * kv + g, 62).rearrange("p (m c) -> p m c", m=2), ACT.Copy).then_inc(hx_ready, 1)
                act.wait_ge(gelu_arg, kv + 1)
                do(hx[:, 2 * kv + 1, 0:124], hx[:, 2 * kv + 1, 0:124], ACT.Tanh, scale=GELU).then_inc(gelu_tanh, 1)
            act.wait_ge(hid_done, 3)
            square2(3, bank(0, 2 * NB2), 2 * NB2)
            root2(3, 64, 2 * NB2)
            act.wait_ge(hid_done, 4)
            own(do(vc[0:NB2], bank(2)[0:NB2, 0:128].rearrange("p (g d) -> p g d", g=2), ACT.Copy))
            if phase_end("cmp"):
                return
            with act.Fori(0, 4) as i, tiles.loop(i, 4, 4), uses.loop(i, 4, 4), own.loop(i, 4, 2 * LT + 5):
                c0 = i * 5 + NORM0
                s0, t0 = i * NS2, i * turns2
                for c in range(4):
                    normed2(c0 + c)

                def exp(n):
                    u = heads2[n]
                    st = stat2[:, n % 4]
                    act.wait_ge(max2, s0 + n + 1)
                    before = [x["turn"] for x in heads2[:max(n - 2, 0)] if x["turn"] is not None] if n >= 4 else []
                    if n >= 4 and heads2[n - 4]["turn"] is not None and heads2[n - 3]["turn"] is not None:
                        before = before[:-1]
                    act.wait_ge(turned2, t0 + (before[-1] + 1) if before else i * turns2)
                    if u["kind"] == "B":
                        own(do(st[:, 4:5], st[:, 6:7], ACT.Exp))
                    do(prob2[:, n % 4, 0:u["w"]], score_bank(n, u["w"]), ACT.Exp, bias=st[:, 1:2],
                       accum_out=st[:, 2:3]).then_inc(exp2, 1)

                heads_done = [0]

                def copy(n):
                    u = heads2[n]
                    tn = u["turn"]
                    if tn is None:
                        return
                    act.wait_ge(turned2, t0 + tn + 1)
                    act.wait_ge(pv2, i * 5 + heads_done[0])
                    q0 = u["qt"] * P
                    if u["sub"] == "cmp":
                        ins = do(pTcmp[0:NB2, q0:q0 + P], bank(4 + tn % 2)[0:NB2, 0:P], ACT.Copy)
                    else:
                        k0, k1 = u["lo"] // P, u["lo"] // P + u["w"] // P
                        ins = do(pT2[:, int(u["sub"] == "win"), k0:k1, q0:q0 + P],
                                 bank(4 + tn % 2, u["w"]).rearrange("p (s q) -> p s q", q=P), ACT.Copy)
                    ins.then_inc(pT2_ready, 1)

                exp(0)
                for n in range(NS2):
                    if n + 1 < NS2:
                        exp(n + 1)
                    copy(n)
                    if n and heads2[n - 1]["end"] and heads2[n - 1]["kind"] == "A":
                        root2(c0 + 4, P)
                    if heads2[n]["end"]:
                        heads_done[0] += 1
                        if heads2[n]["kind"] == "A":
                            act.wait_ge(pv2, i * 5 + 1)
                            square2(c0 + 4, bank(1))
                            keep(c0 + 4, bank(1)).then_inc(o2_read, 1)
            if phase_end("heads"):
                return
            for b in range(3):
                with act.Fori(0, KT // 2) as i, tiles.loop(i, KT // 2, 4), uses.loop(i, KT // 2, 4):
                    for s in range(2):
                        p = product()
                        last_read()
                        release(do(tha2, bank(2 * p), ACT.Tanh, scale=0.5))
                        skip()
            if phase_end("branches2"):
                return
            skip(8)
            if phase_end("out2"):
                return
            squares(xT, LAT)
            if phase_end("norm3"):
                return
            with act.Fori(0, 8) as i, tiles.loop(i, 8, 4), uses.loop(i, 8, 4):
                for _ in range(4):
                    p = product()
                    last_read()
                    do(rl, bank(2 * p), ACT.Relu).then_inc(relu_ready, 1)
                    skip()
            if phase_end("up"):
                return
            for _ in range(8):
                uses.next()
            if phase_end("down"):
                return
            for t in range(LT):
                act.wait_ge(out_turned, t + 1)
                do(ob[:, t], pair(uses.slot(), 1024), ACT.Copy).then_inc(out_copied, 1)
                uses.next()
            phase_end("end")

        @block.vector
        def _(dve):
            tiles, uses = Turns(RING), Turns(2)
            own = Steps(dve, dve_own)
            ends, norms = [0], [0]
            v = nc.vector

            def phase_end(name):
                dve.drain().then_inc(phase, 1)
                ends[0] += 3
                dve.wait_ge(phase, ends[0])
                return name == stop

            def stt(o, a0, s, a1, op0, op1):
                return v.scalar_tensor_tensor(out=o, in0=a0, scalar=s, in1=a1, op0=op0, op1=op1)

            def product():
                dve.wait_ge(w_used, tiles.number() + 1)
                return uses.slot()

            def release(ins):
                ins.then_inc(pair_free[uses.slot()], 1)
                skip()

            def skip(n=1):
                for _ in range(n):
                    tiles.next()
                    uses.next()

            def all_read():
                for s in range(2):
                    dve.wait_ge(pair_free[s], uses.uses_of(s))

            def last_read():
                k = uses.k - 1
                dve.wait_ge(pair_free[k % 2], k // 2 + 1 + uses.add)

            own(v.memset(consts, EPS))
            own(v.memset(onec, 1.0))
            for _ in range(KT):
                uses.next()
            if phase_end("load"):
                return

            def branch(b, n):
                with dve.Fori(0, KT // 2) as i, tiles.loop(i, KT // 2, 4), uses.loop(i, KT // 2, 4), \
                        own.loop(i, KT // 2, 2):
                    for s in range(2):
                        skip()
                        p = product()
                        last_read()
                        own.settle()
                        release(stt(tmp[:, 0:n], tha[:, 0:n], 1.0, pair(p, n), ALU.add, ALU.mult))
                        last_read()
                        dst = row(acc, i * 2 + s, 0, n)
                        if b == 0:
                            own(v.tensor_scalar(dst, tmp[:, 0:n], 0.5, None, ALU.mult))
                        else:
                            own(stt(dst, tmp[:, 0:n], 0.5, dst, ALU.mult, ALU.add))

            for l in range(DEPTH):
                n = ALL if l == 0 else LAT
                qu = QU[l]
                dve.wait_ge(cond_tanh, l + 1)
                pc = par[l][:, R_C:R_C + 16]
                own(stt(cond_s, cond_t, 1.0, pc, ALU.add, ALU.mult))
                own.settle()
                v.tensor_scalar(cond.rearrange("p a b -> p (a b)"), cond_s, 0.5, None, ALU.mult).then_inc(cond_ready, 1)
                with dve.Fori(0, 6) as i, tiles.loop(i, 6, 4), uses.loop(i, 6, 4):
                    for s in range(4):
                        p = product()
                        release(v.tensor_copy(row(modl, i * 4 + s), pair(p, 2)))
                all_read()

                def over(o, w):
                    return par[l][:, o:o + w].unsqueeze(2).to_broadcast([P, w, 2])

                own(v.tensor_tensor(modl[:], modl[:], over(R_BADA, 24), ALU.add))
                own.settle()
                own(stt(scale1[:], modl[:, 8:16], 1.0, over(R_GPRE, 8), ALU.add, ALU.mult))
                own(v.tensor_tensor(gpost[:], modl[:, 16:24], over(R_GPOST, 8), ALU.mult))
                own(v.tensor_scalar(half_bg[:], par[l][:, R_BG:R_BG + 24], 0.5, None, ALU.mult))
                own.settle()
                if phase_end(f"ada{l}"):
                    return
                norms[0] += 1
                dve.wait_ge(rs_ready, norms[0])
                for f in range(KT):
                    own(v.tensor_tensor(hT[:, f], xT[:, f], rs, ALU.mult))
                    own.settle()
                    for k, (lo, hi) in enumerate(spans(ALL)):
                        own(v.tensor_scalar(hT[:, f, lo:hi], hT[:, f, lo:hi], scale1[:, f, k:k + 1],
                                            modl[:, f, k:k + 1], ALU.mult, ALU.add))
                if phase_end(f"norm{l}"):
                    return
                edges = (0, LAT + 1, LAT + 2, LAT + 2 + CTX + 1)
                for e in edges:
                    own(v.memset(conv_u[:, e:e + 1], 0.0))
                stretches = [(0, 0, LAT)] + ([(LAT + 2, LAT, CTX)] if n == ALL else [])
                ns = len(stretches)
                with dve.Fori(0, KT) as i, tiles.loop(i, KT, 4), uses.loop(i, KT, 4), own.loop(i, KT, 4 * ns):
                    p = product()
                    dve.wait_ge(z_tanh, i + 16 * l + 1)
                    last_read()
                    release(stt(tmp[:, 0:n], tha[:, 0:n], 1.0, pair(p, n), ALU.add, ALU.mult))
                    last_read()
                    skip()
                    p = product()
                    last_read()
                    for at, o, w in stretches:
                        ins = v.tensor_tensor(conv_u[:, at + 1:at + 1 + w], bcopy[:, o:o + w], pair(p)[:, o:o + w], ALU.mult)
                        own(ins)
                    own.settle()
                    for at, o, w in stretches:
                        t = conv_t[:, o:o + w]
                        own(v.tensor_scalar(t, conv_u[:, at:at + w], col(par[l], i + R_CONV), None, ALU.mult))
                        own.settle()
                        for k in (1, 2):
                            own(stt(t, conv_u[:, at + k:at + k + w], col(par[l], i + (R_CONV + 8 * k)), t, ALU.mult, ALU.add))
                            own.settle()
                    release(stt(tmp[:, 0:n], tmp[:, 0:n], 0.5, conv_t[:, 0:n], ALU.mult, ALU.mult))
                    p = product()
                    last_read()
                    release(v.tensor_tensor(row(y, i, 0, n), tmp[:, 0:n], pair(p, n), ALU.mult))
                if phase_end(f"conv{l}"):
                    return
                branch(0, n)
                if phase_end(f"branch{l}0"):
                    return

                def norm_tile(c, dst, g, m):
                    s = uses.slot()
                    dve.wait_ge(qrs_ready, c + 1)
                    stt(dst[:, 0:m], pair(s, m), g, qrs[:, 0:m], ALU.mult, ALU.mult).then_inc(pair_free[s], 1)
                    skip()
                    last_read()
                    v.tensor_tensor(rope_t, dst[:, 0:LAT], cos, ALU.mult).then_inc(qn_ready, 1)

                def rotate_tile(c, dst):
                    dve.wait_ge(rot_done, c + 1)
                    v.tensor_tensor(rope_s, bank(4), sin, ALU.mult).then_inc(rot_read, 1)
                    dve.wait_ge(rot_read, c + 1)
                    dve.wait_ge(qn_ready, c + 1)
                    v.tensor_tensor(dst[:, 0:LAT], rope_t, rope_s, ALU.add).then_inc(q_ready, 1)

                nb = NORMED * l
                qg, kg = par[l][:, R_QG:R_QG + 1], par[l][:, R_KG:R_KG + 1]
                for c in range(2):
                    norm_tile(nb + c, kT[:, c], kg, ALL)
                    rotate_tile(nb + c, kT[:, c])
                skip(2)
                norm_tile(nb + 2, qT[:, 0], qg, n)
                rotate_tile(nb + 2, qT[:, 0])

                def step(off, i, last_head=False):
                    u0 = i * (2 * qu) + (U_BASE[l] + off * qu)
                    hn = i * 2 + (HEADS * l + off)
                    c = i * 2 + (nb + 3 + off)
                    nq = qT[:, (off + 1) % 2]

                    def maximum(t):
                        w = ALL if t < LT else CTX
                        st = stat[:, t % 2]
                        dve.wait_ge(scores_done, u0 + t + 1)
                        own(v.reduce_max(st[:, 0:1], bank(6, w), AX.X))
                        own.settle()
                        v.tensor_scalar(st[:, 1:2], st[:, 0:1], -HD ** -0.5, None, ALU.mult).then_inc(max_done, 1)

                    def normalise(t):
                        w = ALL if t < LT else CTX
                        st = stat[:, t % 2]
                        dve.wait_ge(exp_done, u0 + t + 1)
                        own(v.reciprocal(st[:, 3:4], st[:, 2:3]))
                        own.settle()
                        pr = prob[:, t % 2, 0:w]
                        v.tensor_scalar(pr, pr, st[:, 3:4], None, ALU.mult).then_inc(prob_done, 1)

                    for t in range(qu):
                        maximum(t)
                        if not last_head and t == NORM_AT[l] + 1:
                            rotate_tile(c, nq)
                        normalise(t)
                        if not last_head and t == NORM_AT[l]:
                            norm_tile(c, nq, qg, n)
                    p = product()
                    dve.wait_ge(za_tanh, hn + 1)
                    dve.wait_ge(head_out, hn)
                    stt(zsi[:, 0:n], zth[:, 0:n], 1.0, pair(p, n), ALU.add, ALU.mult).then_inc(pair_free[p], 1)
                    skip()
                    last_read()
                    v.memset(stat[:, 3, 6:7], 0.0).then_inc(za_silu, 1)
                    dve.wait_ge(pv_done, hn + 1)
                    h = i * 2 + off
                    stt(row(y, h, 0, n), bank(4, n), 0.5, zsi[:, 0:n], ALU.mult, ALU.mult).then_inc(head_out, 1)

                with dve.Fori(0, HEADS // 2 - 1) as i, tiles.loop(i, HEADS // 2 - 1, 4), \
                        uses.loop(i, HEADS // 2 - 1, 4), own.loop(i, HEADS // 2 - 1, 4 * qu):
                    step(0, i)
                    step(1, i)
                step(0, 3)
                step(1, 3, True)
                if phase_end(f"attn{l}"):
                    return
                branch(1, n)
                if phase_end(f"branch{l}1"):
                    return

                own(v.memset(gwd[0:33], 0.0))
                own.settle()
                v.memset(gr[32:33], 1.0).then_inc(wd_zero, 1)
                skip()
                units, nf = GU[l]
                skip()

                def head(i):
                    hh = i + GHEADS * l
                    u0 = hh * NU
                    f0 = i * nf + F_BASE[l]
                    skip(4)
                    for d in range(2):
                        dve.wait_ge(dec_ln, hh * 2 + d + 1)
                        stt(gla[:, d].rearrange("p t m -> p (t m)"), bank(4 + 2 * d, ALL), 0.0, gtmp[:, d], ALU.min,
                            ALU.subtract).then_inc(la_ready, 1)
                    own(v.memset(gS, 0.0))
                    for s in range(2):
                        k = uses.k - 2 - s
                        dve.wait_ge(pair_free[k % 2], k // 2 + 1 + uses.add)

                    def decayed(j):
                        d, t, full = units[j][:3]
                        q_, k_ = (x[:, t * P:(t + 1) * P].unsqueeze(1).to_broadcast([P, 8, P]) for x in (gq, gk))
                        dve.wait_ge(e_ready, u0 + j + 1)
                        dve.wait_ge(s_done, u0 + max(j - 2, 0))
                        dve.wait_ge(s_ready, u0 + max(j - 2, 0))
                        e = 0 if d else P - 1
                        own(v.tensor_copy(gdec[:, j % 3:j % 3 + 1], gE[:, 0, e:e + 1]))
                        if full:
                            own(v.tensor_tensor(gqE[:, j % 3].rearrange("p (l t) -> p l t", l=8), gE[:, 0:8], q_, ALU.mult))
                            ins = v.tensor_tensor(gkE[:, j % 2].rearrange("p (l t) -> p l t", l=8), gE[:, 1:9], k_, ALU.mult)
                        else:
                            ins = v.tensor_tensor(gkE[:, j % 2, 7 * P:8 * P], gE[:, 8], gk[:, t * P:(t + 1) * P], ALU.mult)
                        ins.then_inc(qk_ready, 1)

                    def mask(j):
                        d, t, full, seen, f = units[j]
                        if not full:
                            return
                        dve.wait_ge(att_done, f0 + f + 1)
                        dve.wait_ge(att_ready, f0 + f)
                        v.tensor_tensor(gam, bank(3, 1024).rearrange("p (l t) -> p l t", l=8), pairs[:, d],
                                        ALU.mult).then_inc(masked, 1)
                        dve.wait_ge(masked, f0 + f + 1)
                        dve.wait_ge(o_done, f0 + max(f - 1, 0))
                        v.tensor_reduce(gatt[:, f % 2], gam.rearrange("p l t -> p t l"), AX.X, ALU.add).then_inc(att_ready, 1)

                    def keep(j):
                        d, t, full, seen, f = units[j]
                        if full:
                            dve.wait_ge(o_done, f0 + f + 1)
                            ts_ = slice(t * P, (t + 1) * P)
                            dst = y[:, 2 * i:2 * i + 2, ts_] if isinstance(i, int) else y[:, ds(i * 2, 2), ts_]
                            o_ = bank(5, DV).rearrange("p (a t) -> p a t", a=2)
                            if seen:
                                dve.wait_ge(o_read, f0 + f)
                                v.tensor_tensor(dst, dst, o_, ALU.add).then_inc(o_read, 1)
                            else:
                                v.tensor_copy(dst, o_).then_inc(o_read, 1)
                        dve.wait_ge(s_done, u0 + j + 1)
                        own.settle()
                        dve.wait_ge(s_ready, u0 + j)
                        stt(gS[:, d], gS[:, d], gdec[:, j % 3:j % 3 + 1], bank(7, DV), ALU.mult, ALU.add).then_inc(s_ready, 1)

                    decayed(0)
                    for j in range(NU):
                        if j + 1 < NU:
                            decayed(j + 1)
                        mask(j)
                        if j:
                            keep(j - 1)
                    keep(NU - 1)
                    dve.wait_ge(grs_ready, hh * 2 + 2)
                    for a_ in range(2):
                        dst = row(y, 2 * i + a_, 0, n)
                        ins = stt(dst, dst, par[l][:, R_GLAG + a_:R_GLAG + a_ + 1], gtmp[:, 0, 0:n], ALU.mult, ALU.mult)
                        if a_ == 0:
                            own(ins)
                        else:
                            ins.then_inc(gla_out, 1)

                with dve.Fori(0, GHEADS - 1) as i, tiles.loop(i, GHEADS - 1, 4), uses.loop(i, GHEADS - 1, 4), \
                        own.loop(i, GHEADS - 1, 1 + NU + nf + 1):
                    head(i)
                head(GHEADS - 1)
                tiles.k -= 1
                uses.k -= 1
                if phase_end(f"gla{l}"):
                    return
                with dve.Fori(0, 2) as i, tiles.loop(i, 2, 4), uses.loop(i, 2, 4), own.loop(i, 2, 4):
                    for s in range(4):
                        p = product()
                        dve.wait_ge(z_tanh, i * 4 + (16 * l + 8 + s + 1))
                        own.settle()
                        release(stt(tmp[:, 0:n], tha[:, 0:n], 1.0, pair(p, n), ALU.add, ALU.mult))
                        last_read()
                        dst = row(y, i * 4 + s, 0, n)
                        own(stt(dst, tmp[:, 0:n], 0.5, dst, ALU.mult, ALU.mult))
                if phase_end(f"glaz{l}"):
                    return
                branch(2, n)
                if phase_end(f"branch{l}2"):
                    return
                skip(8)
                if phase_end(f"out{l}"):
                    return
                norms[0] += 1
                dve.wait_ge(rs_ready, norms[0])
                for f in range(KT):
                    own(v.tensor_tensor(y[:, f, 0:n], y[:, f, 0:n], rs[:, 0:n], ALU.mult))
                    own.settle()
                    for k, (lo, hi) in enumerate(spans(n)):
                        own(stt(xT[:, f, lo:hi], y[:, f, lo:hi], gpost[:, f, k:k + 1], xT[:, f, lo:hi], ALU.mult, ALU.add))
                if phase_end(f"post{l}"):
                    return
            def normed_h(g0):
                norms[0] += 1
                dve.wait_ge(rs_ready, norms[0])
                for f in range(KT):
                    own(stt(hT[:, f, 0:LAT], xT[:, f, 0:LAT], par2[:, g0 + f:g0 + f + 1], rs[:, 0:LAT], ALU.mult, ALU.mult))

            v.memset(relb[BUCKETS:BUCKETS + 1], NEG).then_inc(relb_ready, 1)
            for g in (0, 2, 4):
                gcol = par2[:, S_GAIN + g:S_GAIN + g + 1]
                own(v.tensor_scalar(gcol, gcol, 0.125, None, ALU.mult))
            scol = par2[:, S_SUB:S_SUB + 1]
            own(v.tensor_scalar(scol, scol, 1.0 - LAM0, None, ALU.mult))
            dve.wait_ge(in2, 64)
            for k in range(2):
                own(v.tensor_tensor(lamp, lamb[:, 128 * k:128 * k + 64], lamb[:, 128 * k + 64:128 * k + 128], ALU.mult))
                own.settle()
                v.tensor_reduce(lam[:, k:k + 1], lamp, AX.X, ALU.add).then_inc(lam_sum, 1)
                dve.wait_ge(lam_sum, k + 1)
            normed_h(S_MIX)
            if phase_end("norm2"):
                return

            def normed_tile(c, dst, gain):
                dve.wait_ge(rs2_ready, c + 1)
                stt(dst, n2raw, gain, n2rs, ALU.mult, ALU.mult).then_inc(n2_ready, 1)

            def gain(g):
                return par2[:, S_GAIN + g:S_GAIN + g + 1]

            own(v.tensor_tensor(lam[:, 0:1], lam[:, 3:4], lam[:, 2:3], ALU.subtract))
            own.settle()
            own(v.tensor_scalar(lam[:, 0:1], lam[:, 0:1], -LAM0, None, ALU.add))
            skip(13)
            for c, (dst, g) in enumerate(((kB, 3), (kS, 6), (kW, 7))):
                normed_tile(c, dst, gain(g))
            all_read()
            own(v.tensor_scalar(gates, gates, 0.5, 0.5, ALU.mult, ALU.add))
            if phase_end("kv2"):
                return
            for kv in range(2):
                src = tk[:, kv]
                win = bass.AP(src.tensor, src.offset, [list(src.ap[0]), [16, NB2], [1, 32]])
                if kv:
                    dve.wait_ge(hid_done, 1)
                v.tensor_tensor(tpos, win, pos[:, kv].unsqueeze(1).to_broadcast([P, NB2, 32]), ALU.add).then_inc(hid_ready, 1)
            for kv in range(2):
                x_, u_ = hx[:, 2 * kv, 0:124], hx[:, 2 * kv + 1, 0:124]
                dve.wait_ge(hid_done, kv + 1)
                dve.wait_ge(hx_ready, 2 * kv + 2)
                own(v.tensor_tensor(u_, x_, x_, ALU.mult))
                own.settle()
                own(v.tensor_scalar(u_, u_, 0.044715, 1.0, ALU.mult, ALU.add))
                own.settle()
                v.tensor_tensor(u_, u_, x_, ALU.mult).then_inc(gelu_arg, 1)
                dve.wait_ge(gelu_tanh, kv + 1)
                own(stt(u_, u_, 1.0, x_, ALU.add, ALU.mult))
                own.settle()
                v.tensor_scalar(hid[:, kv, 0:124], u_, 0.5, None, ALU.mult).then_inc(hid_ready, 1)
            dve.wait_ge(rs2_ready, 4)
            stt(kc[:, 0:62], bank(0, 62), par2[:, S_GAIN + 5:S_GAIN + 6], n2rs[:, 0:62], ALU.mult, ALU.mult).then_inc(n2_ready, 1)
            if phase_end("cmp"):
                return
            own2 = sum(1 + {"c0": 2, "c1": 2, "b": 3, "sel": 1, "win": 1, "cmp": 2}[u["sub"]] for u in heads2)
            with dve.Fori(0, 4) as i, tiles.loop(i, 4, 4), uses.loop(i, 4, 4), \
                    own.loop(i, 4, own2 + 1):
                c0 = i * 5 + NORM0
                s0, t0 = i * NS2, i * turns2
                dve.wait_ge(pv2, i * 5)
                own(v.tensor_scalar(vAh, vA[:, :, ds(i * P, P)], 1.0, None, ALU.mult))
                for c, g in enumerate((0, 1, 2, 4)):
                    normed_tile(c0 + c, qt_[:, c], gain(g))
                skip(4)

                def maximum(n):
                    u = heads2[n]
                    st = stat2[:, n % 4]
                    dve.wait_ge(scores2, s0 + n + 1)
                    own.settle()
                    own(v.reduce_max(st[:, 0:1], score_bank(n, u["w"]), AX.X))
                    own.settle()
                    if u["kind"] == "B":
                        sink = sinkb[:, ds(i + 4 * u["g"], 1)]
                        own(v.tensor_scalar(st[:, 1:2], st[:, 0:1], sink, -1.0, ALU.max, ALU.mult))
                        own.settle()
                        ins = v.tensor_scalar(st[:, 6:7], st[:, 1:2], sink, None, ALU.add)
                    else:
                        ins = v.tensor_scalar(st[:, 1:2], st[:, 0:1], -1.0, None, ALU.mult)
                    ins.then_inc(max2, 1)

                def normalise(n):
                    u = heads2[n]
                    st = stat2[:, n % 4]
                    pr = prob2[:, n % 4, 0:u["w"]]
                    dve.wait_ge(exp2, s0 + n + 1)
                    if u["kind"] == "B":
                        own(v.tensor_tensor(st[:, 2:3], st[:, 2:3], st[:, 4:5], ALU.add))
                        own.settle()
                    own(v.reciprocal(st[:, 3:4], st[:, 2:3]))
                    own.settle()
                    if u["sub"] == "c0":
                        own(v.tensor_scalar(pr, pr, st[:, 3:4], None, ALU.mult))
                        return
                    if u["sub"] == "c1":
                        own(v.tensor_tensor(st[:, 5:6], st[:, 3:4], lam[:, 0:1], ALU.mult))
                        own.settle()
                        p0 = prob2[:, (n - 1) % 4, 0:u["w"]]
                        ins = stt(p0, pr, st[:, 5:6], p0, ALU.mult, ALU.add)
                    elif u["kind"] == "B":
                        ins = v.tensor_scalar(pr, pr, st[:, 3:4], None, ALU.mult)
                    else:
                        k = {"cmp": 0, "sel": 1, "win": 2}[u["sub"]]
                        gate = gates[:, u["qt"], ds(i * 3 + 12 * u["g"] + k, 1)]
                        if u["sub"] == "cmp":
                            own(v.tensor_tensor(st[:, 5:6], st[:, 3:4], gate, ALU.mult))
                            own.settle()
                            ins = stt(pr, pr, st[:, 5:6], cmask[:, 0, u["qt"], 0:NB2], ALU.mult, ALU.mult)
                        else:
                            ins = v.tensor_scalar(pr, pr, st[:, 3:4], gate, ALU.mult, ALU.mult)
                    ins.then_inc(prob2_ready, 1)

                def outputs(n):
                    u = heads2[n]
                    if u["kind"] == "A":
                        normed_tile(c0 + 4, row(y2, i), scol)
                    elif u["g"] == 1:
                        nh = sum(x["end"] for x in heads2[:n + 1])
                        dve.wait_ge(pv2, i * 5 + nh)
                        v.tensor_copy(row(y2, i + (4 if u["kind"] == "B" else 8)), bank(1)).then_inc(o2_read, 1)

                maximum(0)
                for n in range(NS2):
                    if n + 1 < NS2:
                        maximum(n + 1)
                    normalise(n)
                    if n >= 2 and heads2[n - 2]["end"]:
                        outputs(n - 2)
                outputs(NS2 - 1)
            if phase_end("heads"):
                return
            for b in range(3):
                with dve.Fori(0, KT // 2) as i, tiles.loop(i, KT // 2, 4), uses.loop(i, KT // 2, 4), \
                        own.loop(i, KT // 2, 2):
                    for s in range(2):
                        skip()
                        p = product()
                        last_read()
                        own.settle()
                        release(stt(tmp2, tha2, 1.0, bank(2 * p), ALU.add, ALU.mult))
                        last_read()
                        dst = row(acc, i * 2 + s, 0, LAT)
                        if b == 0:
                            own(v.tensor_scalar(dst, tmp2, 0.5, None, ALU.mult))
                        else:
                            own(stt(dst, tmp2, 0.5, dst, ALU.mult, ALU.add))
            if phase_end("branches2"):
                return

            def residual():
                p = uses.slot()
                dst = row(xT, add_at[0], 0, LAT)
                return v.tensor_tensor(dst, dst, bank(2 * p), ALU.add)

            add_at = [0]
            with dve.Fori(0, 2) as i, tiles.loop(i, 2, 4), uses.loop(i, 2, 4):
                for s in range(4):
                    product()
                    add_at[0] = i * 4 + s
                    release(residual())
            if phase_end("out2"):
                return
            normed_h(S_MLP)
            if phase_end("norm3"):
                return
            with dve.Fori(0, 8) as i, tiles.loop(i, 8, 4), uses.loop(i, 8, 4):
                for s in range(4):
                    p = product()
                    dve.wait_ge(relu_ready, i * 4 + s + 1)
                    release(v.tensor_tensor(row(U, i * 4 + s), rl, bank(2 * p), ALU.mult))
            if phase_end("up"):
                return
            with dve.Fori(0, 4) as i, tiles.loop(i, 4, 8), uses.loop(i, 4, 2):
                for s in range(2):
                    for _ in range(3):
                        tiles.next()
                    dve.wait_ge(w_used, tiles.number() + 1)
                    add_at[0] = i * 2 + s
                    release(residual())
            if phase_end("down"):
                return
            phase_end("end")



_OUTS = [((1, 512, 1024), "float32")]


def kernel(**inputs):
    import numpy as _np
    import concourse.bacc as _bacc
    from concourse import mybir as _mybir
    from concourse.bass_utils import run_bass_kernel_spmd as _run

    nc = _bacc.Bacc("TRN2", target_bir_lowering=False, num_devices=1)
    arrays, args = {}, {}
    given = dict(inputs, con=constants(), con2=constants2())
    for name, value in given.items():
        v = _np.ascontiguousarray(value)
        arrays[f"in_{name}"] = v
        args[name] = nc.dram_tensor(f"in_{name}", v.shape, _mybir.dt.from_np(v.dtype), kind="ExternalInput").ap()
    shape, dtype = _OUTS[0]
    out = nc.dram_tensor("out_0", shape, _mybir.dt.from_np(_np.dtype(dtype)), kind="ExternalOutput").ap()
    two_blocks(nc, args, out)
    r = _run(nc, [arrays], core_ids=[0])
    return r.results[0]["out_0"]
```

```python
from contextlib import ExitStack, contextmanager

import numpy as np

import concourse.bass as bass
from concourse import mybir

F32 = mybir.dt.float32
F32R = mybir.dt.float32r
ACT = mybir.ActivationFunctionType
ALU = mybir.AluOpType
AX = mybir.AxisListType
ds = bass.ds

P = 128
D = 1024
KT = D // P
LAT, CTX = 512, 256
ALL = LAT + CTX
LT, CT = LAT // P, CTX // P
NT = LT + CT
DEPTH = 2
HEADS, HD = 8, 128
GHEADS, DK, DV = 4, 128, 256
RANK = 16
TAU = 16.0
EPS = 1e-6
LEVELS = 7
NEG = -1e30

CB, CC, CX, CZ = 0, 1024, 2048, 3072
CQ = 4096
CK = CQ + HEADS * HD
CV = CK + 256
CZA = CV + 256
GQ = CZA + 1024
GK = GQ + 512
GV = GK + 512
GR = GV + 1024
GZ = GR + 2 * RANK
CMG = GZ + 1024

AQ, AK, AV = 0, 512, 1024
BQ = 1536
BK = BQ + 512
BV = BK + 128
CQ2 = BV + 128
CKV = CQ2 + 512
CG = CKV + 768
MG2 = CG + 24
NB2 = 31
BUCKETS = 32
TOE = LAT + P - 1
FF = 4096

R_BADA, R_GPRE, R_GPOST, R_CONV, R_GLAG, R_BG, R_QG, R_KG, R_C = 0, 24, 32, 40, 64, 66, 90, 91, 92
R_ROWS = 108
LAM0 = 0.8 - 0.6
GELU = float(np.sqrt(2 / np.pi))
N_PHASES1 = 1 + 11 * DEPTH - 1
N_LAYER1 = 12
S_GAIN, S_SUB, S_MIX, S_MLP = 0, 8, 9, 17
S_ROWS = 25

RING = 4


def constants():
    i = np.arange(P)
    c = {"ident": np.eye(P), "ones": np.ones((P, P)), "blk": (i[:, None] // 64 == i[None] // 64),
         "anti": np.eye(P)[::-1]}
    rot = np.zeros((P, P))
    for d in range(P):
        if d % 64 < 32:
            rot[d + 32, d] = -1
        else:
            rot[d - 32, d] = 1
    c["rot"] = rot
    t = np.arange(LAT)
    pos = np.stack([t // 64, t % 64]).astype(np.float32)
    freq = (np.float32(10000.0) ** (-np.arange(32, dtype=np.float32) * np.float32(2.0) / np.float32(64))).astype(np.float32)
    ang = pos[i // 64] * freq[i % 32][:, None]
    c["cos"], c["sin"] = np.cos(ang), np.sin(ang)
    s, t = i[:, None], i[None, :]
    sums, pairs = [], []
    for back in (False, True):
        m = np.zeros((9, P, P))
        k = np.zeros((8, P, P))
        m[0], m[8] = (s <= t), (s > t)
        for lv in range(LEVELS):
            h = 64 >> lv
            mid = (t // (2 * h)) * 2 * h + h
            m[1 + lv] = np.where(t >= mid, (s >= mid) & (s <= t), (s > t) & (s < mid))
            k[lv] = (s // (2 * h) == t // (2 * h)) & (s % (2 * h) < h) & (t % (2 * h) >= h)
        k[7] = s == t
        if back:
            m, k = m[:, ::-1, ::-1], k[:, ::-1, ::-1]
        sums.append(m.transpose(1, 0, 2).reshape(P, -1) / TAU)
        pairs.append(k.transpose(1, 0, 2).reshape(P, -1))
    c["sums"], c["pairs"] = np.concatenate(sums, 1), np.concatenate(pairs, 1)
    return np.concatenate([np.asarray(v, np.float32) for v in c.values()], axis=1)


C_AT = {}
_at = 0
for _n, _w in (("ident", P), ("ones", P), ("blk", P), ("anti", P), ("rot", P), ("cos", LAT), ("sin", LAT),
               ("sums", 2 * 9 * P), ("pairs", 2 * 8 * P)):
    C_AT[_n] = (_at, _w)
    _at += _w
C_COLS = _at


C2_COLS = 2 * (TOE + 1) + 2 * LT * 32


def constants2():
    dist = LAT - 1 - np.arange(TOE)
    n = np.maximum(dist, 0)
    nf = np.maximum(n, 1).astype(np.float32)
    large = 16 + (np.log(nf / np.float32(16)) / np.float32(np.log(128 / 16)) * 16).astype(np.int32)
    bucket = np.where(n < 16, n, np.minimum(large, BUCKETS - 1))
    out = np.zeros((P, 2 * (TOE + 1) + 2 * LT * 32), np.float32)
    for w, ok in enumerate((dist >= 0, (dist >= 0) & (dist < 128))):
        b = np.where(ok, bucket, BUCKETS)
        out[b, w * (TOE + 1) + np.arange(TOE)] = 1
    t = np.arange(LAT)
    keep = (np.arange(NB2)[None] * 16 + 31 <= t[:, None]).reshape(LT, P, NB2).transpose(1, 0, 2)
    base = 2 * (TOE + 1)
    m = out[:, base:].reshape(P, 2, LT, 32)
    m[:, 0, :, :NB2] = keep
    m[:, 1, :, :NB2] = np.where(keep, 0, NEG)
    return out


class Steps:

    def __init__(self, eng, sem):
        self.eng, self.sem, self.base, self.k = eng, sem, 0, 0

    def __call__(self, ins):
        ins.then_inc(self.sem, 1)
        self.k += 1

    def settle(self):
        self.eng.wait_ge(self.sem, self.base + self.k)

    @contextmanager
    def loop(self, i, n, per):
        start = self.base + self.k
        self.base, self.k = start + i * per, 0
        yield
        assert self.k == per, (self.k, per)
        self.base, self.k = start + n * per, 0


class Turns:

    def __init__(self, size):
        self.size, self.k, self.add = size, 0, 0

    def slot(self):
        return self.k % self.size

    def earlier(self):
        return self.k // self.size + self.add

    def number(self):
        return self.k + self.add * self.size

    def next(self):
        self.k += 1

    def uses_of(self, slot):
        return (self.k - slot + self.size - 1) // self.size + self.add

    @contextmanager
    def loop(self, i, n, per):
        assert per % self.size == 0, per
        start = self.k
        self.add = i * (per // self.size)
        yield
        assert self.k == start + per, (self.k - start, per)
        self.k, self.add = start + n * per, 0


N_INPUTS = 3 + 10 * DEPTH + 5


def two_blocks(nc, a, out, stop=None):
    ctx = ExitStack()
    with ctx:
        def sb(name, shape):
            return ctx.enter_context(nc.sbuf_tensor(name, shape, F32))

        def sem(name):
            return ctx.enter_context(nc.semaphore(name))

        rounded_twin = {}

        def sb_twins(name, shape, cuts=()):
            with nc.sbuf_tensor(name, shape, F32) as plain:
                pass
            edges = [0, *cuts, int(np.prod(shape[1:]))]
            rounded_twin[plain[:].tensor.name] = [
                (lo, hi, ctx.enter_context(nc.sbuf_tensor(f"{name}_parts{lo}", [P, hi - lo], F32R)))
                for lo, hi in zip(edges, edges[1:])]
            return plain

        def as_part(x):
            at = x.offset
            for lo, hi, twin in rounded_twin[x.tensor.name]:
                if lo <= at < hi:
                    return bass.AP(twin[:].tensor, at - lo, [[hi - lo, P]] + [list(d) for d in x.ap][1:])

        ring = sb_twins("ring", [P, RING, KT, P])
        xT = sb_twins("xT", [P, KT, ALL])
        hT = sb_twins("hT", [P, KT, ALL])
        con = sb("con", [P, C_COLS])
        par = [sb(f"par{l}", [P, R_ROWS]) for l in range(DEPTH)]
        par2 = sb("par2", [P, S_ROWS])
        mods = sb("mods", [P, DEPTH * 24, 2])
        scale1 = sb("scale1", [P, KT, 2])
        gpost = sb("gpost", [P, KT, 2])
        half_bg = sb("half_bg", [P, 24])
        stat = sb("stat", [P, 4, 8])
        FREE = 2 * KT * ALL + 15424
        arena = sb_twins("arena", [P, FREE], [2 * KT * ALL])
        ps = ctx.enter_context(nc.psum_tensor("ps", [P, 8 * 512], F32))
        small = sb("small", [P, 96])
        cond_t, cond_s = small[:, 0:16], small[:, 16:32]
        cond0 = small[:, 32:48].rearrange("p (a b) -> p a b", a=2)
        conds = [cond0, sb("cond1", [P, 2, 8])[:]]
        eps, one = small[:, 48:49], small[:, 49:50]
        consts, onec = eps, one
        used = [0]
        whi = ctx.enter_context(nc.sbuf_tensor("whi", [P, 2, KT, P], F32R))[:]
        ringR = as_part(ring[:])

        def take(*shape, at=None):
            n = int(np.prod(shape))
            o = used[0] if at is None else at
            used[0] = o + n
            assert used[0] <= FREE, (shape, used[0], FREE)
            v = arena[:, o:o + n]
            if len(shape) == 2:
                v = v.rearrange("p (a b) -> p a b", a=shape[0])
            if len(shape) == 3:
                v = v.rearrange("p (a b c) -> p a b c", a=shape[0], b=shape[1])
            return v

        def const(name):
            o, w = C_AT[name]
            return con[:, o:o + w]

        ident, ones, blk, anti, rot = (const(n) for n in ("ident", "ones", "blk", "anti", "rot"))
        cos, sin = const("cos"), const("sin")
        sums = const("sums").rearrange("p (d n) -> p d n", d=2)
        pairs = const("pairs").rearrange("p (d l t) -> p d l t", d=2, l=8)

        y = take(KT, ALL)
        acc = take(KT, ALL)
        base = used[0]
        y_in = take(NT, D, at=0)
        tab = [take(P) for _ in range(3)]
        sqb = take(2, ALL, at=base)
        rs = take(ALL)
        lnb = take(ALL)
        tha = take(ALL)
        tmp = take(ALL)
        conv_u = take(LAT + 2 + CTX + 2)
        conv_t = take(ALL)
        bcopy = take(ALL)
        rounded = take(KT * ALL)
        kT = take(2, ALL, at=base)
        vN = take(NT, 256)
        qT = take(2, ALL)
        qsq = take(ALL)
        qln = take(ALL)
        qrs = take(ALL)
        rope_t = take(LAT)
        rope_s = take(LAT)
        prob = take(2, ALL)
        pT = take(NT, LAT)
        pTc = take(CT, CTX)
        zth = take(ALL)
        zsi = take(ALL)
        gr = take(ALL, at=base)
        gwd = take(2, 512)
        gq = take(ALL)
        gk = take(ALL)
        gv = take(NT, DV)
        gla = take(2, NT, P)
        gtmp = take(2, ALL)
        gE = take(9, P)
        gqE = take(3, 8 * P)
        gkE = take(2, 8 * P)
        gatt = take(2, P)
        gkN = take(2, P)
        gS = take(2, DV)
        gdec = take(3)
        gam = gtmp.rearrange("p a b -> p (a b)")[:, 0:8 * P].rearrange("p (l t) -> p l t", l=8)
        gsq = gqE.rearrange("p a b -> p (a b)")[:, 0:2 * ALL].rearrange("p (a b) -> p a b", a=2)

        spare = [C_AT["cos"][0]]

        def take_con(*shape):
            n = int(np.prod(shape))
            o = spare[0]
            spare[0] = o + n
            assert spare[0] <= C_COLS
            v_ = con[:, o:o + n]
            if len(shape) == 2:
                v_ = v_.rearrange("p (a b) -> p a b", a=shape[0])
            return v_

        con2 = take_con(C2_COLS)
        onehot = con2[:, 0:2 * (TOE + 1)].rearrange("p (w m) -> p w m", w=2)
        cmask = con2[:, 2 * (TOE + 1):].rearrange("p (k t c) -> p k t c", k=2, t=LT)
        vA = take_con(LT, 512)
        vB, vS, vW = (take_con(LT, P) for _ in range(3))
        y2 = take(12, LAT, at=0)
        acc2 = acc
        kB, kS, kW = take(LAT, at=base), take(LAT), take(LAT)
        gates = take(LT, 24)
        kc = take(64)
        vc = take(2, 64)
        lam, sinkb = small[:, 50:54], small[:, 54:62]
        stat2 = small[:, 64:96].rearrange("p (a b) -> p a b", a=4)
        n2sq, n2ln, n2rs, n2raw = take(LAT), take(LAT), take(LAT), take(LAT)
        assert used[0] >= base + 4 * ALL
        base2 = used[0]
        relb = take(20, at=base2)
        brow = take(2, TOE + 1)
        lamb = take(256)
        lamp = take(64)
        prep_end = used[0]
        w1k = take(32, 256, at=0)
        w1v = take(32, 256, at=base2)
        tk = take(2, LAT, at=8192)
        posrow = take(2, P, at=base2 + 8192)
        pos = take(2, 32)
        tpos = take(NB2, 32)
        w2k, w2v = take(2, P), take(2, 64)
        hid = take(2, 128)
        hx = take(4, 128)
        qt_ = take(4, LAT, at=base2)
        wb = take(5, LAT)
        prob2 = take(4, LAT)
        pT2 = take(2, LT, LAT)
        pTcmp = take(LAT)
        vAh = take(LT, P, at=KT * ALL)
        tha2, tmp2 = take(LAT, at=base2), take(LAT)
        U = take(FF // P, LAT, at=0)
        rl = take(LAT)
        h3 = take(KT, LAT)
        ob = take(LT, D, at=0)

        def parts(hi, lo):
            return as_part(hi), as_part(lo)

        roundA = rounded.rearrange("p (f n) -> p f n", f=KT)
        round2 = rounded.rearrange("p (f n) -> p f n", f=12)
        hP = parts(xT[:], hT[:])
        yP, accP = parts(roundA, y), parts(roundA, acc)
        y2P = parts(round2, y2)
        h3P = parts(h3, hT[:])
        x_dram = nc.dram_tensor("x_kept", [P, KT, ALL], F32).ap()

        def bank(b, n=512):
            return ps[:, b * 512:b * 512 + n]

        def pair(s, n=ALL):
            return ps[:, s * 1024:s * 1024 + n]

        w_landed = [sem(f"w_landed{s}") for s in range(RING)]
        w_used = sem("w_used")
        w_rounded, w_split = sem("w_rounded"), sem("w_split")
        part_hi, part_lo = sem("part_hi"), sem("part_lo")
        h_ready, h_hi, h_lo = sem("h_ready"), sem("h_hi"), sem("h_lo")
        x_kept, x_back = sem("x_kept"), sem("x_back")
        pair_free = [sem(f"pair_free{s}") for s in range(2)]
        phase, inputs_in, out_done = sem("phase"), sem("inputs_in"), sem("out_done")
        act_own, dve_own = sem("act_own"), sem("dve_own")
        x_turned, par_turned = sem("x_turned"), sem("par_turned")
        sq_ready, sq_used, ms_done, rs_ready = sem("sq_ready"), sem("sq_used"), sem("ms_done"), sem("rs_ready")
        cond_tanh, cond_ready, z_tanh, mod_read = sem("cond_tanh"), sem("cond_ready"), sem("z_tanh"), sem("mod_read")
        scores_done, max_done, exp_done, prob_done = (sem(n) for n in ("scores_done", "max_done", "exp_done", "prob_done"))
        turned, pT_ready, pv_done, head_out = (sem(n) for n in ("turned", "pT_ready", "pv_done", "head_out"))
        qsq_ready, qms_done, qms_read, qrs_ready = (sem(n) for n in ("qsq_ready", "qms_done", "qms_read", "qrs_ready"))
        qn_ready, rot_done, rot_read, q_ready = (sem(n) for n in ("qn_ready", "rot_done", "rot_read", "q_ready"))
        za_tanh, za_silu = sem("za_tanh"), sem("za_silu")
        wd_zero, wd_in = sem("wd_zero"), sem("wd_in")
        dec_done, dec_ln, la_ready = sem("dec_done"), sem("dec_ln"), sem("la_ready")
        sum_done, e_ready, qk_ready, att_done = (sem(n) for n in ("sum_done", "e_ready", "qk_ready", "att_done"))
        att_ready, k_turned, kN_ready = sem("att_ready"), sem("k_turned"), sem("kN_ready")
        o_done, o_read, s_done, s_ready = sem("o_done"), sem("o_read"), sem("s_done"), sem("s_ready")
        gsq_ready, gms_done, grs_ready, gla_out = (sem(n) for n in ("gsq_ready", "gms_done", "grs_ready", "gla_out"))
        masked = sem("masked")

        relb_ready = sem("relb_ready")
        in2, tab2_turned, rows_done, rows_kept = sem("in2"), sem("tab2_turned"), sem("rows_done"), sem("rows_kept")
        rows_mm, lam_sum, w1_in, hid_ready, hid_done = (sem(n) for n in ("rows_mm", "lam_sum", "w1_in", "hid_ready", "hid_done"))
        hx_ready, gelu_arg, gelu_tanh = sem("hx_ready"), sem("gelu_arg"), sem("gelu_tanh")
        bias_in, sq2_ready, ms2_done, rs2_ready = sem("bias_in"), sem("sq2_ready"), sem("ms2_done"), sem("rs2_ready")
        n2_ready, scores2, max2, exp2 = sem("n2_ready"), sem("scores2"), sem("max2"), sem("exp2")
        prob2_ready, turned2, pT2_ready, pv2 = sem("prob2_ready"), sem("turned2"), sem("pT2_ready"), sem("pv2")
        o2_read, relu_ready, out_turned, out_copied = sem("o2_read"), sem("relu_ready"), sem("out_turned"), sem("out_copied")
        rows_dram = nc.dram_tensor("bias_rows", [20, TOE + 1], F32).ap()

        heads2, turns2 = [], 0
        for kind, g, subs in (("A", 0, ("c0", "c1")), ("B", 0, ("b",)), ("B", 1, ("b",)),
                              ("C", 0, ("sel", "win", "cmp")), ("C", 1, ("sel", "win", "cmp"))):
            for qt in range(LT):
                for sub in subs:
                    lo = max(qt - 1, 0) * P if kind == "B" else 0
                    w = NB2 if sub == "cmp" else (qt + 1) * P - lo
                    tn = None if sub == "c0" else turns2
                    turns2 += tn is not None
                    heads2.append(dict(kind=kind, g=g, qt=qt, sub=sub, lo=lo, w=w, turn=tn,
                                       end=qt == LT - 1 and sub == subs[-1]))
        NS2 = len(heads2)
        NORM0 = 4
        LEAD = 3

        def mm(o, l, r, first, last):
            return nc.tensor.matmul(o, l, r, start=first, stop=last)

        def row(buf, j, lo=0, hi=None):
            if isinstance(j, int):
                return buf[:, j, lo:hi]
            return buf[:, ds(j, 1), lo:hi].rearrange("p a n -> p (a n)")

        def score_bank(n, w):
            return bank((6, 7, 0, 2)[n % 4], w)

        def col(buf, j):
            return buf[:, j:j + 1] if isinstance(j, int) else buf[:, ds(j, 1)]

        def spans(n):
            return [(0, LAT)] + ([(LAT, ALL)] if n == ALL else [])

        def gla_units(l):
            fwd = [4, 5, 0, 1, 2, 3]
            bwd = [5, 4, 3, 2, 1, 0]
            units, seen, f = [], set(), 0
            for a_, b_ in zip(fwd, bwd):
                for d, t in ((0, a_), (1, b_)):
                    full = l == 0 or t < LT
                    units.append((d, t, full, t in seen, f))
                    if full:
                        seen.add(t)
                        f += 1
            return units, f

        FILL = [[((0, 4), None, None), ((4, 8), None, None), ((8, 16), None, None), (None, (0, 2), (2, 5)),
                 (None, (5, 7), (7, 10)), (None, (10, 14), None), (None, (14, 16), None)],
                [((0, 4), None, None), ((4, 8), None, None), (None, (0, 2), (2, 4)), (None, (4, 6), (6, 7)),
                 (None, (7, 8), None)]]
        FILL_LAST = [[(None, (0, 2), None), (None, (2, 4), None), (None, (4, 6), None), (None, (6, 8), None),
                      (None, (8, 12), None), (None, (12, 15), None), (None, (15, 16), None)],
                     [(None, (0, 2), None), (None, (2, 4), None), (None, (4, 6), None), (None, (6, 7), None),
                      (None, (7, 8), None)]]
        SQUARE_AT, NORM_AT = [2, 1], [3, 2]

        GU = [gla_units(l) for l in range(DEPTH)]
        NU = 2 * NT
        F_BASE = [0, GHEADS * GU[0][1]]
        QU = [NT, LT]
        U_BASE = [0, HEADS * NT]
        NORMED = 2 + HEADS
        N_ROWS = [R_ROWS, R_ROWS, S_ROWS]

        block = ctx.enter_context(nc.Block())

        @block.sync
        def _(sp):
            tiles = Turns(RING)

            def load(src, kt=KT, m=P):
                if not (isinstance(tiles.number(), int) and tiles.number() < RING):
                    sp.wait_ge(w_used, tiles.number() + 1 - RING)
                v = src.rearrange("(k p) m -> p k m", p=P)
                s = tiles.slot()
                for h in (64, 0):
                    sp.dma_start(ring[h:h + 64, s, 0:kt, 0:m], v[h:h + 64]).then_inc(w_landed[s], 16)
                tiles.next()

            def rows(dst, r, src, c0=0):
                n, w = src.shape
                sp.dma_start(dst[r:r + n, c0:c0 + w], src).then_inc(inputs_in, 16)

            sp.dma_start(con[:], a["con"]).then_inc(inputs_in, 16)
            sp.dma_start(y_in[:, 0:LT, :], a["x"][0].rearrange("(t p) f -> p t f", p=P)).then_inc(inputs_in, 16)
            sp.dma_start(y_in[:, LT:NT, :], a["ctx"][0].rearrange("(t p) f -> p t f", p=P)).then_inc(inputs_in, 16)

            def as_rows(v):
                return v.rearrange("(r c) -> r c", c=P)

            for l in range(DEPTH):
                dst = tab[l]
                rows(dst, R_BADA, as_rows(a["b_ada"][l]))
                rows(dst, R_GPRE, as_rows(a["g_pre"][l]))
                rows(dst, R_GPOST, as_rows(a["g_post"][l]))
                rows(dst, R_CONV, a["conv_w"][l].rearrange("k (r c) -> (k r) c", c=P))
                rows(dst, R_GLAG, as_rows(a["gla_norm_g"][l]))
                rows(dst, R_BG, as_rows(a["b_gate"][l]))
                rows(dst, R_QG, as_rows(a["q_norm_g"][l]))
                rows(dst, R_KG, as_rows(a["k_norm_g"][l]))
                rows(dst, R_C, as_rows(a["c"][0]))
                rows(dst, R_C + 8, as_rows(a["c_ctx"]))
            rows(tab[2], S_GAIN, a["qk_gain_2"][0])
            rows(tab[2], S_GAIN, a["qk_gain_2"][0], c0=64)
            rows(tab[2], S_SUB, a["diff_subln_2"])
            rows(tab[2], S_MIX, as_rows(a["norm_mix_2"][0]))
            rows(tab[2], S_MLP, as_rows(a["norm_mlp_2"][0]))

            def keep_x(phases, n):
                sp.wait_ge(phase, 3 * phases)
                sp.dma_start(x_dram[:, :, 0:n], xT[:, :, 0:n]).then_inc(x_kept, 16)

            def bring_x(phases, n, kept):
                sp.wait_ge(phase, 3 * phases)
                sp.wait_ge(x_kept, 16 * kept)
                sp.dma_start(xT[:, :, 0:n], x_dram[:, :, 0:n]).then_inc(x_back, 16)

            def load_two(src, c):
                for o in ((P, 0) if tiles.slot() == 3 else (0, P)):
                    load(src[:, ds(c + o, P)])

            for l in range(DEPTH):
                w = a["w_in"][l]
                if l == 0:
                    for s in range(4):
                        load(a["w_ada"][0][:, s * P:(s + 1) * P])
                    keep_x(1, ALL)
                    with sp.Fori(0, 3) as i, tiles.loop(i, 3, 4):
                        for s in range(4):
                            load(a["w_ada"][0][:, ds(i * 512 + (4 + s) * P, P)])
                if l == 1:
                    for c in (CZ, CC, CX, CB):
                        load(w[:, c:c + P])
                    keep_x(N_LAYER1, ALL)
                for layer, first, count in (((0, 16, 2), (1, 0, 6)) if l == 0 else ((1, 0, 7),)):
                    at = l if l else 2 * layer
                    per = 8 if l == 0 else 4
                    with sp.Fori(0, count) as i, tiles.loop(i, count, per):
                        for s, c in enumerate((CZ, CC, CX, CB)):
                            load(w[:, ds(i * P + (at * P + c), P)])
                            if l == 0:
                                load(a["w_ada"][layer][:, ds(i * 512 + (first + s) * P, P)])

                def branch(b, src, kt=KT):
                    with sp.Fori(0, KT // 2) as i, tiles.loop(i, KT // 2, 4):
                        for s in range(2):
                            load(w[:, ds(i * 256 + CMG + b * D + s * P, P)])
                            load(src[:, ds(i * 256 + s * P, P)], kt)

                branch(0, a["w_br_conv"][l])
                load(w[:, CK:CK + P])
                load(w[:, CK + P:CK + 2 * P])
                load_two(w, CV)
                load(w[:, CQ:CQ + P])
                with sp.Fori(0, HEADS // 2 - 1) as i, tiles.loop(i, HEADS // 2 - 1, 4):
                    for s in range(2):
                        load(w[:, ds(i * 256 + CQ + (s + 1) * P, P)])
                        load(w[:, ds(i * 256 + CZA + s * P, P)])
                load(w[:, CQ + 7 * P:CQ + 8 * P])
                load(w[:, CZA + 6 * P:CZA + 7 * P])
                load(w[:, CZA + 7 * P:CZA + 8 * P])
                branch(1, a["w_br_attn"][l])
                load(w[:, GR:GR + 32], m=32)
                load(w[:, GQ:GQ + P])
                with sp.Fori(0, GHEADS - 1) as i, tiles.loop(i, GHEADS - 1, 4):
                    load_two(w, i * DV + GV)
                    load(w[:, ds(i * P + GK, P)])
                    load(w[:, ds(i * P + GQ + P, P)])
                load_two(w, (GHEADS - 1) * DV + GV)
                load(w[:, GK + (GHEADS - 1) * P:GK + GHEADS * P])
                with sp.Fori(0, 2) as i, tiles.loop(i, 2, 4):
                    for s in range(4):
                        load(w[:, ds(i * 512 + GZ + s * P, P)])
                branch(2, a["w_br_gla"][l])
                for s in range(8):
                    if s == 4:
                        bring_x(10 * (l + 1), ALL, l + 1)
                    load(a["w_out"][l][:, s * P:(s + 1) * P])
            w = a["w_in_2"][0]
            for c in range(4):
                load(w[:, AV + c * P:AV + (c + 1) * P])
            sp.wait_ge(phase, 3 * N_PHASES1)
            sp.dma_start(con2, a["con2"]).then_inc(in2, 16)
            sp.dma_start(relb[0:BUCKETS], a["rel_bias_2"]).then_inc(in2, 16)
            sp.dma_start(lamb, a["diff_lambda_2"][0].rearrange("(o a) b -> o (a b)", o=1).to_broadcast([P, 256])).then_inc(in2, 16)
            sp.dma_start(sinkb, a["sinks_2"].to_broadcast([P, 8])).then_inc(in2, 16)
            keep_x(N_PHASES1, LAT)
            for c in (BV, CKV + 3 * P, BK, CKV, CKV + P, CKV + 2 * P, CKV + 4 * P, CKV + 5 * P):
                load(w[:, c:c + P])
            load(w[:, CG:CG + 24], m=24)

            def load_halves(c, i):
                sp.wait_ge(w_used, tiles.number() + 1 - RING)
                s = tiles.slot()
                for g in (1, 0):
                    sp.dma_start(ring[:, s, :, g * 64:(g + 1) * 64],
                                 w[:, ds(i * 64 + c + g * 256, 64)].rearrange("(k p) m -> p k m", p=P))\
                        .then_inc(w_landed[s], 16)
                tiles.next()

            sp.wait_ge(rows_kept, 48)
            with sp.Fori(0, 4) as i, tiles.loop(i, 4, 4):
                load(w[:, ds(i * P + AQ, P)])
                load(w[:, ds(i * P + AK, P)])
                load_halves(BQ, i)
                load_halves(CQ2, i)
                sp.wait_ge(phase, 3 * (N_PHASES1 + 3))
                sp.wait_ge(scores2, i * NS2)
                for k in (4, 3, 2, 1, 0):
                    r = rows_dram[ds(i + 4 * k, 1), 0:LAT]
                    sp.dma_start(wb[:, k], bass.AP(r.tensor, r.offset, [[1, P], [1, LAT]])).then_inc(bias_in, 16)
            for b in range(3):
                wbr = a["w_branch_2"][0, b]
                with sp.Fori(0, KT // 2) as i, tiles.loop(i, KT // 2, 4):
                    for s in range(2):
                        load(w[:, ds(i * 256 + MG2 + b * D + s * P, P)])
                        src = wbr[:, ds(i * 256 + s * P, P)]
                        if b == 0:
                            load(src, 4)
                        else:
                            sp.wait_ge(w_used, tiles.number() + 1 - RING)
                            v = src.rearrange("(h k p) m -> h p k m", h=2, p=64)
                            for h in (1, 0):
                                sp.dma_start(ring[h * 64:(h + 1) * 64, tiles.slot(), 0:4], v[h])\
                                    .then_inc(w_landed[tiles.slot()], 16)
                            tiles.next()
            for s in range(8):
                if s == 4:
                    bring_x(N_PHASES1 + 5, LAT, 3)
                load(a["w_out_2"][0][:, s * P:(s + 1) * P])
            with sp.Fori(0, 8) as i, tiles.loop(i, 8, 4):
                for s in range(4):
                    load(a["w_up_2"][0][:, ds(i * 512 + s * P, P)])
            with sp.Fori(0, 4) as i, tiles.loop(i, 4, 8):
                for s in range(2):
                    for k in range(4):
                        load(a["w_down_2"][0][k * D:(k + 1) * D, ds(i * 256 + s * P, P)])
            for t in range(LT):
                sp.wait_ge(out_copied, t + 1)
                sp.dma_start(out[0, t * P:(t + 1) * P, :], ob[:, t]).then_inc(out_done, 16)
            sp.wait_ge(out_done, 16 * LT)

        @block.gpsimd
        def _(pool):
            tiles, splits = Turns(RING), Turns(2)
            v = nc.gpsimd

            def split(kt=KT, m=P, back=2):
                s, h = tiles.slot(), splits.slot()
                pool.wait_ge(w_landed[s], tiles.earlier() * 32 + 32)
                pool.wait_ge(w_used, tiles.number() + 1 - back)
                raw = ring[:, s, 0:kt, 0:m]
                hi = whi[:, h, 0:kt, 0:m]
                v.tensor_tensor(hi, raw, ones[:, 0:m].unsqueeze(1).to_broadcast([P, kt, m]), ALU.mult).then_inc(w_rounded, 1)
                pool.wait_ge(w_rounded, splits.number() + 1)
                v.tensor_tensor(ringR[:, s, 0:kt, 0:m], raw, hi.bitcast(F32), ALU.subtract).then_inc(w_split, 1)
                tiles.next()
                splits.next()

            def split_all(n):
                with pool.Fori(0, n // 4) as i, tiles.loop(i, n // 4, 4), splits.loop(i, n // 4, 4):
                    for _ in range(4):
                        split()

            pool.wait_ge(inputs_in, 16 * N_INPUTS)
            for l in range(DEPTH):
                if l == 0:
                    for _ in range(16):
                        tiles.next()
                    with pool.Fori(0, KT) as i, tiles.loop(i, KT, 8), splits.loop(i, KT, 4):
                        for _ in range(4):
                            split(back=4)
                            tiles.next()
                else:
                    split_all(4 * KT)
                split_all(16 + 20 + 16)
                split(m=32)
                split()
                pool.wait_ge(wd_zero, l + 1)
                for d, (wn, bn) in enumerate((("w_decay_fwd", "b_decay_fwd"), ("w_decay_bwd", "b_decay_bwd"))):
                    pool.dma_start(gwd[d * RANK:(d + 1) * RANK, d], a[wn][l]).then_inc(wd_in, 16)
                    pool.dma_start(gwd[32:33, d], a[bn][l:l + 1, :]).then_inc(wd_in, 16)
                split_all(12)
                for _ in range(3):
                    split()
                split_all(8 + 16 + 8)
            split()
            split()
            pool.wait_ge(rows_done, 2)
            pool.dma_start(rows_dram[0:4], brow[0:4, 0]).then_inc(rows_kept, 16)
            pool.dma_start(rows_dram[4:12], brow[4:12, 1]).then_inc(rows_kept, 16)
            pool.dma_start(rows_dram[12:20], brow[12:20, 0]).then_inc(rows_kept, 16)
            pool.wait_ge(phase, 3 * (N_PHASES1 + 1))
            pool.wait_ge(rows_kept, 48)
            for kv, (w1, w2) in enumerate(((w1k, w2k), (w1v, w2v))):
                for h in (0, 64):
                    pool.dma_start(w1[h:h + 64], a["cmp_w1_2"][0, kv].rearrange("(j d) h -> d j h", d=64)).then_inc(w1_in, 16)
                    pool.dma_start(posrow[0:32, kv, h:h + 64], a["cmp_pos_2"][0, kv]).then_inc(w1_in, 16)
                for h in (0, 64)[:2 - kv]:
                    pool.dma_start(w2[:, :, h:h + 64], a["cmp_w2_2"][0, kv].rearrange("(k p) d -> p k d", p=P)).then_inc(w1_in, 16)
            for _ in range(10):
                split()
            split(m=24)
            split_all(16)
            for _ in range(3):
                with pool.Fori(0, KT // 2) as i, tiles.loop(i, KT // 2, 4), splits.loop(i, KT // 2, 4):
                    for _ in range(2):
                        split()
                        split(kt=4)
            split_all(8 + 32)

        @block.tensor
        def _(pe):
            tiles, uses, splits = Turns(RING), Turns(2), Turns(2)
            ends = [0]
            norms = [0]

            def phase_end(name):
                pe.drain().then_inc(phase, 1)
                ends[0] += 3
                pe.wait_ge(phase, ends[0])
                return name == stop

            def all_read():
                for s in range(2):
                    pe.wait_ge(pair_free[s], uses.uses_of(s))

            def begin_tile():
                pe.wait_ge(w_split, splits.number() + 1)
                pe.wait_ge(pair_free[uses.slot()], uses.earlier())
                return this_tile(), uses.slot()

            def this_tile():
                return whi[:, splits.slot()], ringR[:, tiles.slot()]

            def end_tile(last):
                last.then_inc(w_used, 1)
                tiles.next()
                splits.next()
                uses.next()

            def product_of_parts(o, w, x, first, last):
                mm(o, w[0], x[0], first, False)
                mm(o, w[0], x[1], False, False)
                return mm(o, w[1], x[0], False, last)

            def tile_step(w, s, src, k, lo, hi, kt=KT, m=P):
                return product_of_parts(pair(s)[0:m, lo:hi], [t[:, k, 0:m] for t in w], [x[:, k, lo:hi] for x in src],
                                        k == 0, k == kt - 1)

            def turned_tile(src, n=ALL, kt=KT, m=P):
                w, s = begin_tile()
                for lo, hi in spans(n):
                    for k in range(kt):
                        last = tile_step(w, s, src, k, lo, hi, kt, m)
                end_tile(last)

            def token_tile(nt=NT, m=P):
                w, s = begin_tile()
                for t in range(nt):
                    for k in range(KT):
                        last = product_of_parts(pair(s, 1024)[:, t * m:(t + 1) * m],
                                                [x[:, k, t * P:(t + 1) * P] for x in hP], [z[:, k, 0:m] for z in w],
                                                k == 0, k == KT - 1)
                end_tile(last)

            def two_token_tiles(nt):
                assert splits.slot() == tiles.slot() % 2
                pe.wait_ge(w_split, splits.number() + 2)
                at = 0 if nt == NT else uses.slot() * 1024
                for _ in range(1 + (nt == NT)):
                    pe.wait_ge(pair_free[uses.slot()], uses.earlier())
                    uses.next()
                s = tiles.slot()
                w = whi, (ringR[:, 0:4:3] if s == 3 else ringR[:, s:s + 2])
                for t in range(nt):
                    o = ps[:, at + t * 256:at + (t + 1) * 256].rearrange("p (a m) -> p a m", a=2)
                    for k in range(KT):
                        last = product_of_parts(o, [x[:, k, t * P:(t + 1) * P] for x in hP], [z[:, :, k, :] for z in w],
                                                k == 0, k == KT - 1)
                last.then_inc(w_used, 2)
                for _ in range(2):
                    tiles.next()
                    splits.next()

            def mean_square(n):
                for f in range(KT):
                    pe.wait_ge(sq_ready, norms[0] * KT + f + 1)
                    for lo, hi in spans(n):
                        last = mm(bank(4, 1024)[:, lo:hi], ones, sqb[:, f % 2, lo:hi], f == 0, f == KT - 1)
                    last.then_inc(sq_used, 1)
                norms[0] += 1

            pe.wait_ge(inputs_in, 16 * N_INPUTS)
            for j in range(3):
                n = N_ROWS[j]
                nc.tensor.transpose(bank(4 + j, n), tab[j][0:n, :], ident[0:n, 0:n]).then_inc(par_turned, 1)
            for f in range(KT):
                pe.wait_ge(pair_free[uses.slot()], uses.earlier())
                for t in range(NT):
                    last = nc.tensor.transpose(pair(uses.slot())[:, t * P:(t + 1) * P],
                                               y_in[:, t, f * P:(f + 1) * P], ident)
                last.then_inc(x_turned, 1)
                uses.next()
            if phase_end("load"):
                return

            parts_made = [0]

            def branch(n):
                parts_made[0] += KT
                with pe.Fori(0, KT // 2) as i, tiles.loop(i, KT // 2, 4), uses.loop(i, KT // 2, 4), splits.loop(i, KT // 2, 4):
                    for s in range(2):
                        turned_tile(hP, n)
                        pe.wait_ge(part_lo, parts_made[0])
                        turned_tile(yP, n)

            for l in range(DEPTH):
                n = ALL if l == 0 else LAT
                qu = QU[l]
                if l == 0:
                    mean_square(ALL)
                    pe.wait_ge(cond_ready, DEPTH)
                    with pe.Fori(0, 4) as i, tiles.loop(i, 4, 4), uses.loop(i, 4, 4):
                        for _ in range(4):
                            pe.wait_ge(w_landed[tiles.slot()], tiles.earlier() * 32 + 32)
                            pe.wait_ge(pair_free[uses.slot()], uses.earlier())
                            for k in range(KT):
                                last = mm(pair(uses.slot())[:, 0:2], ring[:, tiles.slot(), k], conds[0][:, :, k],
                                          k == 0, k == KT - 1)
                            last.then_inc(w_used, 1)
                            tiles.next()
                            uses.next()
                    if phase_end("ada0"):
                        return
                else:
                    mean_square(ALL)
                if phase_end(f"norm{l}"):
                    return

                def conv(i, cond):
                    for s in range(4):
                        turned_tile(hP, n)
                        if cond is None:
                            continue
                        pe.wait_ge(w_landed[tiles.slot()], tiles.earlier() * 32 + 32)
                        if s == 0:
                            pe.wait_ge(mod_read, i)
                        for k in range(KT):
                            last = mm(bank(6)[:, 2 * s:2 * s + 2], ring[:, tiles.slot(), k], cond[:, :, k], k == 0, k == KT - 1)
                        last.then_inc(w_used, 1)
                        tiles.next()

                if l == 0:
                    with pe.Fori(0, 2) as i, tiles.loop(i, 2, 8), uses.loop(i, 2, 4), splits.loop(i, 2, 4):
                        conv(i, conds[0])
                    with pe.Fori(0, 6) as i, tiles.loop(i, 6, 8), uses.loop(i, 6, 4), splits.loop(i, 6, 4):
                        conv(i + 2, conds[1])
                else:
                    with pe.Fori(0, KT) as i, tiles.loop(i, KT, 4), uses.loop(i, KT, 4), splits.loop(i, KT, 4):
                        conv(i, None)
                if phase_end(f"conv{l}"):
                    return
                branch(n)
                if phase_end(f"branch{l}0"):
                    return

                def norm_mm(c, m, free=None):
                    pe.wait_ge(qsq_ready, c + 1)
                    pe.wait_ge(*(free or (rot_read, c)))
                    for lo, hi in spans(m):
                        last = mm(bank(4, 1024)[:, lo:hi], ones, qsq[:, lo:hi], True, True)
                    last.then_inc(qms_done, 1)

                def rotate(c, src, free=None):
                    pe.wait_ge(qn_ready, c + 1)
                    pe.wait_ge(*(free or (qms_read, c + 1)))
                    mm(bank(4), rot, src[:, 0:LAT], True, True).then_inc(rot_done, 1)

                nb = NORMED * l
                turned_tile(hP)
                norm_mm(nb, ALL)
                rotate(nb, kT[:, 0])
                turned_tile(hP)
                norm_mm(nb + 1, ALL)
                rotate(nb + 1, kT[:, 1])
                two_token_tiles(NT)
                turned_tile(hP, n)
                norm_mm(nb + 2, n)
                rotate(nb + 2, qT[:, 0])

                def step(off, i, kv, last_head=False):
                    q, nq = qT[:, off % 2], qT[:, (off + 1) % 2]
                    u0 = i * (2 * qu) + (U_BASE[l] + off * qu)
                    hn = i * 2 + (HEADS * l + off)
                    c = i * 2 + (nb + 3 + off)

                    def scores(t):
                        if t == 0:
                            pe.wait_ge(q_ready, c)
                        pe.wait_ge(exp_done, u0 + t)
                        qs = q[:, t * P:(t + 1) * P]
                        if t < LT:
                            mm(bank(6), qs, kT[:, kv, 0:LAT], True, True)
                            mm(bank(7, CTX), qs, kT[:, kv, LAT:ALL], True, True).then_inc(scores_done, 1)
                        else:
                            mm(bank(6, CTX), qs, kT[:, kv, LAT:ALL], True, True).then_inc(scores_done, 1)

                    def turn(t, free):
                        pe.wait_ge(prob_done, u0 + t + 1)
                        pe.wait_ge(*free)
                        for s in range(NT if t < LT else CT):
                            x = nc.tensor.transpose(bank(4, 1024)[:, s * P:(s + 1) * P],
                                                    prob[:, t % 2, s * P:(s + 1) * P], ident)
                        x.then_inc(turned, 1)

                    steps = KT * len(spans(n))

                    def fill(part):
                        if part is None:
                            return
                        if part[0] == 0:
                            begin_tile()
                        w, s = this_tile(), uses.slot()
                        for k in range(*part):
                            last = tile_step(w, s, hP, k % KT, *spans(n)[k // KT])
                        if part[1] == steps:
                            end_tile(last)

                    table = FILL_LAST[l] if last_head else FILL[l]
                    for t in range(qu):
                        queries, gate1, gate2 = table[t]
                        scores(t)
                        fill(queries)
                        fill(gate1)
                        free = (pT_ready, u0 + t) if t else (head_out, hn)
                        if not last_head and t == NORM_AT[l]:
                            norm_mm(c, n, free)
                            free = (qms_read, c + 1)
                        if not last_head and t == NORM_AT[l] + 1:
                            rotate(c, nq, free)
                            free = (rot_read, c + 1)
                        fill(gate2)
                        turn(t, free)
                    fill(table[qu][1])
                    pe.wait_ge(pT_ready, u0 + qu)
                    for s in range(NT):
                        last = mm(bank(4), vN[:, s, kv * P:(kv + 1) * P], pT[:, s], s == 0, s == NT - 1)
                    if qu > LT:
                        for s in range(CT):
                            last = mm(bank(5, CTX), vN[:, LT + s, kv * P:(kv + 1) * P], pTc[:, s], s == 0, s == CT - 1)
                    last.then_inc(pv_done, 1)

                all_read()
                with pe.Fori(0, 2) as i, tiles.loop(i, 2, 4), uses.loop(i, 2, 4), splits.loop(i, 2, 4):
                    step(0, i, 0)
                    step(1, i, 0)
                step(0, 2, 1)
                step(1, 2, 1)
                step(0, 3, 1)
                step(1, 3, 1, True)
                if phase_end(f"attn{l}"):
                    return
                branch(n)
                if phase_end(f"branch{l}1"):
                    return

                turned_tile(hP, ALL, m=32)
                pe.wait_ge(wd_in, 64 * (l + 1))
                all_read()
                units, nf = GU[l]
                turned_tile(hP, n)

                def head(i, last_head=False):
                    hh = i + GHEADS * l
                    u0 = hh * NU
                    f0 = i * nf + F_BASE[l]
                    pe.wait_ge(grs_ready, hh * 2)
                    pe.wait_ge(s_ready, u0)
                    for d in range(2):
                        for t in range(NT):
                            last = mm(bank(4 + 2 * d, 1024)[:, t * P:(t + 1) * P], gr[0:33, t * P:(t + 1) * P],
                                      gwd[0:33, d, i * P:(i + 1) * P] if isinstance(i, int) else gwd[0:33, d, ds(i * P, P)],
                                      True, True)
                    last.then_inc(dec_done, 1)
                    two_token_tiles(NT)
                    turned_tile(hP)
                    pe.wait_ge(la_ready, hh * 2 + 2)

                    def exponents(j):
                        d, t, full = units[j][:3]
                        pe.wait_ge(e_ready, u0 + j)
                        if full:
                            for c in range(3):
                                last = mm(bank(c, 384), gla[:, d, t], sums[:, d, c * 384:(c + 1) * 384], True, True)
                        else:
                            for c, k in ((0, 0), (1, 8)):
                                last = mm(bank(c, P), gla[:, d, t], sums[:, d, k * P:(k + 1) * P], True, True)
                        last.then_inc(sum_done, 1)

                    def levels(j):
                        d, t, full, _, f = units[j]
                        pe.wait_ge(qk_ready, u0 + j + 1)
                        pe.wait_ge(kN_ready, u0 + j)
                        nc.tensor.transpose(bank(6, P), gkE[:, j % 2, 7 * P:8 * P], ident).then_inc(k_turned, 1)
                        if full:
                            pe.wait_ge(masked, f0 + f)
                            for lv in range(LEVELS):
                                mm(bank(3, 1024)[:, lv * P:(lv + 1) * P], gkE[:, j % 2, lv * P:(lv + 1) * P],
                                   gqE[:, j % 3, (lv + 1) * P:(lv + 2) * P], True, True)
                            mm(bank(3, 1024)[:, 7 * P:8 * P], gk[:, t * P:(t + 1) * P], gq[:, t * P:(t + 1) * P],
                               True, True).then_inc(att_done, 1)

                    def outputs(j):
                        d, t, full, _, f = units[j]
                        if full:
                            pe.wait_ge(s_ready, u0 + max(j - 1, 0))
                            pe.wait_ge(att_ready, f0 + f + 1)
                            pe.wait_ge(o_read, f0 + f)
                            for v in range(2):
                                mm(bank(5, DV)[:, v * P:(v + 1) * P], gS[:, d, v * P:(v + 1) * P], gqE[:, j % 3, 0:P],
                                   True, False)
                                last = mm(bank(5, DV)[:, v * P:(v + 1) * P], gv[:, t, v * P:(v + 1) * P], gatt[:, f % 2],
                                          False, True)
                            last.then_inc(o_done, 1)
                        pe.wait_ge(kN_ready, u0 + j + 1)
                        pe.wait_ge(s_ready, u0 + j)
                        mm(bank(7, DV), gkN[:, j % 2], gv[:, t], True, True).then_inc(s_done, 1)

                    all_read()
                    exponents(0)
                    for j in range(NU):
                        if j + 1 < NU:
                            exponents(j + 1)
                        levels(j)
                        if j:
                            outputs(j - 1)
                    outputs(NU - 1)
                    if not last_head:
                        pe.wait_ge(e_ready, u0 + NU)
                        pe.wait_ge(masked, f0 + nf)
                        turned_tile(hP, n)
                    pe.wait_ge(gsq_ready, hh + 1)
                    for lo, hi in spans(n):
                        for v in range(2):
                            last = mm(bank(4, 1024)[:, lo:hi], ones, gsq[:, v, lo:hi], v == 0, v == 1)
                    last.then_inc(gms_done, 1)

                with pe.Fori(0, GHEADS - 1) as i, tiles.loop(i, GHEADS - 1, 4), uses.loop(i, GHEADS - 1, 4), \
                        splits.loop(i, GHEADS - 1, 4):
                    head(i)
                head(GHEADS - 1, True)
                if phase_end(f"gla{l}"):
                    return
                with pe.Fori(0, 2) as i, tiles.loop(i, 2, 4), uses.loop(i, 2, 4), splits.loop(i, 2, 4):
                    for _ in range(4):
                        turned_tile(hP, n)
                if phase_end(f"glaz{l}"):
                    return
                branch(n)
                if phase_end(f"branch{l}2"):
                    return
                parts_made[0] += KT
                pe.wait_ge(part_lo, parts_made[0])
                with pe.Fori(0, 2) as i, tiles.loop(i, 2, 4), uses.loop(i, 2, 4), splits.loop(i, 2, 4):
                    for _ in range(4):
                        turned_tile(accP, n)
                if phase_end(f"out{l}"):
                    return
                mean_square(n)
                if phase_end(f"post{l}"):
                    return
            norms2, turn_base = [0], [0]

            def block_norm_mm(c, m, n=LAT):
                pe.wait_ge(sq2_ready, c + 1)
                pe.wait_ge(rs2_ready, c)
                mm(bank(3, n), m, n2sq[:, 0:n], True, True).then_inc(ms2_done, 1)

            mean_square(LAT)
            pe.wait_ge(in2, 64)
            pe.wait_ge(relb_ready, 1)
            for w_ in range(2):
                for lo, hi in ((0, 512), (512, TOE)):
                    last = mm(pair(w_)[0:20, lo:hi], relb[0:BUCKETS + 1, 0:20], onehot[0:BUCKETS + 1, w_, lo:hi], True, True)
            last.then_inc(rows_mm, 1)
            if phase_end("norm2"):
                return
            for _ in range(3):
                two_token_tiles(LT)
            turned_tile(hP, LAT)
            block_norm_mm(0, blk)
            for _ in range(3):
                turned_tile(hP, LAT)
            block_norm_mm(1, blk)
            turned_tile(hP, LAT)
            block_norm_mm(2, blk)
            token_tile(LT)
            token_tile(LT, m=24)
            pe.wait_ge(w1_in, 16 * 11)
            for kv in range(2):
                nc.tensor.transpose(bank(6 + kv, 32), posrow[0:32, kv], ident[0:32, 0:32]).then_inc(tab2_turned, 1)
            if phase_end("kv2"):
                return
            for kv, w1 in enumerate((w1k, w1v)):
                pe.wait_ge(hid_ready, kv + 1)
                for m in range(2):
                    for g in range(2):
                        for j in range(32):
                            last = mm(bank(6 - 2 * kv + g)[:, m * NB2:(m + 1) * NB2], w1[g * 64:(g + 1) * 64, j, m * P:(m + 1) * P],
                                      tpos[g * 64:(g + 1) * 64, :, j], j == 0, j == 31)
                last.then_inc(hid_done, 1)
            pe.wait_ge(hid_ready, 3)
            for k in range(2):
                last = mm(bank(0, 2 * NB2), w2k[:, k], hid[:, 0, k * 62:(k + 1) * 62], k == 0, k == 1)
            last.then_inc(hid_done, 1)
            block_norm_mm(3, blk, 2 * NB2)
            pe.wait_ge(hid_ready, 4)
            for g in range(2):
                for k in range(2):
                    o = k * 62 + g * NB2
                    last = mm(bank(2)[0:NB2, g * 64:(g + 1) * 64], hid[:, 1, o:o + NB2], w2v[:, k], k == 0, k == 1)
            last.then_inc(hid_done, 1)
            if phase_end("cmp"):
                return
            with pe.Fori(0, 4) as i, tiles.loop(i, 4, 4), uses.loop(i, 4, 4), splits.loop(i, 4, 4):
                c0 = i * 5 + NORM0
                s0, t0 = i * NS2, i * turns2
                pe.wait_ge(exp2, i * NS2)
                for c in range(4):
                    turned_tile(hP, LAT)
                    if c:
                        block_norm_mm(c0 + (c - 1), blk)
                block_norm_mm(c0 + 3, blk)
                pe.wait_ge(n2_ready, c0 + 4)
                pe.wait_ge(bias_in, i * 80 + 80)

                def scores(n):
                    u = heads2[n]
                    b = score_bank(n, u["w"])
                    pe.wait_ge(exp2, s0 + max(n - 3, 0))
                    g, q0 = u["g"] * 64, u["qt"] * P
                    if u["kind"] == "A":
                        g = 64 * (u["sub"] == "c1")
                        q, k = qt_[g:g + 64, 0, q0:q0 + P], qt_[g:g + 64, 1]
                    elif u["kind"] == "B":
                        q, k = qt_[g:g + 64, 2, q0:q0 + P], kB[g:g + 64]
                    else:
                        q, k = qt_[g:g + 64, 3, q0:q0 + P], (kW if u["sub"] == "win" else kS)[g:g + 64]
                    if u["sub"] == "cmp":
                        mm(b, q, kc[g:g + 64, u["g"] * NB2:(u["g"] + 1) * NB2], True, False)
                        mm(b, ident, cmask[:, 1, u["qt"], 0:NB2], False, True).then_inc(scores2, 1)
                    else:
                        slot = {"A": 0, "B": 1, "C": 3}[u["kind"]] + u["g"]
                        mm(b, q, k[:, u["lo"]:u["lo"] + u["w"]], True, False)
                        mm(b, anti, wb[:, slot, LAT - u["w"]:LAT], False, True).then_inc(scores2, 1)

                def turn(n):
                    u = heads2[n]
                    tn = u["turn"]
                    if tn is None:
                        return
                    pe.wait_ge(prob2_ready, t0 + tn + 1)
                    pe.wait_ge(pT2_ready, t0 + (tn - 1) if tn else i * turns2)
                    src = prob2[:, (n - 1 if u["kind"] == "A" else n) % 4]
                    if u["sub"] == "cmp":
                        last = nc.tensor.transpose(bank(4 + tn % 2)[0:NB2, 0:P], src[:, 0:NB2], ident)
                    else:
                        for k in range(u["w"] // P):
                            last = nc.tensor.transpose(bank(4 + tn % 2)[:, k * P:(k + 1) * P], src[:, k * P:(k + 1) * P], ident)
                    last.then_inc(turned2, 1)

                def values(n):
                    u = heads2[n]
                    g = u["g"] * 64
                    pe.wait_ge(pT2_ready, t0 + u["turn"] + 1)
                    pe.wait_ge(o2_read, i * 3 + {"A": 0, "B": 1, "C": 2}[u["kind"]])
                    if u["kind"] == "A":
                        for s in range(LT):
                            last = mm(bank(1)[:, s * P:], vAh[:, s], pT2[:, 0, s, s * P:], s == 0, s == LT - 1)
                    elif u["kind"] == "B":
                        for t in range(LT):
                            for s in range(max(t - 1, 0), t + 1):
                                last = mm(bank(1)[g:g + 64, t * P:(t + 1) * P], vB[:, s, g:g + 64],
                                          pT2[:, 0, s, t * P:(t + 1) * P], s == max(t - 1, 0), s == t)
                    else:
                        for s in range(LT):
                            mm(bank(1)[g:g + 64, s * P:], vS[:, s, g:g + 64], pT2[:, 0, s, s * P:], s == 0, False)
                            mm(bank(1)[g:g + 64, s * P:], vW[:, s, g:g + 64], pT2[:, 1, s, s * P:], False, False)
                        last = mm(bank(1)[g:g + 64, :], vc[0:NB2, u["g"]], pTcmp[0:NB2], False, True)
                    last.then_inc(pv2, 1)

                for n in range(LEAD):
                    scores(n)
                for n in range(NS2):
                    if n + LEAD < NS2:
                        scores(n + LEAD)
                    ended = n > 0 and heads2[n - 1]["end"]
                    if ended:
                        values(n - 1)
                    turn(n)
                    if ended and heads2[n - 1]["kind"] == "A":
                        block_norm_mm(c0 + 4, ones)
                values(NS2 - 1)
            if phase_end("heads"):
                return
            parts_made[0] += 12
            for b in range(3):
                with pe.Fori(0, KT // 2) as i, tiles.loop(i, KT // 2, 4), uses.loop(i, KT // 2, 4), splits.loop(i, KT // 2, 4):
                    for s in range(2):
                        turned_tile(hP, LAT)
                        pe.wait_ge(part_lo, parts_made[0])
                        turned_tile([x[:, 4 * b:4 * b + 4] for x in y2P], LAT, kt=4)
            if phase_end("branches2"):
                return
            parts_made[0] += KT
            pe.wait_ge(part_lo, parts_made[0])
            with pe.Fori(0, 2) as i, tiles.loop(i, 2, 4), uses.loop(i, 2, 4), splits.loop(i, 2, 4):
                for _ in range(4):
                    turned_tile(accP, LAT)
            if phase_end("out2"):
                return
            mean_square(LAT)
            if phase_end("norm3"):
                return
            with pe.Fori(0, 8) as i, tiles.loop(i, 8, 4), uses.loop(i, 8, 4), splits.loop(i, 8, 4):
                for _ in range(4):
                    turned_tile(h3P, LAT)
            if phase_end("up"):
                return
            with pe.Fori(0, 4) as i, tiles.loop(i, 4, 8), uses.loop(i, 4, 2):
                for _ in range(2):
                    pe.wait_ge(pair_free[uses.slot()], uses.earlier())
                    for f in range(4):
                        pe.wait_ge(w_landed[tiles.slot()], tiles.earlier() * 32 + 32)
                        for k in range(KT):
                            last = mm(bank(2 * uses.slot()), ring[:, tiles.slot(), k], U[:, f * KT + k],
                                      f == 0 and k == 0, f == 3 and k == KT - 1)
                        last.then_inc(w_used, 1)
                        tiles.next()
                    uses.next()
            if phase_end("down"):
                return
            for t in range(LT):
                if t >= 2:
                    pe.wait_ge(out_copied, t - 1)
                for f in range(KT):
                    last = nc.tensor.transpose(pair(uses.slot(), 1024)[:, f * P:(f + 1) * P], xT[:, f, t * P:(t + 1) * P], ident)
                last.then_inc(out_turned, 1)
                uses.next()
            phase_end("end")

        @block.scalar
        def _(act):
            tiles, uses = Turns(RING), Turns(2)
            own = Steps(act, act_own)
            ends, norms = [0], [0]

            def do(o, i, f, **kw):
                return nc.scalar.activation(o, i, f, **kw)

            def phase_end(name):
                act.drain().then_inc(phase, 1)
                ends[0] += 3
                act.wait_ge(phase, ends[0])
                return name == stop

            def product():
                act.wait_ge(w_used, tiles.number() + 1)
                return uses.slot()

            def release(ins):
                ins.then_inc(pair_free[uses.slot()], 1)
                skip()

            def skip(n=1):
                for _ in range(n):
                    tiles.next()
                    uses.next()

            def last_read():
                k = uses.k - 1
                act.wait_ge(pair_free[k % 2], k // 2 + 1 + uses.add)

            def inverse_root(dst, lnbuf, src, count, sem_read=None):
                ins = do(lnbuf, src, ACT.Ln, scale=1.0 / count, bias=eps)
                if sem_read is None:
                    own(ins)
                    own.settle()
                else:
                    ins.then_inc(sem_read[0], 1)
                    act.wait_ge(*sem_read)
                return do(dst, lnbuf, ACT.Exp, scale=-0.5)

            def squares(src, n):
                for f in range(KT):
                    c = norms[0] * KT + f
                    if f >= 2:
                        act.wait_ge(sq_used, c - 1)
                    do(sqb[:, f % 2, 0:n], src[:, f, 0:n], ACT.Square).then_inc(sq_ready, 1)
                norms[0] += 1
                act.wait_ge(sq_used, norms[0] * KT)
                inverse_root(rs[:, 0:n], lnb[:, 0:n], bank(4, n), D).then_inc(rs_ready, 1)

            parts_made, normed = [0], [0]

            def round_rows(dst, src, n):
                for f in range(src.shape[1]):
                    do(dst[0][:, f, 0:n], src[:, f, 0:n], ACT.Copy).then_inc(part_hi, 1)

            def round_input(dst, n, kept):
                if kept:
                    act.wait_ge(x_kept, 16 * kept)
                for f in range(KT):
                    normed[0] += 1
                    act.wait_ge(h_ready, normed[0])
                    do(dst[:, f, 0:n], hT[:, f, 0:n], ACT.Copy).then_inc(h_hi, 1)

            for j in range(3):
                act.wait_ge(par_turned, j + 1)
                own(do((par + [par2])[j][:, 0:N_ROWS[j]], bank(4 + j, N_ROWS[j]), ACT.Copy))
            for f in range(KT):
                act.wait_ge(x_turned, f + 1)
                do(xT[:, f, :], pair(uses.slot()), ACT.Copy).then_inc(pair_free[uses.slot()], 1)
                uses.next()
            if phase_end("load"):
                return

            def branch(b, n):
                round_rows(yP, y, n)
                with act.Fori(0, KT // 2) as i, tiles.loop(i, KT // 2, 4), uses.loop(i, KT // 2, 4):
                    for s in range(2):
                        p = product()
                        last_read()
                        release(do(tha[:, 0:n], pair(p, n), ACT.Tanh, scale=0.5,
                                   bias=col(half_bg, i * 2 + (b * KT + s))))
                        skip()

            for l in range(DEPTH):
                n = ALL if l == 0 else LAT
                qu = QU[l]
                if l == 0:
                    for k in range(DEPTH):
                        act.wait_ge(cond_ready, k)
                        do(cond_t, par[k][:, R_C:R_C + 16], ACT.Tanh, scale=0.5).then_inc(cond_tanh, 1)
                    squares(xT, ALL)
                    skip(16)
                    if phase_end("ada0"):
                        return
                else:
                    squares(xT, ALL)
                round_input(hP[0], ALL, l + 1)
                if phase_end(f"norm{l}"):
                    return
                per = 8 if l == 0 else 4

                def next_tile(k=1):
                    for _ in range(k):
                        tiles.next()
                        if per == 8:
                            tiles.next()
                        uses.next()

                with act.Fori(0, KT) as i, tiles.loop(i, KT, per), uses.loop(i, KT, 4):
                    p = product()
                    last_read()
                    do(tha[:, 0:n], pair(p, n), ACT.Tanh, scale=0.5).then_inc(z_tanh, 1)
                    next_tile()
                    p = product()
                    do(bcopy[:, 0:n], pair(p, n), ACT.Copy).then_inc(pair_free[p], 1)
                    next_tile(3)
                if phase_end(f"conv{l}"):
                    return
                branch(0, n)
                if phase_end(f"branch{l}0"):
                    return

                def copy_values(dst):
                    product()
                    for _ in range(2):
                        lo, hi = ((0, 4), (4, 6))[uses.slot()]
                        release(do(dst[:, lo:hi], ps[:, lo * 256:hi * 256].rearrange("p (t m) -> p t m", m=256), ACT.Copy))

                def square_tile(c, m):
                    p = product()
                    act.wait_ge(qms_done, c)
                    do(qsq[:, 0:m], pair(p, m), ACT.Square).then_inc(qsq_ready, 1)
                    skip()

                def root_tile(c, m):
                    act.wait_ge(qms_done, c + 1)
                    act.wait_ge(qn_ready, c)
                    inverse_root(qrs[:, 0:m], qln[:, 0:m], bank(4, m), HD, (qms_read, c + 1)).then_inc(qrs_ready, 1)

                nb = NORMED * l
                for c in range(2):
                    square_tile(nb + c, ALL)
                    root_tile(nb + c, ALL)
                copy_values(vN)
                square_tile(nb + 2, n)
                root_tile(nb + 2, n)

                def step(off, i, last_head=False):
                    u0 = i * (2 * qu) + (U_BASE[l] + off * qu)
                    hn = i * 2 + (HEADS * l + off)
                    c = i * 2 + (nb + 3 + off)

                    def exp(t):
                        w = ALL if t < LT else CTX
                        act.wait_ge(max_done, u0 + t + 1)
                        if t >= 2:
                            act.wait_ge(turned, u0 + t - 1)
                        else:
                            act.wait_ge(pv_done, hn)
                        do(prob[:, t % 2, 0:w], bank(6, w), ACT.Exp, scale=HD ** -0.5, bias=stat[:, t % 2, 1:2],
                           accum_out=stat[:, t % 2, 2:3]).then_inc(exp_done, 1)

                    def copy(t):
                        act.wait_ge(turned, u0 + t + 1)
                        act.wait_ge(pv_done, hn)
                        if t < LT:
                            do(pT[:, :, t * P:(t + 1) * P], bank(4, ALL).rearrange("p (s q) -> p s q", q=P),
                               ACT.Copy).then_inc(pT_ready, 1)
                        else:
                            o = (t - LT) * P
                            do(pTc[:, :, o:o + P], bank(4, CTX).rearrange("p (s q) -> p s q", q=P),
                               ACT.Copy).then_inc(pT_ready, 1)

                    for t in range(qu):
                        exp(t)
                        if not last_head and t == SQUARE_AT[l]:
                            square_tile(c, n)
                        if not last_head and t == NORM_AT[l]:
                            root_tile(c, n)
                        copy(t)
                    p = product()
                    act.wait_ge(za_silu, hn)
                    do(zth[:, 0:n], pair(p, n), ACT.Tanh, scale=0.5).then_inc(za_tanh, 1)
                    skip()

                with act.Fori(0, HEADS // 2 - 1) as i, tiles.loop(i, HEADS // 2 - 1, 4), uses.loop(i, HEADS // 2 - 1, 4):
                    step(0, i)
                    step(1, i)
                step(0, 3)
                step(1, 3, True)
                if phase_end(f"attn{l}"):
                    return
                branch(1, n)
                if phase_end(f"branch{l}1"):
                    return
                p = product()
                do(gr[0:32, :], pair(p)[0:32, :], ACT.Copy).then_inc(pair_free[uses.slot()], 1)
                skip()
                units, nf = GU[l]
                def queries():
                    p = product()
                    release(do(gq[:, 0:n], pair(p, n), ACT.Copy, scale=DK ** -0.5))

                def head(i, last_head=False):
                    hh = i + GHEADS * l
                    u0 = hh * NU
                    act.wait_ge(dec_done, hh + 1)
                    act.wait_ge(gla_out, hh)
                    for d in range(2):
                        own(do(gtmp[:, d], bank(4 + 2 * d, ALL), ACT.Abs))
                        own.settle()
                        own(do(gtmp[:, d], gtmp[:, d], ACT.Exp, scale=-1.0))
                        own.settle()
                        do(gtmp[:, d], gtmp[:, d], ACT.Ln, bias=one).then_inc(dec_ln, 1)
                    copy_values(gv)
                    p = product()
                    release(do(gk, pair(p), ACT.Copy))

                    def exponentials(j):
                        act.wait_ge(sum_done, u0 + j + 1)
                        act.wait_ge(qk_ready, u0 + j)
                        if units[j][2]:
                            ins = do(gE, bank(0, 1536).rearrange("p (c m) -> p c m", c=3)[:, :, 0:384], ACT.Exp)
                        else:
                            ins = do(gE[:, 0:9:8], bank(0, 1024).rearrange("p (c m) -> p c m", c=2)[:, :, 0:P], ACT.Exp)
                        ins.then_inc(e_ready, 1)

                    exponentials(0)
                    for j in range(NU):
                        if j + 1 < NU:
                            exponentials(j + 1)
                        act.wait_ge(k_turned, u0 + j + 1)
                        act.wait_ge(s_done, u0 + max(j - 1, 0))
                        do(gkN[:, j % 2], bank(6, P), ACT.Copy).then_inc(kN_ready, 1)
                    act.wait_ge(s_done, u0 + NU)
                    act.wait_ge(o_read, (i + 1) * nf + F_BASE[l])
                    yh = y[:, 2 * i:2 * i + 2, 0:n] if isinstance(i, int) else y[:, ds(i * 2, 2), 0:n]
                    do(gsq[:, :, 0:n], yh, ACT.Square).then_inc(gsq_ready, 1)
                    if not last_head:
                        queries()
                    act.wait_ge(gms_done, hh + 1)
                    inverse_root(gtmp[:, 0, 0:n], gtmp[:, 1, 0:n], bank(4, n), DV, (grs_ready, hh * 2 + 1))\
                        .then_inc(grs_ready, 1)

                queries()
                with act.Fori(0, GHEADS - 1) as i, tiles.loop(i, GHEADS - 1, 4), uses.loop(i, GHEADS - 1, 4), \
                        own.loop(i, GHEADS - 1, 4):
                    head(i)
                head(GHEADS - 1, True)
                if phase_end(f"gla{l}"):
                    return
                with act.Fori(0, 2) as i, tiles.loop(i, 2, 4), uses.loop(i, 2, 4):
                    for s in range(4):
                        p = product()
                        last_read()
                        do(tha[:, 0:n], pair(p, n), ACT.Tanh, scale=0.5).then_inc(z_tanh, 1)
                        skip()
                if phase_end(f"glaz{l}"):
                    return
                branch(2, n)
                if phase_end(f"branch{l}2"):
                    return
                round_rows(accP, acc, n)
                with act.Fori(0, 2) as i, tiles.loop(i, 2, 4), uses.loop(i, 2, 4):
                    for s in range(4):
                        p = product()
                        release(do(row(y, i * 4 + s, 0, n), pair(p, n), ACT.Copy))
                if phase_end(f"out{l}"):
                    return
                squares(y, n)
                if phase_end(f"post{l}"):
                    return
            squares(xT, LAT)
            act.wait_ge(rows_mm, 1)
            for w_ in range(2):
                do(brow[0:20, w_, 0:TOE], pair(w_)[0:20, 0:TOE], ACT.Copy).then_inc(rows_done, 1)
            act.wait_ge(lam_sum, 2)
            own(do(lam[:, 2:4], lam[:, 0:2], ACT.Exp))
            round_input(hP[0], LAT, 3)
            if phase_end("norm2"):
                return

            def square2(c, src, n=LAT):
                act.wait_ge(ms2_done, c)
                do(n2sq[:, 0:n], src, ACT.Square).then_inc(sq2_ready, 1)

            def root2(c, count, n=LAT):
                act.wait_ge(ms2_done, c + 1)
                act.wait_ge(n2_ready, c)
                inverse_root(n2rs[:, 0:n], n2ln[:, 0:n], bank(3, n), count).then_inc(rs2_ready, 1)

            def tokens_out(dst):
                p = product()
                release(do(dst, bank(2 * p).rearrange("p (t m) -> p t m", m=P), ACT.Copy))

            def keep(c, src):
                act.wait_ge(n2_ready, c)
                return do(n2raw, src, ACT.Copy)

            def normed2(c):
                p = product()
                square2(c, bank(2 * p))
                release(keep(c, bank(2 * p)))
                root2(c, 64)

            def two_out(*dst):
                product()
                tiles.next()
                src = pair(uses.slot(), 1024).rearrange("p (t a m) -> p a t m", a=2, m=P)
                own(do(dst[0], src[:, 0], ACT.Copy))
                release(do(dst[1], src[:, 1], ACT.Copy))

            two_out(vA[:, :, 0:P], vA[:, :, P:2 * P])
            two_out(vA[:, :, 2 * P:3 * P], vA[:, :, 3 * P:4 * P])
            two_out(vB, vS)
            normed2(0)
            for kv in range(2):
                p = product()
                release(do(tk[:, kv], bank(2 * p), ACT.Copy))
            normed2(1)
            normed2(2)
            tokens_out(vW)
            p = product()
            release(do(gates, bank(2 * p, 96).rearrange("p (t m) -> p t m", m=24), ACT.Tanh, scale=0.5))
            for kv in range(2):
                act.wait_ge(tab2_turned, kv + 1)
                own(do(pos[:, kv], bank(6 + kv, 32), ACT.Copy))
            if phase_end("kv2"):
                return
            for kv in range(2):
                act.wait_ge(hid_done, kv + 1)
                for g in range(2):
                    do(hx[:, 2 * kv, 0:124].rearrange("p (m g c) -> p m g c", m=2, g=2)[:, :, g],
                       bank(6 - 2 * kv + g, 62).rearrange("p (m c) -> p m c", m=2), ACT.Copy).then_inc(hx_ready, 1)
                act.wait_ge(gelu_arg, kv + 1)
                do(hx[:, 2 * kv + 1, 0:124], hx[:, 2 * kv + 1, 0:124], ACT.Tanh, scale=GELU).then_inc(gelu_tanh, 1)
            act.wait_ge(hid_done, 3)
            square2(3, bank(0, 2 * NB2), 2 * NB2)
            root2(3, 64, 2 * NB2)
            act.wait_ge(hid_done, 4)
            own(do(vc[0:NB2], bank(2)[0:NB2, 0:128].rearrange("p (g d) -> p g d", g=2), ACT.Copy))
            if phase_end("cmp"):
                return
            with act.Fori(0, 4) as i, tiles.loop(i, 4, 4), uses.loop(i, 4, 4), own.loop(i, 4, 2 * LT + 5):
                c0 = i * 5 + NORM0
                s0, t0 = i * NS2, i * turns2
                for c in range(4):
                    normed2(c0 + c)

                def exp(n):
                    u = heads2[n]
                    st = stat2[:, n % 4]
                    act.wait_ge(max2, s0 + n + 1)
                    before = [x["turn"] for x in heads2[:max(n - 2, 0)] if x["turn"] is not None] if n >= 4 else []
                    if n >= 4 and heads2[n - 4]["turn"] is not None and heads2[n - 3]["turn"] is not None:
                        before = before[:-1]
                    act.wait_ge(turned2, t0 + (before[-1] + 1) if before else i * turns2)
                    if u["kind"] == "B":
                        own(do(st[:, 4:5], st[:, 6:7], ACT.Exp))
                    do(prob2[:, n % 4, 0:u["w"]], score_bank(n, u["w"]), ACT.Exp, bias=st[:, 1:2],
                       accum_out=st[:, 2:3]).then_inc(exp2, 1)

                heads_done = [0]

                def copy(n):
                    u = heads2[n]
                    tn = u["turn"]
                    if tn is None:
                        return
                    act.wait_ge(turned2, t0 + tn + 1)
                    act.wait_ge(pv2, i * 5 + heads_done[0])
                    q0 = u["qt"] * P
                    if u["sub"] == "cmp":
                        ins = do(pTcmp[0:NB2, q0:q0 + P], bank(4 + tn % 2)[0:NB2, 0:P], ACT.Copy)
                    else:
                        k0, k1 = u["lo"] // P, u["lo"] // P + u["w"] // P
                        ins = do(pT2[:, int(u["sub"] == "win"), k0:k1, q0:q0 + P],
                                 bank(4 + tn % 2, u["w"]).rearrange("p (s q) -> p s q", q=P), ACT.Copy)
                    ins.then_inc(pT2_ready, 1)

                exp(0)
                for n in range(NS2):
                    if n + 1 < NS2:
                        exp(n + 1)
                    copy(n)
                    if n and heads2[n - 1]["end"] and heads2[n - 1]["kind"] == "A":
                        root2(c0 + 4, P)
                    if heads2[n]["end"]:
                        heads_done[0] += 1
                        if heads2[n]["kind"] == "A":
                            act.wait_ge(pv2, i * 5 + 1)
                            square2(c0 + 4, bank(1))
                            keep(c0 + 4, bank(1)).then_inc(o2_read, 1)
            if phase_end("heads"):
                return
            round_rows(y2P, y2, LAT)
            for b in range(3):
                with act.Fori(0, KT // 2) as i, tiles.loop(i, KT // 2, 4), uses.loop(i, KT // 2, 4):
                    for s in range(2):
                        p = product()
                        last_read()
                        release(do(tha2, bank(2 * p), ACT.Tanh, scale=0.5))
                        skip()
            if phase_end("branches2"):
                return
            round_rows(accP, acc, LAT)
            skip(8)
            if phase_end("out2"):
                return
            squares(xT, LAT)
            round_input(h3P[0], LAT, 0)
            if phase_end("norm3"):
                return
            with act.Fori(0, 8) as i, tiles.loop(i, 8, 4), uses.loop(i, 8, 4):
                for _ in range(4):
                    p = product()
                    last_read()
                    do(rl, bank(2 * p), ACT.Relu).then_inc(relu_ready, 1)
                    skip()
            if phase_end("up"):
                return
            for _ in range(8):
                uses.next()
            if phase_end("down"):
                return
            for t in range(LT):
                act.wait_ge(out_turned, t + 1)
                do(ob[:, t], pair(uses.slot(), 1024), ACT.Copy).then_inc(out_copied, 1)
                uses.next()
            phase_end("end")

        @block.vector
        def _(dve):
            tiles, uses = Turns(RING), Turns(2)
            own = Steps(dve, dve_own)
            ends, norms = [0], [0]
            v = nc.vector

            def phase_end(name):
                dve.drain().then_inc(phase, 1)
                ends[0] += 3
                dve.wait_ge(phase, ends[0])
                return name == stop

            def stt(o, a0, s, a1, op0, op1):
                return v.scalar_tensor_tensor(out=o, in0=a0, scalar=s, in1=a1, op0=op0, op1=op1)

            def product():
                dve.wait_ge(w_used, tiles.number() + 1)
                return uses.slot()

            def release(ins):
                ins.then_inc(pair_free[uses.slot()], 1)
                skip()

            def skip(n=1):
                for _ in range(n):
                    tiles.next()
                    uses.next()

            def all_read():
                for s in range(2):
                    dve.wait_ge(pair_free[s], uses.uses_of(s))

            def last_read():
                k = uses.k - 1
                dve.wait_ge(pair_free[k % 2], k // 2 + 1 + uses.add)

            parts_made, normed = [0], [0]

            def keep_rest(dst, src, n):
                for f in range(src.shape[1]):
                    parts_made[0] += 1
                    dve.wait_ge(part_hi, parts_made[0])
                    v.tensor_tensor(dst[1][:, f, 0:n], src[:, f, 0:n], dst[0][:, f, 0:n].bitcast(F32),
                                    ALU.subtract).then_inc(part_lo, 1)

            def input_ready(ins):
                ins.then_inc(h_ready, 1)
                normed[0] += 1

            def input_rest(dst, f, n):
                k = normed[0] // KT * KT + f + 1 if normed[0] % KT else normed[0] - KT + f + 1
                dve.wait_ge(h_hi, k)
                own(v.tensor_tensor(dst[1][:, f, 0:n], hT[:, f, 0:n], dst[0][:, f, 0:n].bitcast(F32), ALU.subtract))

            own(v.memset(consts, EPS))
            own(v.memset(onec, 1.0))
            for _ in range(KT):
                uses.next()
            if phase_end("load"):
                return

            def branch(b, n):
                keep_rest(yP, y, n)
                with dve.Fori(0, KT // 2) as i, tiles.loop(i, KT // 2, 4), uses.loop(i, KT // 2, 4), \
                        own.loop(i, KT // 2, 2):
                    for s in range(2):
                        skip()
                        p = product()
                        last_read()
                        own.settle()
                        release(stt(tmp[:, 0:n], tha[:, 0:n], 1.0, pair(p, n), ALU.add, ALU.mult))
                        last_read()
                        dst = row(acc, i * 2 + s, 0, n)
                        if b == 0:
                            own(v.tensor_scalar(dst, tmp[:, 0:n], 0.5, None, ALU.mult))
                        else:
                            own(stt(dst, tmp[:, 0:n], 0.5, dst, ALU.mult, ALU.add))

            for l in range(DEPTH):
                n = ALL if l == 0 else LAT
                qu = QU[l]
                def over(o, w):
                    return par[l][:, o:o + w].unsqueeze(2).to_broadcast([P, w, 2])

                modl = mods[:, 24 * l:24 * l + 24]
                if l == 0:
                    for k in range(DEPTH):
                        dve.wait_ge(cond_tanh, k + 1)
                        pc = par[k][:, R_C:R_C + 16]
                        own(stt(cond_s, cond_t, 1.0, pc, ALU.add, ALU.mult))
                        own.settle()
                        v.tensor_scalar(conds[k].rearrange("p a b -> p (a b)"), cond_s, 0.5, None, ALU.mult).then_inc(cond_ready, 1)
                        dve.wait_ge(cond_ready, k + 1)
                    with dve.Fori(0, 4) as i, tiles.loop(i, 4, 4), uses.loop(i, 4, 4):
                        for s in range(4):
                            p = product()
                            release(v.tensor_copy(row(mods, i * 4 + s), pair(p, 2)))
                    all_read()
                    own(v.tensor_tensor(modl[:, 0:16], modl[:, 0:16], over(R_BADA, 16), ALU.add))
                else:
                    own(v.tensor_tensor(modl, modl, over(R_BADA, 24), ALU.add))
                    own.settle()
                    own(v.tensor_tensor(gpost[:], modl[:, 16:24], over(R_GPOST, 8), ALU.mult))
                own.settle()
                own(stt(scale1[:], modl[:, 8:16], 1.0, over(R_GPRE, 8), ALU.add, ALU.mult))
                own(v.tensor_scalar(half_bg[:], par[l][:, R_BG:R_BG + 24], 0.5, None, ALU.mult))
                own.settle()
                if l == 0 and phase_end("ada0"):
                    return
                norms[0] += 1
                dve.wait_ge(rs_ready, norms[0])
                for f in range(KT):
                    own(v.tensor_tensor(hT[:, f], xT[:, f], rs, ALU.mult))
                    own.settle()
                    for k, (lo, hi) in enumerate(spans(ALL)):
                        ins = v.tensor_scalar(hT[:, f, lo:hi], hT[:, f, lo:hi], scale1[:, f, k:k + 1],
                                              modl[:, f, k:k + 1], ALU.mult, ALU.add)
                        (own if k == 0 else input_ready)(ins)
                    if f:
                        input_rest(hP, f - 1, ALL)
                input_rest(hP, KT - 1, ALL)
                if phase_end(f"norm{l}"):
                    return
                edges = (0, LAT + 1, LAT + 2, LAT + 2 + CTX + 1)
                for e in edges:
                    own(v.memset(conv_u[:, e:e + 1], 0.0))
                stretches = [(0, 0, LAT)] + ([(LAT + 2, LAT, CTX)] if n == ALL else [])
                ns = len(stretches)
                per = 8 if l == 0 else 4

                def next_tile():
                    tiles.next()
                    if per == 8:
                        tiles.next()
                    uses.next()

                with dve.Fori(0, KT) as i, tiles.loop(i, KT, per), uses.loop(i, KT, 4), own.loop(i, KT, 4 * ns):
                    p = product()
                    dve.wait_ge(z_tanh, i + 16 * l + 1)
                    last_read()
                    stt(tmp[:, 0:n], tha[:, 0:n], 1.0, pair(p, n), ALU.add, ALU.mult).then_inc(pair_free[p], 1)
                    next_tile()
                    last_read()
                    next_tile()
                    p = product()
                    last_read()
                    for at, o, w in stretches:
                        ins = v.tensor_tensor(conv_u[:, at + 1:at + 1 + w], bcopy[:, o:o + w], pair(p)[:, o:o + w], ALU.mult)
                        own(ins)
                    own.settle()
                    for at, o, w in stretches:
                        t = conv_t[:, o:o + w]
                        own(v.tensor_scalar(t, conv_u[:, at:at + w], col(par[l], i + R_CONV), None, ALU.mult))
                        own.settle()
                        for k in (1, 2):
                            own(stt(t, conv_u[:, at + k:at + k + w], col(par[l], i + (R_CONV + 8 * k)), t, ALU.mult, ALU.add))
                            own.settle()
                    stt(tmp[:, 0:n], tmp[:, 0:n], 0.5, conv_t[:, 0:n], ALU.mult, ALU.mult).then_inc(pair_free[p], 1)
                    next_tile()
                    p = product()
                    last_read()
                    v.tensor_tensor(row(y, i, 0, n), tmp[:, 0:n], pair(p, n), ALU.mult).then_inc(pair_free[p], 1)
                    next_tile()
                    if l == 0:
                        dve.wait_ge(w_used, tiles.number())
                        v.tensor_copy(mods[:, ds(i * 4 + 16, 4)], bank(6, 8).rearrange("p (a b) -> p a b", a=4)).then_inc(mod_read, 1)
                if l == 0:
                    dve.wait_ge(mod_read, KT)
                    own(v.tensor_tensor(modl[:, 16:24], modl[:, 16:24], over(R_BADA + 16, 8), ALU.add))
                    own.settle()
                    own(v.tensor_tensor(gpost[:], modl[:, 16:24], over(R_GPOST, 8), ALU.mult))
                if phase_end(f"conv{l}"):
                    return
                branch(0, n)
                if phase_end(f"branch{l}0"):
                    return

                def norm_tile(c, dst, g, m):
                    s = uses.slot()
                    dve.wait_ge(qrs_ready, c + 1)
                    stt(dst[:, 0:m], pair(s, m), g, qrs[:, 0:m], ALU.mult, ALU.mult).then_inc(pair_free[s], 1)
                    skip()
                    last_read()
                    v.tensor_tensor(rope_t, dst[:, 0:LAT], cos, ALU.mult).then_inc(qn_ready, 1)

                def rotate_tile(c, dst):
                    dve.wait_ge(rot_done, c + 1)
                    v.tensor_tensor(rope_s, bank(4), sin, ALU.mult).then_inc(rot_read, 1)
                    dve.wait_ge(rot_read, c + 1)
                    dve.wait_ge(qn_ready, c + 1)
                    v.tensor_tensor(dst[:, 0:LAT], rope_t, rope_s, ALU.add).then_inc(q_ready, 1)

                nb = NORMED * l
                qg, kg = par[l][:, R_QG:R_QG + 1], par[l][:, R_KG:R_KG + 1]
                for c in range(2):
                    norm_tile(nb + c, kT[:, c], kg, ALL)
                    rotate_tile(nb + c, kT[:, c])
                skip(2)
                norm_tile(nb + 2, qT[:, 0], qg, n)
                rotate_tile(nb + 2, qT[:, 0])

                def step(off, i, last_head=False):
                    u0 = i * (2 * qu) + (U_BASE[l] + off * qu)
                    hn = i * 2 + (HEADS * l + off)
                    c = i * 2 + (nb + 3 + off)
                    nq = qT[:, (off + 1) % 2]

                    def maximum(t):
                        w = ALL if t < LT else CTX
                        st = stat[:, t % 2]
                        dve.wait_ge(scores_done, u0 + t + 1)
                        own(v.reduce_max(st[:, 0:1], bank(6, w), AX.X))
                        own.settle()
                        v.tensor_scalar(st[:, 1:2], st[:, 0:1], -HD ** -0.5, None, ALU.mult).then_inc(max_done, 1)

                    def normalise(t):
                        w = ALL if t < LT else CTX
                        st = stat[:, t % 2]
                        dve.wait_ge(exp_done, u0 + t + 1)
                        own(v.reciprocal(st[:, 3:4], st[:, 2:3]))
                        own.settle()
                        pr = prob[:, t % 2, 0:w]
                        v.tensor_scalar(pr, pr, st[:, 3:4], None, ALU.mult).then_inc(prob_done, 1)

                    for t in range(qu):
                        maximum(t)
                        if not last_head and t == NORM_AT[l] + 1:
                            rotate_tile(c, nq)
                        normalise(t)
                        if not last_head and t == NORM_AT[l]:
                            norm_tile(c, nq, qg, n)
                    p = product()
                    dve.wait_ge(za_tanh, hn + 1)
                    dve.wait_ge(head_out, hn)
                    stt(zsi[:, 0:n], zth[:, 0:n], 1.0, pair(p, n), ALU.add, ALU.mult).then_inc(pair_free[p], 1)
                    skip()
                    last_read()
                    v.memset(stat[:, 3, 6:7], 0.0).then_inc(za_silu, 1)
                    dve.wait_ge(pv_done, hn + 1)
                    h = i * 2 + off
                    stt(row(y, h, 0, n), bank(4, n), 0.5, zsi[:, 0:n], ALU.mult, ALU.mult).then_inc(head_out, 1)

                with dve.Fori(0, HEADS // 2 - 1) as i, tiles.loop(i, HEADS // 2 - 1, 4), \
                        uses.loop(i, HEADS // 2 - 1, 4), own.loop(i, HEADS // 2 - 1, 4 * qu):
                    step(0, i)
                    step(1, i)
                step(0, 3)
                step(1, 3, True)
                if phase_end(f"attn{l}"):
                    return
                branch(1, n)
                if phase_end(f"branch{l}1"):
                    return

                own(v.memset(gwd[0:33], 0.0))
                own.settle()
                v.memset(gr[32:33], 1.0).then_inc(wd_zero, 1)
                skip()
                units, nf = GU[l]
                skip()

                def head(i):
                    hh = i + GHEADS * l
                    u0 = hh * NU
                    f0 = i * nf + F_BASE[l]
                    skip(4)
                    for d in range(2):
                        dve.wait_ge(dec_ln, hh * 2 + d + 1)
                        stt(gla[:, d].rearrange("p t m -> p (t m)"), bank(4 + 2 * d, ALL), 0.0, gtmp[:, d], ALU.min,
                            ALU.subtract).then_inc(la_ready, 1)
                    own(v.memset(gS, 0.0))
                    for s in range(2):
                        k = uses.k - 2 - s
                        dve.wait_ge(pair_free[k % 2], k // 2 + 1 + uses.add)

                    def decayed(j):
                        d, t, full = units[j][:3]
                        q_, k_ = (x[:, t * P:(t + 1) * P].unsqueeze(1).to_broadcast([P, 8, P]) for x in (gq, gk))
                        dve.wait_ge(e_ready, u0 + j + 1)
                        dve.wait_ge(s_done, u0 + max(j - 2, 0))
                        dve.wait_ge(s_ready, u0 + max(j - 2, 0))
                        e = 0 if d else P - 1
                        own(v.tensor_copy(gdec[:, j % 3:j % 3 + 1], gE[:, 0, e:e + 1]))
                        if full:
                            own(v.tensor_tensor(gqE[:, j % 3].rearrange("p (l t) -> p l t", l=8), gE[:, 0:8], q_, ALU.mult))
                            ins = v.tensor_tensor(gkE[:, j % 2].rearrange("p (l t) -> p l t", l=8), gE[:, 1:9], k_, ALU.mult)
                        else:
                            ins = v.tensor_tensor(gkE[:, j % 2, 7 * P:8 * P], gE[:, 8], gk[:, t * P:(t + 1) * P], ALU.mult)
                        ins.then_inc(qk_ready, 1)

                    def mask(j):
                        d, t, full, seen, f = units[j]
                        if not full:
                            return
                        dve.wait_ge(att_done, f0 + f + 1)
                        dve.wait_ge(att_ready, f0 + f)
                        v.tensor_tensor(gam, bank(3, 1024).rearrange("p (l t) -> p l t", l=8), pairs[:, d],
                                        ALU.mult).then_inc(masked, 1)
                        dve.wait_ge(masked, f0 + f + 1)
                        dve.wait_ge(o_done, f0 + max(f - 1, 0))
                        v.tensor_reduce(gatt[:, f % 2], gam.rearrange("p l t -> p t l"), AX.X, ALU.add).then_inc(att_ready, 1)

                    def keep(j):
                        d, t, full, seen, f = units[j]
                        if full:
                            dve.wait_ge(o_done, f0 + f + 1)
                            ts_ = slice(t * P, (t + 1) * P)
                            dst = y[:, 2 * i:2 * i + 2, ts_] if isinstance(i, int) else y[:, ds(i * 2, 2), ts_]
                            o_ = bank(5, DV).rearrange("p (a t) -> p a t", a=2)
                            if seen:
                                dve.wait_ge(o_read, f0 + f)
                                v.tensor_tensor(dst, dst, o_, ALU.add).then_inc(o_read, 1)
                            else:
                                v.tensor_copy(dst, o_).then_inc(o_read, 1)
                        dve.wait_ge(s_done, u0 + j + 1)
                        own.settle()
                        dve.wait_ge(s_ready, u0 + j)
                        stt(gS[:, d], gS[:, d], gdec[:, j % 3:j % 3 + 1], bank(7, DV), ALU.mult, ALU.add).then_inc(s_ready, 1)

                    decayed(0)
                    for j in range(NU):
                        if j + 1 < NU:
                            decayed(j + 1)
                        mask(j)
                        if j:
                            keep(j - 1)
                    keep(NU - 1)
                    dve.wait_ge(grs_ready, hh * 2 + 2)
                    for a_ in range(2):
                        dst = row(y, 2 * i + a_, 0, n)
                        ins = stt(dst, dst, par[l][:, R_GLAG + a_:R_GLAG + a_ + 1], gtmp[:, 0, 0:n], ALU.mult, ALU.mult)
                        if a_ == 0:
                            own(ins)
                        else:
                            ins.then_inc(gla_out, 1)

                with dve.Fori(0, GHEADS - 1) as i, tiles.loop(i, GHEADS - 1, 4), uses.loop(i, GHEADS - 1, 4), \
                        own.loop(i, GHEADS - 1, 1 + NU + nf + 1):
                    head(i)
                head(GHEADS - 1)
                tiles.k -= 1
                uses.k -= 1
                if phase_end(f"gla{l}"):
                    return
                with dve.Fori(0, 2) as i, tiles.loop(i, 2, 4), uses.loop(i, 2, 4), own.loop(i, 2, 4):
                    for s in range(4):
                        p = product()
                        dve.wait_ge(z_tanh, i * 4 + (16 * l + 8 + s + 1))
                        own.settle()
                        release(stt(tmp[:, 0:n], tha[:, 0:n], 1.0, pair(p, n), ALU.add, ALU.mult))
                        last_read()
                        dst = row(y, i * 4 + s, 0, n)
                        own(stt(dst, tmp[:, 0:n], 0.5, dst, ALU.mult, ALU.mult))
                if phase_end(f"glaz{l}"):
                    return
                branch(2, n)
                if phase_end(f"branch{l}2"):
                    return
                keep_rest(accP, acc, n)
                skip(8)
                if phase_end(f"out{l}"):
                    return
                norms[0] += 1
                dve.wait_ge(rs_ready, norms[0])
                dve.wait_ge(x_back, 16 * (l + 1))
                for f in range(KT):
                    own(v.tensor_tensor(y[:, f, 0:n], y[:, f, 0:n], rs[:, 0:n], ALU.mult))
                    own.settle()
                    for k, (lo, hi) in enumerate(spans(n)):
                        own(stt(xT[:, f, lo:hi], y[:, f, lo:hi], gpost[:, f, k:k + 1], xT[:, f, lo:hi], ALU.mult, ALU.add))
                if phase_end(f"post{l}"):
                    return
            def normed_h(g0, dst):
                norms[0] += 1
                dve.wait_ge(rs_ready, norms[0])
                for f in range(KT):
                    input_ready(stt(hT[:, f, 0:LAT], xT[:, f, 0:LAT], par2[:, g0 + f:g0 + f + 1], rs[:, 0:LAT],
                                    ALU.mult, ALU.mult))
                    if f:
                        input_rest(dst, f - 1, LAT)
                input_rest(dst, KT - 1, LAT)

            v.memset(relb[BUCKETS:BUCKETS + 1], NEG).then_inc(relb_ready, 1)
            for g in (0, 2, 4):
                gcol = par2[:, S_GAIN + g:S_GAIN + g + 1]
                own(v.tensor_scalar(gcol, gcol, 0.125, None, ALU.mult))
            scol = par2[:, S_SUB:S_SUB + 1]
            own(v.tensor_scalar(scol, scol, 1.0 - LAM0, None, ALU.mult))
            dve.wait_ge(in2, 64)
            for k in range(2):
                own(v.tensor_tensor(lamp, lamb[:, 128 * k:128 * k + 64], lamb[:, 128 * k + 64:128 * k + 128], ALU.mult))
                own.settle()
                v.tensor_reduce(lam[:, k:k + 1], lamp, AX.X, ALU.add).then_inc(lam_sum, 1)
                dve.wait_ge(lam_sum, k + 1)
            normed_h(S_MIX, hP)
            if phase_end("norm2"):
                return

            def normed_tile(c, dst, gain):
                dve.wait_ge(rs2_ready, c + 1)
                stt(dst, n2raw, gain, n2rs, ALU.mult, ALU.mult).then_inc(n2_ready, 1)

            def gain(g):
                return par2[:, S_GAIN + g:S_GAIN + g + 1]

            own(v.tensor_tensor(lam[:, 0:1], lam[:, 3:4], lam[:, 2:3], ALU.subtract))
            own.settle()
            own(v.tensor_scalar(lam[:, 0:1], lam[:, 0:1], -LAM0, None, ALU.add))
            for _ in range(3):
                tiles.next()
            skip(10)
            for c, (dst, g) in enumerate(((kB, 3), (kS, 6), (kW, 7))):
                normed_tile(c, dst, gain(g))
            all_read()
            own(v.tensor_scalar(gates, gates, 0.5, 0.5, ALU.mult, ALU.add))
            if phase_end("kv2"):
                return
            for kv in range(2):
                src = tk[:, kv]
                win = bass.AP(src.tensor, src.offset, [list(src.ap[0]), [16, NB2], [1, 32]])
                if kv:
                    dve.wait_ge(hid_done, 1)
                v.tensor_tensor(tpos, win, pos[:, kv].unsqueeze(1).to_broadcast([P, NB2, 32]), ALU.add).then_inc(hid_ready, 1)
            for kv in range(2):
                x_, u_ = hx[:, 2 * kv, 0:124], hx[:, 2 * kv + 1, 0:124]
                dve.wait_ge(hid_done, kv + 1)
                dve.wait_ge(hx_ready, 2 * kv + 2)
                own(v.tensor_tensor(u_, x_, x_, ALU.mult))
                own.settle()
                own(v.tensor_scalar(u_, u_, 0.044715, 1.0, ALU.mult, ALU.add))
                own.settle()
                v.tensor_tensor(u_, u_, x_, ALU.mult).then_inc(gelu_arg, 1)
                dve.wait_ge(gelu_tanh, kv + 1)
                own(stt(u_, u_, 1.0, x_, ALU.add, ALU.mult))
                own.settle()
                v.tensor_scalar(hid[:, kv, 0:124], u_, 0.5, None, ALU.mult).then_inc(hid_ready, 1)
            dve.wait_ge(rs2_ready, 4)
            stt(kc[:, 0:62], bank(0, 62), par2[:, S_GAIN + 5:S_GAIN + 6], n2rs[:, 0:62], ALU.mult, ALU.mult).then_inc(n2_ready, 1)
            if phase_end("cmp"):
                return
            own2 = sum(1 + {"c0": 2, "c1": 2, "b": 3, "sel": 1, "win": 1, "cmp": 2}[u["sub"]] for u in heads2)
            with dve.Fori(0, 4) as i, tiles.loop(i, 4, 4), uses.loop(i, 4, 4), \
                    own.loop(i, 4, own2 + 1):
                c0 = i * 5 + NORM0
                s0, t0 = i * NS2, i * turns2
                dve.wait_ge(pv2, i * 5)
                own(v.tensor_scalar(vAh, vA[:, :, ds(i * P, P)], 1.0, None, ALU.mult))
                for c, g in enumerate((0, 1, 2, 4)):
                    normed_tile(c0 + c, qt_[:, c], gain(g))
                skip(4)

                def maximum(n):
                    u = heads2[n]
                    st = stat2[:, n % 4]
                    dve.wait_ge(scores2, s0 + n + 1)
                    own.settle()
                    own(v.reduce_max(st[:, 0:1], score_bank(n, u["w"]), AX.X))
                    own.settle()
                    if u["kind"] == "B":
                        sink = sinkb[:, ds(i + 4 * u["g"], 1)]
                        own(v.tensor_scalar(st[:, 1:2], st[:, 0:1], sink, -1.0, ALU.max, ALU.mult))
                        own.settle()
                        ins = v.tensor_scalar(st[:, 6:7], st[:, 1:2], sink, None, ALU.add)
                    else:
                        ins = v.tensor_scalar(st[:, 1:2], st[:, 0:1], -1.0, None, ALU.mult)
                    ins.then_inc(max2, 1)

                def normalise(n):
                    u = heads2[n]
                    st = stat2[:, n % 4]
                    pr = prob2[:, n % 4, 0:u["w"]]
                    dve.wait_ge(exp2, s0 + n + 1)
                    if u["kind"] == "B":
                        own(v.tensor_tensor(st[:, 2:3], st[:, 2:3], st[:, 4:5], ALU.add))
                        own.settle()
                    own(v.reciprocal(st[:, 3:4], st[:, 2:3]))
                    own.settle()
                    if u["sub"] == "c0":
                        own(v.tensor_scalar(pr, pr, st[:, 3:4], None, ALU.mult))
                        return
                    if u["sub"] == "c1":
                        own(v.tensor_tensor(st[:, 5:6], st[:, 3:4], lam[:, 0:1], ALU.mult))
                        own.settle()
                        p0 = prob2[:, (n - 1) % 4, 0:u["w"]]
                        ins = stt(p0, pr, st[:, 5:6], p0, ALU.mult, ALU.add)
                    elif u["kind"] == "B":
                        ins = v.tensor_scalar(pr, pr, st[:, 3:4], None, ALU.mult)
                    else:
                        k = {"cmp": 0, "sel": 1, "win": 2}[u["sub"]]
                        gate = gates[:, u["qt"], ds(i * 3 + 12 * u["g"] + k, 1)]
                        if u["sub"] == "cmp":
                            own(v.tensor_tensor(st[:, 5:6], st[:, 3:4], gate, ALU.mult))
                            own.settle()
                            ins = stt(pr, pr, st[:, 5:6], cmask[:, 0, u["qt"], 0:NB2], ALU.mult, ALU.mult)
                        else:
                            ins = v.tensor_scalar(pr, pr, st[:, 3:4], gate, ALU.mult, ALU.mult)
                    ins.then_inc(prob2_ready, 1)

                def outputs(n):
                    u = heads2[n]
                    if u["kind"] == "A":
                        normed_tile(c0 + 4, row(y2, i), scol)
                    elif u["g"] == 1:
                        nh = sum(x["end"] for x in heads2[:n + 1])
                        dve.wait_ge(pv2, i * 5 + nh)
                        v.tensor_copy(row(y2, i + (4 if u["kind"] == "B" else 8)), bank(1)).then_inc(o2_read, 1)

                maximum(0)
                for n in range(NS2):
                    if n + 1 < NS2:
                        maximum(n + 1)
                    normalise(n)
                    if n >= 2 and heads2[n - 2]["end"]:
                        outputs(n - 2)
                outputs(NS2 - 1)
            if phase_end("heads"):
                return
            keep_rest(y2P, y2, LAT)
            for b in range(3):
                with dve.Fori(0, KT // 2) as i, tiles.loop(i, KT // 2, 4), uses.loop(i, KT // 2, 4), \
                        own.loop(i, KT // 2, 2):
                    for s in range(2):
                        skip()
                        p = product()
                        last_read()
                        own.settle()
                        release(stt(tmp2, tha2, 1.0, bank(2 * p), ALU.add, ALU.mult))
                        last_read()
                        dst = row(acc, i * 2 + s, 0, LAT)
                        if b == 0:
                            own(v.tensor_scalar(dst, tmp2, 0.5, None, ALU.mult))
                        else:
                            own(stt(dst, tmp2, 0.5, dst, ALU.mult, ALU.add))
            if phase_end("branches2"):
                return

            def residual():
                p = uses.slot()
                dst = row(xT, add_at[0], 0, LAT)
                return v.tensor_tensor(dst, dst, bank(2 * p), ALU.add)

            add_at = [0]
            keep_rest(accP, acc, LAT)
            dve.wait_ge(x_back, 48)
            with dve.Fori(0, 2) as i, tiles.loop(i, 2, 4), uses.loop(i, 2, 4):
                for s in range(4):
                    product()
                    add_at[0] = i * 4 + s
                    release(residual())
            if phase_end("out2"):
                return
            normed_h(S_MLP, h3P)
            if phase_end("norm3"):
                return
            with dve.Fori(0, 8) as i, tiles.loop(i, 8, 4), uses.loop(i, 8, 4):
                for s in range(4):
                    p = product()
                    dve.wait_ge(relu_ready, i * 4 + s + 1)
                    release(v.tensor_tensor(row(U, i * 4 + s), rl, bank(2 * p), ALU.mult))
            if phase_end("up"):
                return
            with dve.Fori(0, 4) as i, tiles.loop(i, 4, 8), uses.loop(i, 4, 2):
                for s in range(2):
                    for _ in range(3):
                        tiles.next()
                    dve.wait_ge(w_used, tiles.number() + 1)
                    add_at[0] = i * 2 + s
                    release(residual())
            if phase_end("down"):
                return
            phase_end("end")



_OUTS = [((1, 512, 1024), "float32")]


def kernel(**inputs):
    import numpy as _np
    import concourse.bacc as _bacc
    from concourse import mybir as _mybir
    from concourse.bass_utils import run_bass_kernel_spmd as _run

    nc = _bacc.Bacc("TRN2", target_bir_lowering=False, num_devices=1)
    arrays, args = {}, {}
    given = dict(inputs, con=constants(), con2=constants2())
    for name, value in given.items():
        v = _np.ascontiguousarray(value)
        arrays[f"in_{name}"] = v
        args[name] = nc.dram_tensor(f"in_{name}", v.shape, _mybir.dt.from_np(v.dtype), kind="ExternalInput").ap()
    shape, dtype = _OUTS[0]
    out = nc.dram_tensor("out_0", shape, _mybir.dt.from_np(_np.dtype(dtype)), kind="ExternalOutput").ap()
    two_blocks(nc, args, out)
    r = _run(nc, [arrays], core_ids=[0])
    return r.results[0]["out_0"]
```
